# Optimizing a Trainium2 kernel written in Bass

```python
import jax, jax.numpy as jnp
from jax import lax
import numpy as np
import math

D_MODEL = 2048
BATCH = 1
SEQ = 256
DEPTH = 1

GRID_W = 64
WIN_R = 8
WIN_C = 16
QCB = 16
NCB = GRID_W // QCB
KCW = QCB + WIN_C
N_ATT_HEADS = 8
ATT_HEAD_DIM = 128
ATT_WIDTH = N_ATT_HEADS * ATT_HEAD_DIM
N_DN_HEADS = 8
DN_HEAD_DIM = 128
DN_KEY_WIDTH = N_DN_HEADS * DN_HEAD_DIM
DN_VAL_WIDTH = N_DN_HEADS * DN_HEAD_DIM
DN_QKV_WIDTH = 2 * DN_KEY_WIDTH + DN_VAL_WIDTH
CONV_K = 5
CHUNK = 64
N_DIR = 2
IN_SPLITS = (3 * ATT_WIDTH, DN_QKV_WIDTH, DN_VAL_WIDTH, N_DIR * N_DN_HEADS, N_DIR * N_DN_HEADS, D_MODEL, D_MODEL)
IN_WIDTH = sum(IN_SPLITS)
D_FF = 4 * D_MODEL
RMS_EPS = 1e-6
L2_EPS = 1e-6
NEG_INF = -1e30


def _rmsnorm(x, w):
    xf = x.astype(jnp.float32)
    y = xf * lax.rsqrt(jnp.mean(xf * xf, axis=-1, keepdims=True) + RMS_EPS)
    return (y * w.astype(jnp.float32)).astype(x.dtype)

def _l2norm(x):
    return x * lax.rsqrt(jnp.sum(x * x, axis=-1, keepdims=True) + L2_EPS)

def _window_tables(wr):
    qcol = np.arange(GRID_W).reshape(NCB, QCB)
    cs = np.clip(qcol - WIN_C // 2, 0, GRID_W - WIN_C)
    kcs = np.clip(np.arange(NCB) * QCB - WIN_C // 2, 0, GRID_W - KCW)
    col_idx = kcs[:, None] + np.arange(KCW)[None, :]
    kk = np.arange(wr * KCW)
    key_row = kk // KCW
    key_col = col_idx[:, kk % KCW]
    kc = key_col[:, None, :]
    col_mask = (kc >= cs[..., None]) & (kc < cs[..., None] + WIN_C)
    dc_idx = np.clip(kc - qcol[..., None] + WIN_C - 1, 0, 2 * WIN_C - 2)
    return col_idx, key_row, col_mask, dc_idx

def _neighbourhood_attention(q, k, v, rpb):
    b, s, h, dh = q.shape
    rows = s // GRID_W
    wr = min(WIN_R, rows)
    col_idx, key_row, col_mask, dc_idx = _window_tables(wr)
    key_row = jnp.asarray(key_row, jnp.int32)
    dc_idx = jnp.asarray(dc_idx, jnp.int32)
    rpb_flat = rpb.reshape(h, -1).astype(jnp.float32)

    def grid(a):
        return a.reshape(b, rows, GRID_W, h, dh).transpose(1, 0, 3, 2, 4)

    qg, kg, vg = grid(q), grid(k), grid(v)

    def band(a, rs):
        a = lax.dynamic_slice_in_dim(a, rs, wr, axis=0)[:, :, :, col_idx]
        return a.transpose(1, 2, 3, 0, 4, 5).reshape(b, h, NCB, wr * KCW, dh)

    def row_step(args):
        r, q_r = args
        rs = jnp.clip(r - wr // 2, 0, rows - wr)
        kb, vb = band(kg, rs), band(vg, rs)
        qb = q_r.reshape(b, h, NCB, QCB, dh)
        sc = jnp.einsum('bhjqd,bhjkd->bhjqk', qb, kb, preferred_element_type=jnp.float32) * (dh ** -0.5)
        dr = rs - r + key_row + (WIN_R - 1)
        bias = rpb_flat[:, dr[None, None, :] * (2 * WIN_C - 1) + dc_idx]
        sc = jnp.where(col_mask, sc + bias[None], NEG_INF)
        p = jax.nn.softmax(sc, axis=-1).astype(vb.dtype)
        return jnp.einsum('bhjqk,bhjkd->bhjqd', p, vb).reshape(b, h, GRID_W, dh)

    o = lax.map(row_step, (jnp.arange(rows, dtype=jnp.int32), qg))
    return o.transpose(1, 0, 3, 2, 4).reshape(b, s, h * dh)

def _centred_depthwise_conv(x, w):
    c = x.shape[-1]
    pad = CONV_K // 2
    return lax.conv_general_dilated(x, w.reshape(CONV_K, 1, c).astype(x.dtype), (1,), [(pad, pad)],
                                    dimension_numbers=('NWC', 'WIO', 'NWC'), feature_group_count=c)

def _chunk_gated_delta(q, k, v, g, beta):
    b, t, h, dk = q.shape
    dv = v.shape[-1]
    n = t // CHUNK

    def chunks(a):
        return a.reshape(b, n, CHUNK, h, -1).transpose(1, 0, 3, 2, 4)

    q = chunks(q) * (dk ** -0.5)
    k, v = chunks(k), chunks(v)
    g = chunks(g[..., None])[..., 0]
    beta = chunks(beta[..., None])[..., 0]
    gc = jnp.cumsum(g, axis=-1)
    incl = jnp.tril(jnp.ones((CHUNK, CHUNK), dtype=bool))
    strict = jnp.tril(jnp.ones((CHUNK, CHUNK), dtype=bool), -1)
    decay = jnp.exp(jnp.where(incl, gc[..., :, None] - gc[..., None, :], -jnp.inf))
    kb = k * beta[..., None]
    a_mat = jnp.where(strict, jnp.einsum('nbhid,nbhjd->nbhij', kb, k) * decay, 0.0)
    rhs = jnp.concatenate([v * beta[..., None], kb * jnp.exp(gc)[..., None]], axis=-1)
    sol = lax.linalg.triangular_solve(a_mat, rhs, left_side=True, lower=True, unit_diagonal=True)
    u, w = sol[..., :dv], sol[..., dv:]
    qk = jnp.einsum('nbhid,nbhjd->nbhij', q, k) * decay
    qg = q * jnp.exp(gc)[..., None]
    kg = k * jnp.exp(gc[..., -1:] - gc)[..., None]
    glast = jnp.exp(gc[..., -1])

    def step(state, inp):
        qg_c, kg_c, u_c, w_c, qk_c, gl_c = inp
        v_new = u_c - jnp.einsum('bhck,bhkv->bhcv', w_c, state)
        o = jnp.einsum('bhck,bhkv->bhcv', qg_c, state) + jnp.einsum('bhij,bhjv->bhiv', qk_c, v_new)
        state = state * gl_c[..., None, None] + jnp.einsum('bhck,bhcv->bhkv', kg_c, v_new)
        return state, o

    s0 = jnp.zeros((b, h, dk, dv), jnp.float32)
    _, o = lax.scan(step, s0, (qg, kg, u, w, qk, glast))
    return o.transpose(1, 0, 3, 2, 4).reshape(b, t, h, dv)

def _bidirectional_gated_deltanet(qkv_raw, z, beta_raw, alpha_raw, conv_w, a_log, dt_bias, onorm_w):
    b, s, _ = qkv_raw.shape
    qkv = jax.nn.silu(_centred_depthwise_conv(qkv_raw, conv_w)).astype(jnp.float32)
    q, k, v = jnp.split(qkv, [DN_KEY_WIDTH, 2 * DN_KEY_WIDTH], axis=-1)
    q = _l2norm(q.reshape(b, s, N_DN_HEADS, DN_HEAD_DIM))
    k = _l2norm(k.reshape(b, s, N_DN_HEADS, DN_HEAD_DIM))
    v = v.reshape(b, s, N_DN_HEADS, DN_HEAD_DIM)
    beta = jax.nn.sigmoid(beta_raw.astype(jnp.float32)).reshape(b, s, N_DIR, N_DN_HEADS)
    g = -jnp.exp(a_log.astype(jnp.float32)) * jax.nn.softplus(
        alpha_raw.astype(jnp.float32).reshape(b, s, N_DIR, N_DN_HEADS) + dt_bias.astype(jnp.float32))
    q2 = jnp.concatenate([q, q[:, ::-1]], axis=0)
    k2 = jnp.concatenate([k, k[:, ::-1]], axis=0)
    v2 = jnp.concatenate([v, v[:, ::-1]], axis=0)
    g2 = jnp.concatenate([g[:, :, 0], g[:, ::-1, 1]], axis=0)
    b2 = jnp.concatenate([beta[:, :, 0], beta[:, ::-1, 1]], axis=0)
    o2 = _chunk_gated_delta(q2, k2, v2, g2, b2)
    o = o2[:b] + o2[b:, ::-1]
    zh = z.astype(jnp.float32).reshape(b, s, N_DN_HEADS, DN_HEAD_DIM)
    o = _rmsnorm(o, onorm_w) * jax.nn.silu(zh)
    return o.reshape(b, s, DN_VAL_WIDTH).astype(qkv_raw.dtype)

def first_inputs(seed: int = 0) -> dict:
    key = jax.random.key(seed)
    ks = jax.random.split(key, 16)
    f32 = jnp.float32
    nrm = lambda kk, shape, scale: jax.random.normal(kk, shape, f32) * scale
    dt = jnp.exp(jax.random.uniform(ks[5], (N_DIR, N_DN_HEADS), f32, np.log(1e-3), np.log(1e-1)))
    return {
        "x": nrm(ks[0], (BATCH, SEQ, D_MODEL), 1.0),
        "norm_mix_w": 1.0 + nrm(ks[1], (D_MODEL,), 0.02),
        "w_in": nrm(ks[2], (D_MODEL, IN_WIDTH), D_MODEL ** -0.5),
        "conv_w": nrm(ks[3], (CONV_K, DN_QKV_WIDTH), CONV_K ** -0.5),
        "a_log": jnp.log(jax.random.uniform(ks[4], (N_DIR, N_DN_HEADS), f32, 1.0, 16.0)),
        "dt_bias": dt + jnp.log(-jnp.expm1(-dt)),
        "onorm_w": 1.0 + nrm(ks[6], (DN_HEAD_DIM,), 0.02),
        "rpb": nrm(ks[7], (N_ATT_HEADS, 2 * WIN_R - 1, 2 * WIN_C - 1), 0.1),
        "w_proj_a": nrm(ks[8], (ATT_WIDTH, D_MODEL), ATT_WIDTH ** -0.5),
        "w_proj_b": nrm(ks[9], (DN_VAL_WIDTH, D_MODEL), DN_VAL_WIDTH ** -0.5),
        "w_out": nrm(ks[10], (D_MODEL, D_MODEL), D_MODEL ** -0.5),
        "norm_mlp_w": 1.0 + nrm(ks[11], (D_MODEL,), 0.02),
        "w_mlp_up": nrm(ks[12], (D_MODEL, D_FF), D_MODEL ** -0.5),
        "w_mlp_down": nrm(ks[13], (D_FF, D_MODEL), D_FF ** -0.5),
        "norm_final_w": 1.0 + nrm(ks[14], (D_MODEL,), 0.02),
    }

def first_block(x, norm_mix_w, w_in, conv_w, a_log, dt_bias, onorm_w, rpb, w_proj_a, w_proj_b,
              w_out, norm_mlp_w, w_mlp_up, w_mlp_down, norm_final_w):
    b, s, _ = x.shape
    h = x
    for _ in range(DEPTH):
        xn = _rmsnorm(h, norm_mix_w)
        proj = xn @ w_in
        att_qkv, dn_qkv, dn_z, dn_beta, dn_alpha, gate_a, gate_b = jnp.split(
            proj, list(np.cumsum(IN_SPLITS)[:-1]), axis=-1)
        aq, ak, av = jnp.split(att_qkv.reshape(b, s, 3, N_ATT_HEADS, ATT_HEAD_DIM), 3, axis=2)
        y_a = _neighbourhood_attention(aq[:, :, 0], ak[:, :, 0], av[:, :, 0], rpb)
        y_b = _bidirectional_gated_deltanet(dn_qkv, dn_z, dn_beta, dn_alpha, conv_w, a_log, dt_bias, onorm_w)
        mixed = jax.nn.sigmoid(gate_a) * (y_a @ w_proj_a) + jax.nn.sigmoid(gate_b) * (y_b @ w_proj_b)
        h = h + mixed @ w_out
        hn = _rmsnorm(h, norm_mlp_w)
        h = h + jnp.square(jax.nn.relu(hn @ w_mlp_up)) @ w_mlp_down
    return _rmsnorm(h, norm_final_w)


MIX_WIDTH = D_MODEL
HEAD_DIM = 128
ATTN_WIDTH = MIX_WIDTH // 2
ATTN_HEADS = ATTN_WIDTH // HEAD_DIM
KV_HEADS = 2
GQA_GROUP = ATTN_HEADS // KV_HEADS
WINDOW = 128
ATTN_BLOCK = 128
ROPE_THETA = 10000.0

GLA_WIDTH = MIX_WIDTH - ATTN_WIDTH
GLA_HEADS = 4
GLA_KEY_WIDTH = GLA_WIDTH // 2
GLA_DK = GLA_KEY_WIDTH // GLA_HEADS
GLA_DV = GLA_WIDTH // GLA_HEADS
GLA_DECAY_RANK = 16
GLA_GATE_NORMALIZER = 16.0
GLA_CHUNK = 64

D_FF_2 = 5632
CONV_WIDTH = 3
NORM_EPS = 1e-6

IN_WIDTHS = (ATTN_WIDTH,
             KV_HEADS * HEAD_DIM,
             KV_HEADS * HEAD_DIM,
             GLA_KEY_WIDTH,
             GLA_KEY_WIDTH,
             GLA_WIDTH,
             GLA_WIDTH,
             GLA_DECAY_RANK,
             GLA_DECAY_RANK)
IN_TOTAL = sum(IN_WIDTHS)


def rms_norm(x, g):
    xf = x.astype(jnp.float32)
    y = xf * lax.rsqrt(jnp.mean(xf * xf, axis=-1, keepdims=True) + NORM_EPS)
    return (y * g.astype(jnp.float32)).astype(x.dtype)

def rope(x, pos):
    half = x.shape[-1] // 2
    inv = 1.0 / (ROPE_THETA ** (jnp.arange(half, dtype=jnp.float32) / half))
    ang = pos.astype(jnp.float32)[:, None] * inv[None, :]
    cos = jnp.cos(ang)[:, None, :]
    sin = jnp.sin(ang)[:, None, :]
    xf = x.astype(jnp.float32)
    x1, x2 = xf[..., :half], xf[..., half:]
    return jnp.concatenate([x1 * cos - x2 * sin, x2 * cos + x1 * sin], axis=-1).astype(x.dtype)

def window_attention(q, k, v, sink):
    B, T, HQ, D = q.shape
    nb = T // ATTN_BLOCK
    qb = q.reshape(B, nb, ATTN_BLOCK, KV_HEADS, GQA_GROUP, D)
    pad = ((0, 0), (ATTN_BLOCK, ATTN_BLOCK), (0, 0), (0, 0))
    kb = jnp.pad(k, pad).reshape(B, nb + 2, ATTN_BLOCK, KV_HEADS, D)
    vb = jnp.pad(v, pad).reshape(B, nb + 2, ATTN_BLOCK, KV_HEADS, D)
    kw = jnp.concatenate([kb[:, :-2], kb[:, 1:-1], kb[:, 2:]], axis=2)
    vw = jnp.concatenate([vb[:, :-2], vb[:, 1:-1], vb[:, 2:]], axis=2)
    s = jnp.einsum('bnqhgd,bnshd->bhgnqs', qb, kw).astype(jnp.float32) * (D ** -0.5)
    qi = jnp.arange(ATTN_BLOCK)[:, None]
    sj = jnp.arange(3 * ATTN_BLOCK)[None, :]
    rel = sj - ATTN_BLOCK - qi
    kpos = jnp.arange(nb)[:, None, None] * ATTN_BLOCK - ATTN_BLOCK + sj[None]
    mask = (jnp.abs(rel) <= WINDOW)[None] & (kpos >= 0) & (kpos < T)
    s = jnp.where(mask, s, -jnp.inf)
    sk = sink.astype(jnp.float32).reshape(KV_HEADS, GQA_GROUP)[None, :, :, None, None, None]
    m = jnp.maximum(jnp.max(s, axis=-1, keepdims=True), sk)
    p = jnp.exp(s - m)
    p = p / (jnp.sum(p, axis=-1, keepdims=True) + jnp.exp(sk - m))
    o = jnp.einsum('bhgnqs,bnshd->bnqhgd', p.astype(v.dtype), vw)
    return o.reshape(B, T, HQ * D)

def gla_chunked(q, k, v, g, strict):
    B, H, T, DK = q.shape
    DV = v.shape[-1]
    C = GLA_CHUNK
    n = T // C
    q = q.reshape(B, H, n, C, DK)
    k = k.reshape(B, H, n, C, DK)
    g = g.reshape(B, H, n, C, DK)
    v = v.reshape(B, H, n, C, DV)
    b = jnp.cumsum(g, axis=3)
    b_last = b[:, :, :, -1:, :]
    b_ref = b[:, :, :, C // 2:C // 2 + 1, :]
    a = jnp.einsum('bhnid,bhnjd->bhnij', q * jnp.exp(b - b_ref), k * jnp.exp(b_ref - b))
    mask = jnp.tril(jnp.ones((C, C), dtype=bool), -1 if strict else 0)
    a = jnp.where(mask, a, 0.0)
    o_intra = jnp.einsum('bhnij,bhnje->bhnie', a, v)
    q_in = q * jnp.exp(b)
    k_out = k * jnp.exp(b_last - b)
    chunk_decay = jnp.exp(b_last[:, :, :, 0, :])

    def step(state, inp):
        qc, kc, vc, dc = inp
        o = jnp.einsum('bhid,bhde->bhie', qc, state)
        state = state * dc[..., None] + jnp.einsum('bhjd,bhje->bhde', kc, vc)
        return state, o

    s0 = jnp.zeros((B, H, DK, DV), jnp.float32)
    xs = (jnp.moveaxis(q_in, 2, 0), jnp.moveaxis(k_out, 2, 0),
          jnp.moveaxis(v, 2, 0), jnp.moveaxis(chunk_decay, 2, 0))
    _, o_inter = lax.scan(step, s0, xs)
    o_inter = jnp.moveaxis(o_inter, 0, 2)
    return (o_intra + o_inter).reshape(B, H, T, DV)

def bidirectional_gla(q, k, v, lr_f, lr_b, wa2_f, ba_f, wa2_b, ba_b, gate, out_norm_g):
    B, T, _ = q.shape
    f32 = jnp.float32

    def heads(t, d):
        return jnp.transpose(t.astype(f32).reshape(B, T, GLA_HEADS, d), (0, 2, 1, 3))

    qh = heads(q, GLA_DK) * (GLA_DK ** -0.5)
    kh = heads(k, GLA_DK)
    vh = heads(v, GLA_DV)
    g_f = jax.nn.log_sigmoid((lr_f @ wa2_f + ba_f).astype(f32)) / GLA_GATE_NORMALIZER
    g_b = jax.nn.log_sigmoid((lr_b @ wa2_b + ba_b).astype(f32)) / GLA_GATE_NORMALIZER
    gf = heads(g_f, GLA_DK)
    gb = heads(g_b, GLA_DK)
    o_fwd = gla_chunked(qh, kh, vh, gf, strict=False)
    flip = lambda t: jnp.flip(t, axis=2)
    o_bwd = flip(gla_chunked(flip(qh), flip(kh), flip(vh), flip(gb), strict=True))
    o = jnp.transpose(o_fwd + o_bwd, (0, 2, 1, 3)).astype(v.dtype)
    o = rms_norm(o, out_norm_g)
    o = o * jax.nn.silu(gate.reshape(B, T, GLA_HEADS, GLA_DV))
    return o.reshape(B, T, GLA_WIDTH)

def conv_gated_ffn(h, w_up, conv_w, conv_b, w_down):
    u = h @ w_up
    up_ = jnp.pad(u, ((0, 0), (1, 1), (0, 0)))
    u = up_[:, :-2] * conv_w[0] + up_[:, 1:-1] * conv_w[1] + up_[:, 2:] * conv_w[2] + conv_b
    gate, val = jnp.split(u, 2, axis=-1)
    return (jax.nn.silu(gate) * val) @ w_down

def hybrid_layer(x, norm1_g, w_in, q_norm_g, k_norm_g, sink, wa2_f, ba_f, wa2_b, ba_b,
                 gla_out_norm_g, w_out, norm2_g, w_up, conv_w, conv_b, w_down):
    B, T, _ = x.shape
    pos = jnp.arange(T, dtype=jnp.int32)
    h = rms_norm(x, norm1_g)
    proj = h @ w_in
    offsets = []
    acc = 0
    for w in IN_WIDTHS[:-1]:
        acc += w
        offsets.append(acc)
    q_a, k_a, v_a, q_g, k_g, v_g, gate_g, lr_f, lr_b = jnp.split(proj, offsets, axis=-1)
    qa = rope(rms_norm(q_a.reshape(B, T, ATTN_HEADS, HEAD_DIM), q_norm_g), pos)
    ka = rope(rms_norm(k_a.reshape(B, T, KV_HEADS, HEAD_DIM), k_norm_g), pos)
    va = v_a.reshape(B, T, KV_HEADS, HEAD_DIM)
    o_attn = window_attention(qa, ka, va, sink)
    o_gla = bidirectional_gla(q_g, k_g, v_g, lr_f, lr_b, wa2_f, ba_f, wa2_b, ba_b,
                              gate_g, gla_out_norm_g)
    x = x + jnp.concatenate([o_attn, o_gla], axis=-1) @ w_out
    x = x + conv_gated_ffn(rms_norm(x, norm2_g), w_up, conv_w, conv_b, w_down)
    return x

def second_inputs(seed: int = 0) -> dict:
    key = jax.random.key(seed)
    ks = jax.random.split(key, 20)
    f32 = jnp.float32
    L = DEPTH

    def nrm(k, shape, scale):
        return jax.random.normal(k, shape, f32) * scale

    return {
        "x": nrm(ks[0], (BATCH, SEQ, D_MODEL), 1.0),
        "norm1_g": 1.0 + nrm(ks[1], (L, D_MODEL), 0.02),
        "w_in": nrm(ks[2], (L, D_MODEL, IN_TOTAL), D_MODEL ** -0.5),
        "attn_q_norm_g": 1.0 + nrm(ks[3], (L, HEAD_DIM), 0.02),
        "attn_k_norm_g": 1.0 + nrm(ks[4], (L, HEAD_DIM), 0.02),
        "attn_sink": nrm(ks[5], (L, ATTN_HEADS), 0.5),
        "gla_wa2_fwd": nrm(ks[6], (L, GLA_DECAY_RANK, GLA_KEY_WIDTH), GLA_DECAY_RANK ** -0.5),
        "gla_ba_fwd": nrm(ks[7], (L, GLA_KEY_WIDTH), 0.1),
        "gla_wa2_bwd": nrm(ks[8], (L, GLA_DECAY_RANK, GLA_KEY_WIDTH), GLA_DECAY_RANK ** -0.5),
        "gla_ba_bwd": nrm(ks[9], (L, GLA_KEY_WIDTH), 0.1),
        "gla_out_norm_g": 1.0 + nrm(ks[10], (L, GLA_DV), 0.02),
        "w_out": nrm(ks[11], (L, MIX_WIDTH, D_MODEL), MIX_WIDTH ** -0.5),
        "norm2_g": 1.0 + nrm(ks[12], (L, D_MODEL), 0.02),
        "w_up": nrm(ks[13], (L, D_MODEL, 2 * D_FF_2), D_MODEL ** -0.5),
        "conv_w": nrm(ks[14], (L, CONV_WIDTH, 2 * D_FF_2), CONV_WIDTH ** -0.5),
        "conv_b": nrm(ks[15], (L, 2 * D_FF_2), 0.02),
        "w_down": nrm(ks[16], (L, D_FF_2, D_MODEL), D_FF_2 ** -0.5),
    }

def second_block(x, norm1_g, w_in, attn_q_norm_g, attn_k_norm_g, attn_sink, gla_wa2_fwd,
              gla_ba_fwd, gla_wa2_bwd, gla_ba_bwd, gla_out_norm_g, w_out, norm2_g,
              w_up, conv_w, conv_b, w_down):
    for l in range(DEPTH):
        x = hybrid_layer(x, norm1_g[l], w_in[l], attn_q_norm_g[l], attn_k_norm_g[l],
                         attn_sink[l], gla_wa2_fwd[l], gla_ba_fwd[l], gla_wa2_bwd[l],
                         gla_ba_bwd[l], gla_out_norm_g[l], w_out[l], norm2_g[l],
                         w_up[l], conv_w[l], conv_b[l], w_down[l])
    return x


def setup_inputs(seed=0):
    out = dict(first_inputs(seed))
    for name, value in second_inputs(seed + 1).items():
        if name != "x":
            out[name + "_2"] = value
    return out


def reference(
    x, norm_mix_w, w_in, conv_w, a_log, dt_bias, onorm_w, rpb, w_proj_a, w_proj_b, w_out,
    norm_mlp_w, w_mlp_up, w_mlp_down, norm_final_w, norm1_g_2, w_in_2, attn_q_norm_g_2,
    attn_k_norm_g_2, attn_sink_2, gla_wa2_fwd_2, gla_ba_fwd_2, gla_wa2_bwd_2, gla_ba_bwd_2,
    gla_out_norm_g_2, w_out_2, norm2_g_2, w_up_2, conv_w_2, conv_b_2, w_down_2,
):
    x = first_block(
        x, norm_mix_w, w_in, conv_w, a_log, dt_bias, onorm_w, rpb, w_proj_a, w_proj_b, w_out,
        norm_mlp_w, w_mlp_up, w_mlp_down, norm_final_w,
    )
    return second_block(
        x, norm1_g_2, w_in_2, attn_q_norm_g_2, attn_k_norm_g_2, attn_sink_2, gla_wa2_fwd_2,
        gla_ba_fwd_2, gla_wa2_bwd_2, gla_ba_bwd_2, gla_out_norm_g_2, w_out_2, norm2_g_2, w_up_2,
        conv_w_2, conv_b_2, w_down_2,
    )


_drawn_inputs = setup_inputs


def setup_inputs(seed=0):
    import zlib

    import numpy as np

    out = dict(_drawn_inputs(seed))
    spreads = {}
    factors = {'norm_mix_w': 3.52,
     'onorm_w': 6.092,
     'rpb': 4.103,
     'norm1_g_2': 2.811,
     'attn_q_norm_g_2': 8.0,
     'attn_k_norm_g_2': 8.0,
     'attn_sink_2': 8.0,
     'gla_ba_fwd_2': 4.099,
     'gla_ba_bwd_2': 4.47,
     'gla_out_norm_g_2': 6.41,
     'norm2_g_2': 3.897,
     'conv_b_2': 4.22,
     'norm_mlp_w': 5.08}
    for name, (base, spread) in spreads.items():
        noise = np.random.default_rng([zlib.crc32(name.encode()), seed]).standard_normal(out[name].shape)
        drawn = base * np.exp(spread * noise) if base else spread * noise
        out[name] = __import__('jax').numpy.asarray(drawn.astype(out[name].dtype))
    for name, factor in factors.items():
        out[name] = (out[name] * factor).astype(out[name].dtype)
    return out
```

```python
from contextlib import ExitStack

import numpy as np
import concourse.bass as bass
from concourse import mybir

ALU = mybir.AluOpType
ACT = mybir.ActivationFunctionType
F32 = mybir.dt.float32
F32R = mybir.dt.float32r
U32 = mybir.dt.uint32
AXX = mybir.AxisListType.X

P = 128
SEQ = 256
TT = SEQ // P
D = 2048
KT = D // P
DFF = 4 * D
DFF2 = 5632
HEADS = 8
HD = 128
CHUNK = 64
NCH = SEQ // CHUNK
GRID_W, WIN_C = 64, 16
GLA_H, GLA_DV = 4, 256
LEVELS = 6
EPS = 1e-6
NEG = -1e30
SCALE = float(HD) ** -0.5
BLK_KT = 4
BLK_N = 512
RAW_SLOTS = 4
HL_SLOTS = 2

C_QK, C_V, C_DN, C_Z, C_BA, C_GATES = 0, 2048, 3072, 6144, 7168, 7200
D_QA, D_KV, D_QKG, D_VG, D_GG, D_LR = 0, 1024, 1536, 2560, 3584, 4608


def constants():
    p = np.arange(P)
    j, i = p[:, None], p[None, :]
    same = (j // CHUNK) == (i // CHUNK)
    fwd, bwd = same & (j <= i), same & (j >= i)
    out = {"ident": np.eye(P), "tri": np.stack([fwd, bwd], 1), "block": same,
           "neg": np.stack([np.where(m, 0, NEG) for m in (fwd, bwd)], 1),
           "half": np.stack([p < CHUNK, p >= CHUNK], 1)}
    level = np.zeros((P, 2, LEVELS, P))
    for n in range(LEVELS):
        s = 1 << n
        pair = (j // (2 * s)) == (i // (2 * s))
        level[:, 0, n] = pair & (j // s < i // s)
        level[:, 1, n] = pair & (j // s > i // s)
    out["level"] = level
    out["causal"] = np.stack([fwd, same & (j > i)], 1)
    out["flip"] = (same & (j % GRID_W + i % GRID_W == GRID_W - 1)) / SCALE
    q = p[:, None] + P * np.arange(TT)[None, :]
    k = np.arange(SEQ)
    cs = np.clip(q % GRID_W - WIN_C // 2, 0, GRID_W - WIN_C)[..., None]
    out["window"] = np.where((k % GRID_W >= cs) & (k % GRID_W < cs + WIN_C), 0, NEG)
    out["band"] = np.where(np.abs(k - q[..., None]) <= P, 0, NEG)
    half = HD // 2
    inv = (1.0 / (np.float32(10000.0) ** (np.arange(half, dtype=np.float32) / np.float32(half)))).astype(np.float32)
    ang = q.astype(np.float32)[..., None] * inv
    out["cos"], out["sin"] = np.cos(ang), np.sin(ang)
    return {n: np.ascontiguousarray(a, dtype=np.float32).reshape(P, -1) for n, a in out.items()}


CONST_SHAPES = {"ident": (P,), "tri": (2, P), "block": (P,), "neg": (2, P), "half": (2,), "level": (2, LEVELS, P),
                "causal": (2, P), "window": (TT, SEQ), "band": (TT, SEQ), "cos": (TT, HD // 2),
                "sin": (TT, HD // 2)}


class Chunk:
    def __init__(self, w, row, col, blocks, kind, kt0=0, n=BLK_N):
        self.w, self.row, self.col, self.blocks, self.kind, self.kt0, self.n = w, row, col, blocks, kind, kt0, n


class Phase:
    def __init__(self, body, trips, step, act):
        self.body, self.trips, self.step, self.act = body, trips, step, act
        self.nb = sum(c.blocks for c in body)
        self.nc = len(body)


def number(phases):
    b = c = 0
    for ph in phases:
        ph.b0, ph.c0 = b, c
        for ch in ph.body:
            ch.b, ch.c = b, c
            b += ch.blocks
            c += 1
        b = ph.b0 + ph.nb * ph.trips
        c = ph.c0 + ph.nc * ph.trips
        assert ph.trips == 1 or (ph.nb % RAW_SLOTS == 0 and ph.nc % 2 == 0)
    return b


class Chain:
    def __init__(self, eng, sem):
        self.eng, self.sem, self.n, self.reg = eng, sem, 0, 0

    def __call__(self, ins):
        ins.then_inc(self.sem, 1)
        self.n += 1
        self.eng.wait_ge(self.sem, self.reg + self.n)
        return ins


class Loop:
    def __init__(self, eng, trips, chain=None, per=0):
        self.eng, self.trips, self.chain, self.per = eng, trips, chain, per

    def __enter__(self):
        if self.chain is not None:
            self.n0 = self.chain.n
        if self.trips == 1:
            return 0
        self.ctx = self.eng.Fori(0, self.trips)
        i = self.ctx.__enter__()
        if self.chain is not None:
            self.chain.reg = i * self.per
        return i

    def __exit__(self, *e):
        if self.trips > 1:
            self.ctx.__exit__(*e)
        if self.chain is not None and e[0] is None:
            if self.trips > 1:
                assert self.chain.n - self.n0 == self.per, (self.chain.n - self.n0, self.per)
                self.chain.n = self.n0 + self.per * self.trips
            self.chain.reg = 0


def build(nc, t):
    ctx = ExitStack()
    with ctx:
        def sem(name):
            return ctx.enter_context(nc.semaphore(name))

        BASE = 16512
        RAW0 = BASE
        WH0 = RAW0 + RAW_SLOTS * 8192
        WL0 = WH0 + HL_SLOTS * 8192
        A0 = WL0 + HL_SLOTS * 8192
        R0 = A0 + 32768
        H0 = R0 + 65536
        T0 = H0 + 16384
        K = 1024

        def at(name, shape, off, dt=F32):
            return nc.alloc_sbuf_tensor_at(name, [P] + list(shape), dt, offset=off)

        raw = at("raw", [RAW_SLOTS, BLK_KT, BLK_N], RAW0)
        wh = at("wh", [HL_SLOTS, BLK_KT, BLK_N], WH0, F32R)
        wl = at("wl", [HL_SLOTS, BLK_KT, BLK_N], WL0, F32R)
        a1h = at("a1h", [KT, SEQ], A0, F32R)
        a1l = at("a1l", [KT, SEQ], A0 + 16 * K, F32R)
        a2h = at("a2h", [32, SEQ], R0, F32R)
        a2l = at("a2l", [32, SEQ], R0 + 32 * K, F32R)
        h = at("h", [TT, D], H0)

        tpos = [T0]

        def small(name, shape, dt=F32):
            n = int(np.prod(shape)) * 4
            x = at(name, shape, tpos[0], dt)
            tpos[0] += (n + 31) // 32 * 32
            return x

        ident = small("ident", [P])
        tri = small("tri", [2, P])
        blockm = small("block", [P])
        neg = small("neg", [2, P])
        half = small("half", [2])
        ones = small("ones", [P])
        LV0 = tpos[0]
        level = small("level", [2, LEVELS, P])
        causal = at("causal", [2, P], LV0)
        rope_cs = at("rope_cs", [2, TT, HD // 2], LV0 + 1024)
        cw2 = at("cw2", [3, 88], LV0 + 2048)
        cb2 = at("cb2", [88], LV0 + 3136)
        gq_bc = at("gq_bc", [2, HD], LV0 + 3520)
        gout_bc = at("gout_bc", [GLA_DV], LV0 + 4544)
        sink_bc = at("sink_bc", [HEADS], LV0 + 5568)
        normw = small("normw", [4, KT])
        cw1 = small("cw1", [5, 24])
        dtal = small("dtal", [2, 16])
        onorm = small("onorm", [HD])
        ba = small("ba", [TT, 32])
        sc32 = {n: small(n, [HEADS, 2, TT]) for n in ("bt", "gg", "gc", "gl_c", "bte", "ekg")}
        tmp64 = {n: small(n, [64]) for n in ("ta", "tb", "tc")}
        ghalf = small("ghalf", [2, HEADS, 2, TT])
        glast = small("glast", [2, HEADS, 2, TT])
        st = small("st", [8])
        st8 = small("st8", [64])
        eps = small("eps", [1])
        pdum = small("pdum", [1])
        amx = small("amx", [2, TT]); asm = small("asm", [2, TT]); anm = small("anm", [2, TT]); aes = small("aes", [2, TT])
        S0 = tpos[0]
        assert 229368 - S0 >= 17 * K, 229368 - S0

        dnT = at("dnT", [24, SEQ], R0 + 40 * K)
        attqk = at("attqk", [16, SEQ], R0 + 16 * K)
        attv = at("attv", [TT, 1024], R0 + 8 * K)
        zs = at("zs", [TT, 1024], H0)
        gstage = at("gstage", [2, 1024], H0 + 8 * K)
        cvin = at("cvin", [2, 4, 260], S0)
        cvout = at("cvout", [4, SEQ], S0 + 8352)
        bias = at("bias", [HEADS, TT, SEQ], A0)
        wmask = at("wmask", [TT, SEQ], A0 + 28 * K)
        flip = at("flip", [P], A0 + 30 * K)
        asc = at("asc", [2, TT, SEQ], A0 + 16 * K)
        apr = at("apr", [2, TT, SEQ], A0 + 20 * K)
        apT = at("apT", [2, TT, SEQ], A0 + 24 * K)
        G = 4
        qgT = at("qgT", [G, 2, SEQ], A0)
        kgt = at("kgt", [G, 2, TT, HD], A0 + 8 * K)
        wTs = at("wTs", [G, 2, TT, P], A0 + 16 * K)
        uu = at("uu", [G, 2, TT, HD], A0 + 24 * K)
        qkT = at("qkT", [G, 2, TT, P], R0 + 16 * K)
        kbT = at("kbT", [2, SEQ], R0 + 24 * K)
        kbg = at("kbg", [2, TT, HD], R0 + 24 * K)
        vb = at("vb", [2, TT, HD], R0 + 26 * K)
        egr = at("egr", [2, TT, P], R0 + 28 * K)
        dec = at("dec", [2, TT, P], R0 + 30 * K)
        AT = at("AT", [2, TT, P], R0 + 8 * K)
        TB = at("TB", [2, 4, P], R0 + 10 * K)
        PB = at("PB", [4, P], R0 + 14 * K)
        ATl = at("ATl", [2, TT, LEVELS - 1, P], S0)
        SS = at("SS", [2, G, HD], S0 + 10 * K)
        vn = at("vn", [G, HD], S0 + 14 * K)
        oacc = at("oacc", [TT, HEADS, HD], H0 + 8 * K)
        sqb = at("sqb", [2, 512], S0)
        rtb = at("rtb", [2, 512], S0 + 4 * K)
        osq = at("osq", [TT, HEADS, HD], A0)
        gld = at("gld", [2, 1024], R0 + 16 * K)
        mixa = at("mixa", [1024], R0 + 48 * K)
        mixb = at("mixb", [1024], R0 + 52 * K)
        xs = at("xs", [TT, D], R0)
        junk = at("junk", [D], R0 + 16 * K)
        wrow = at("wrow", [D], R0 + 24 * K)
        ffr = at("ffr", [1024], S0)
        ffq = at("ffq", [1024], S0 + 4 * K)
        qa = at("qa", [TT, 1024], R0 + 16 * K)
        kva = at("kva", [TT, 512], R0 + 24 * K)
        qkg = at("qkg", [8, SEQ], R0 + 48 * K)
        vg = at("vg", [TT, 1024], R0 + 56 * K)
        gg2 = at("gg2", [TT, 1024], S0)
        lrT = at("lrT", [SEQ], S0 + 8 * K)
        wa2 = at("wa2", [2, 512], S0 + 9 * K)
        gtok = at("gtok", [2, TT, 512], R0 + 24 * K)
        rtmp = at("rtmp", [TT, 1024], A0)
        rtmp2 = at("rtmp2", [TT, 1024], A0 + 8 * K)
        qT2 = at("qT2", [10, SEQ], A0 + 16 * K)
        bmask = at("bmask", [TT, SEQ], A0 + 26 * K)
        asc2 = at("asc2", [2, TT, SEQ], A0)
        apr2 = at("apr2", [2, TT, SEQ], A0 + 4 * K)
        apT2 = at("apT2", [2, TT, SEQ], A0 + 8 * K)
        eb = at("eb", [4, SEQ], A0)
        eD = at("eD", [4, SEQ], A0 + 4 * K)
        eE = at("eE", [4, SEQ], A0 + 8 * K)
        qga = at("qga", [4, SEQ], A0 + 12 * K)
        kga = at("kga", [4, SEQ], A0 + 16 * K)
        qin = at("qin", [4, SEQ], A0 + 20 * K)
        kou = at("kou", [4, SEQ], A0 + 24 * K)
        kot = at("kot", [4, TT, P], A0 + 28 * K)
        eb4 = at("eb4", [2048], A0 + 8 * K)
        aTm = at("aTm", [4, TT, P], S0 + 13 * K)
        S2 = at("S2", [2, 4, GLA_DV], R0 + 16 * K)
        oo2 = at("oo2", [TT, 4, GLA_DV], A0)
        oq2 = at("oq2", [TT, 4, GLA_DV], A0 + 8 * K)
        upad = at("upad", [2, 4, 258], S0)
        cg = at("cg", [2, 1024], S0 + 8320)

        bank = [ctx.enter_context(nc.psum_tensor(f"bank{n}", [P, 512], F32)) for n in range(4)]
        gp = [ctx.enter_context(nc.psum_tensor(f"gp{n}", [P, 1024], F32)) for n in range(2)]
        gates_dram = nc.dram_tensor("gates_dram", [8, P, 1024], F32, kind="Internal").ap()

        W1, W2 = t["w_in"], t["w_in_2"]
        acts = {"x1": (a1h, a1l), "hid": (a2h, a2l)}
        full = KT // BLK_KT
        PH = {}
        PH["ba"] = Phase([Chunk(W1, 0, C_BA, 1, "down", n=32)], 1, 0, "x1")
        PH["lead"] = Phase([Chunk(W1, 0, C_V, full, "down")], 1, 0, "x1")
        PH["v"] = Phase([Chunk(W1, 0, C_V + 512, full, "down")], 1, 0, "x1")
        PH["qk"] = Phase([Chunk(W1, 0, C_QK + 512 * n, full, "up") for n in range(2)], 2, 1024, "x1")
        PH["dn"] = Phase([Chunk(W1, 0, C_DN + 512 * n, full, "up") for n in range(2)], 3, 1024, "x1")
        PH["z"] = Phase([Chunk(W1, 0, C_Z + 512 * n, full, "down") for n in range(2)], 1, 0, "x1")
        PH["gates0"] = Phase([Chunk(W1, 0, C_GATES + 512 * n, full, "up") for n in range(2)], 1, 0, "x1")
        PH["gates"] = Phase([Chunk(W1, 0, C_GATES + 1024 + 512 * n, full, "up") for n in range(2)], 3, 1024, "x1")
        PH["mix"] = Phase([Chunk(t["w_proj_a"], 0, 0, 2, "up", 0), Chunk(t["w_proj_b"], 0, 0, 2, "up", 8)], 4, 512, "hid")
        PH["out"] = Phase([Chunk(t["w_out"], 0, 512 * n, full, "down") for n in range(2)], 2, 1024, "x1")
        for g in range(2):
            PH[f"up{g}"] = Phase([Chunk(t["w_mlp_up"], 0, 4096 * g + 512 * n, full, "up") for n in range(2)], 4, 1024, "x1")
            PH[f"down{g}"] = Phase([Chunk(t["w_mlp_down"], 4096 * g, 512 * n, 8, "down") for n in range(2)], 2, 1024, "hid")
        PH["lr"] = Phase([Chunk(W2, 0, D_LR, 1, "up", n=32)], 1, 0, "x1")
        PH["kv"] = Phase([Chunk(W2, 0, D_KV, full, "down")], 1, 0, "x1")
        PH["qa"] = Phase([Chunk(W2, 0, D_QA + 512 * n, full, "down") for n in range(2)], 1, 0, "x1")
        PH["qkg"] = Phase([Chunk(W2, 0, D_QKG + 512 * n, full, "up") for n in range(2)], 1, 0, "x1")
        PH["vg"] = Phase([Chunk(W2, 0, D_VG + 512 * n, full, "down") for n in range(2)], 1, 0, "x1")
        PH["gg"] = Phase([Chunk(W2, 0, D_GG + 512 * n, full, "down") for n in range(2)], 1, 0, "x1")
        PH["out2"] = Phase([Chunk(t["w_out_2"], 0, 512 * n, full, "down") for n in range(2)], 2, 1024, "hid")
        for g, (n0, n1) in enumerate(((0, 6), (6, 11))):
            PH[f"ff{g}"] = Phase([Chunk(t["w_up_2"], 0, base + 512 * n0, full, "up") for base in (0, DFF2)],
                                 n1 - n0, 512, "x1")
            nk = (n1 - n0)
            PH[f"dd{g}"] = Phase([Chunk(t["w_down_2"], 512 * n0, 512 * n, nk, "down") for n in range(4)], 1, 0, "hid")
        order = ["ba", "lead", "v", "qk", "dn", "z", "gates0", "gates", "mix", "out", "up0", "down0", "up1", "down1",
                 "lr", "kv", "qa", "qkg", "vg", "gg", "out2", "ff0", "dd0", "ff1", "dd1"]
        phases = [PH[n] for n in order]
        BLOCKS = number(phases)

        s_raw = [sem(f"s_raw{n}") for n in range(RAW_SLOTS)]
        s_hi, s_lo = sem("s_hi"), sem("s_lo")
        s_blk = sem("s_blk")
        s_free = [sem(f"s_free{n}") for n in range(2)]
        s_act, s_dve, s_pool = sem("s_act"), sem("s_dve"), sem("s_pool")
        names = ("s_const s_const2 s_x s_hx s_ss s_ms s_rt s_xs s_tr s_trh s_trl s_cvo "
                 "  s_bias s_qk s_sc s_mx s_ex s_p s_pt s_pT s_o s_ah s_al  s_bag  s_lsq s_lsum s_lrt s_lfree "
                 "s_gate s_gcm s_gcols   s_r1 s_r1a  s_gram s_dm s_AT s_ATl s_t1p s_t1 s_P s_Pc s_X s_TB s_tok s_tokd "
                 "s_uw s_uwc s_ws s_vn s_os s_oc s_su s_S s_or s_ord s_mixa s_mixh s_mixl  s_ffh s_ffl  s_norm  "
                 " s_qr  s_qn s_q2T s_q2c s_gt s_gta s_gtd s_bm s_bc s_bD s_bE  s_aTp s_aTm s_kop s_koc "
                 "s_kv2 s_S2  s_oev s_or2 s_or2d s_cv  s_store s_od s_qg s_kb s_qks s_t1d s_eb s_ea s_oin s_oi s_sil s_prod s_cv2 "
                 "s_wrow s_roped s_wa s_waz s_wal s_wm s_set").split()
        s_gst = [sem(f"s_gst{n}") for n in range(2)]
        s_gld = [sem(f"s_gld{n}") for n in range(2)]
        S = {n: sem(n) for n in names}

        def raw_value(idx, i, nb):
            return 16 * (idx // RAW_SLOTS + 1) + i * (16 * nb // RAW_SLOTS)

        def last_block(ph):
            return ph.b0 + ph.nb * ph.trips

        NCONST = 18
        NCONST2 = 11
        TG = {"mix": 0, "yb": 8, "mlp": 12, "norm1": 20, "cat": 28, "norm2": 32}
        NS = {"mix": 0, "mlp": 1, "final": 2, "norm1": 3, "norm2": 4}

        def wait_read_out(eng, ph, trip, n):
            ch = ph.body[n]
            eng.wait_ge(s_free[ch.c % 2], ch.c // 2 + 1 + trip * (ph.nc // 2))

        block = ctx.enter_context(nc.Block())

        @block.sync
        def _(sp):
            def stream(ph):
                with Loop(sp, ph.trips) as i:
                    for ch in ph.body:
                        for j in range(ch.blocks):
                            idx = ch.b + j
                            slot = idx % RAW_SLOTS
                            if idx >= RAW_SLOTS:
                                sp.wait_ge(s_hi, idx - RAW_SLOTS + 1 + i * ph.nb)
                                sp.wait_ge(s_lo, idx - RAW_SLOTS + 1 + i * ph.nb)
                            if ch.n == BLK_N:
                                rows = ch.w[ch.row + j * 512:ch.row + (j + 1) * 512, :]
                                src = rows.rearrange("(t p) n -> p t n", p=P)[:, :, bass.ds(ch.col + i * ph.step, BLK_N)] \
                                    if ph.trips > 1 else rows.rearrange("(t p) n -> p t n", p=P)[:, :, ch.col:ch.col + BLK_N]
                                sp.dma_start(raw[:, slot], src).then_inc(s_raw[slot], 16)
                            else:
                                src = ch.w.rearrange("(t p) n -> p t n", p=P)[:, :, ch.col:ch.col + ch.n]
                                dst = raw[:, slot, 0, :].rearrange("p (t n) -> p t n", n=ch.n)
                                sp.dma_start(dst, src).then_inc(s_raw[slot], 16)
            sp.dma_start(h[:, :, :], t["x"][0].rearrange("(t p) n -> p t n", p=P)).then_inc(S["s_x"], 16)
            for name in order:
                stream(PH[name])
            wait_read_out(sp, PH["dd1"], 0, 2)
            wait_read_out(sp, PH["dd1"], 0, 3)
            sp.dma_start(t["out"][0].rearrange("(t p) n -> p t n", p=P), h[:, :, :]).then_inc(S["s_store"], 16)
            sp.wait_ge(S["s_store"], 16)

        @block.scalar
        def _(act):
            chain = Chain(act, s_act)

            def split(idx, i, nb):
                if idx >= BLOCKS:
                    return
                act.wait_ge(s_raw[idx % RAW_SLOTS], raw_value(idx, i, nb))
                if idx >= HL_SLOTS:
                    act.wait_ge(s_blk, idx - HL_SLOTS + 1 + i * nb)
                if idx == 0:
                    nc.scalar.copy(wh[:, 0, 0, :], raw[:, 0, 0, :]).then_inc(s_hi, 1)
                else:
                    nc.scalar.copy(wh[:, idx % HL_SLOTS], raw[:, idx % RAW_SLOTS]).then_inc(s_hi, 1)

            def gemm(ph, read_out, per=0):
                with Loop(act, ph.trips, chain, per) as i:
                    for n, ch in enumerate(ph.body):
                        for j in range(ch.blocks):
                            split(ch.b + 2 + j, i, ph.nb)
                        if read_out is not None:
                            act.wait_ge(s_blk, ch.b + ch.blocks + i * ph.nb)
                            read_out(n, i, gp[ch.c % 2], s_free[ch.c % 2])

            def norm_stats(name):
                k = NS[name]
                for tt in range(TT):
                    a = nc.scalar.activation(junk[:, :], h[:, tt, :], ACT.Square, accum_out=st[:, tt:tt + 1])
                    if tt == 0:
                        chain(a)
                    else:
                        a.then_inc(S["s_ss"], 1)
                act.wait_ge(S["s_ms"], k + 1)
                nc.scalar.activation(st[:, 4:6], st[:, 2:4], ACT.Sqrt).then_inc(S["s_rt"], 1)

            def turn_hi(base, groups, dst, kt0, w=None):
                for g in range(groups):
                    act.wait_ge(S["s_tr"], base + g + 1)
                    if w is None:
                        a = nc.scalar.copy(dst[:, kt0 + 2 * g:kt0 + 2 * g + 2, :], bank[g % 4][:, :].rearrange("p (k n) -> p k n", k=2))
                    else:
                        for m in range(2):
                            kt = 2 * g + m
                            a = nc.scalar.activation(dst[:, kt0 + kt, :], bank[g % 4][:, m * SEQ:(m + 1) * SEQ], ACT.Copy,
                                                     scale=normw[:, w, kt:kt + 1])
                    a.then_inc(S["s_trh"], 1)

            def attention(base, scores, probs, probsT, sink):
                for hh in range(HEADS + 2):
                    if hh < HEADS:
                        act.wait_ge(S["s_mx"], base + hh + 1)
                        if hh >= 2:
                            act.wait_ge(S["s_pt"], base + hh - 1)
                        b = hh % 2
                        for tt in range(TT):
                            a = nc.scalar.activation(probs[:, b, tt, :], scores[:, b, tt, :], ACT.Exp,
                                                     bias=anm[:, b, tt:tt + 1], accum_out=asm[:, b, tt:tt + 1])
                        if sink:
                            a = nc.scalar.activation(aes[:, b, :], anm[:, b, :], ACT.Exp, bias=sink_bc[:, hh:hh + 1])
                        a.then_inc(S["s_ex"], 1)
                    if 1 <= hh <= HEADS:
                        k = hh - 1
                        act.wait_ge(S["s_pt"], base + k + 1)
                        if k >= 2:
                            act.wait_ge(S["s_o"], base + k - 1)
                        nc.scalar.copy(probsT[:, k % 2], bank[2 + k % 2][:, :].rearrange("p (k n) -> p k n", k=2)).then_inc(S["s_pT"], 1)
                    if hh >= 2:
                        k = hh - 2
                        act.wait_ge(S["s_o"], base + k + 1)
                        nc.scalar.copy(a2h[:, k, :], gp[0][:, (k % 2) * 512:(k % 2) * 512 + SEQ]).then_inc(S["s_ah"], 1)

            act.wait_ge(S["s_x"], 16)
            norm_stats("mix")
            act.wait_ge(S["s_const"], 16 * NCONST)
            turn_hi(TG["mix"], 8, a1h, 0, 0)
            split(0, 0, 0)
            split(1, 0, 0)

            def to_ba(n, i, g, free):
                nc.scalar.copy(ba[:, :, :], g[:, :].rearrange("p (t n) -> p t n", t=TT)[:, :, 0:32]).then_inc(free, 1)

            def to_v(col):
                def f(n, i, g, free):
                    nc.scalar.copy(attv[:, :, col:col + 512], g[:, :].rearrange("p (t n) -> p t n", t=TT)).then_inc(free, 1)
                return f

            def to_qk(n, i, g, free):
                nc.scalar.copy(attqk[:, bass.ds(8 * i + 4 * n, 4), :], g[:, :].rearrange("p (m n) -> p m n", m=4)).then_inc(free, 1)

            def to_dn(n, i, g, free):
                nc.scalar.copy(cvin[:, n, :, 2:2 + SEQ], g[:, :].rearrange("p (m n) -> p m n", m=4)).then_inc(free, 1)
                act.wait_ge(S["s_cv"], 2 * i + n + 1)
                nc.scalar.activation(dnT[:, bass.ds(8 * i + 4 * n, 4), :], cvout[:, :, :], ACT.Silu).then_inc(S["s_cvo"], 1)

            def to_z(n, i, g, free):
                nc.scalar.activation(zs[:, :, n * 512:(n + 1) * 512], g[:, :].rearrange("p (t n) -> p t n", t=TT),
                                     ACT.Silu).then_inc(free, 1)

            def to_gates0(n, i, g, free):
                nc.scalar.activation(gstage[:, n, :], g[:, :], ACT.Sigmoid).then_inc(free, 1)

            def to_gates(n, i, g, free):
                act.wait_ge(s_gst[n], 16 * i + 16)
                nc.scalar.activation(gstage[:, n, :], g[:, :], ACT.Sigmoid).then_inc(free, 1)

            gemm(PH["ba"], to_ba)
            gemm(PH["lead"], to_v(0))
            gemm(PH["v"], to_v(512))
            gemm(PH["qk"], to_qk)
            gemm(PH["dn"], to_dn)
            gemm(PH["z"], to_z)
            gemm(PH["gates0"], to_gates0)
            gemm(PH["gates"], to_gates)
            attention(0, asc, apr, apT, False)

            tb, tc = tmp64["tb"], tmp64["tc"]
            beta_in = ba[:, :, 0:16].rearrange("p t (d h) -> p h d t", d=2)
            nc.scalar.activation(sc32["bt"][:, :, :, :], beta_in, ACT.Sigmoid).then_inc(S["s_bag"], 1)
            chain(nc.scalar.activation(dtal[:, 1, :], dtal[:, 1, :], ACT.Exp))
            act.wait_ge(S["s_gate"], 1)
            chain(nc.scalar.activation(tc[:, 0:32], tb[:, 0:32], ACT.Exp))
            nc.scalar.activation(tc[:, 0:32], tc[:, 0:32], ACT.Ln, bias=1.0).then_inc(S["s_bag"], 1)
            act.wait_ge(S["s_gcols"], 1)
            nc.scalar.activation(sc32["ekg"][:, :, :, :], sc32["gl_c"][:, :, :, :], ACT.Exp)
            nc.scalar.activation(sc32["bte"][:, :, :, :], sc32["gc"][:, :, :, :], ACT.Exp)
            nc.scalar.activation(glast[:, :, :, :, :], bank[1][:, 64:128].rearrange("p (a h d t) -> p a h d t", a=2, h=8, d=2),
                                 ACT.Exp).then_inc(S["s_bag"], 1)
            for j in range(9):
                if j < 8:
                    if j >= 2:
                        act.wait_ge(S["s_lsum"], j - 1)
                    nc.scalar.activation(sqb[:, j % 2, :], dnT[:, 2 * j:2 * j + 2, :].rearrange("p k n -> p (k n)"), ACT.Square).then_inc(S["s_lsq"], 1)
                if j >= 1:
                    k = j - 1
                    act.wait_ge(S["s_lsum"], k + 1)
                    if k >= 2:
                        act.wait_ge(S["s_lfree"], k - 1)
                    nc.scalar.activation(rtb[:, k % 2, :], bank[2 + k % 2][:, :], ACT.Sqrt, bias=eps[:, 0:1]).then_inc(S["s_lrt"], 1)
            for hh in range(HEADS):
                g = hh % G
                act.wait_ge(S["s_dm"], hh + 1)
                if hh >= 1:
                    act.wait_ge(S["s_qg"], hh)
                nc.scalar.activation(egr[:, :, :, :], bank[0][:, :].rearrange("p (d t n) -> p d t n", d=2, t=TT), ACT.Exp).then_inc(S["s_r1a"], 1)
                nc.scalar.activation(dec[:, :, :, :], dec[:, :, :, :], ACT.Exp).then_inc(S["s_r1a"], 1)
                act.wait_ge(S["s_t1p"], hh + 1)
                nc.scalar.copy(TB[:, 0, :, :], bank[0][:, :].rearrange("p (q n) -> p q n", q=4)).then_inc(S["s_t1"], 1)
                for n in range(1, LEVELS):
                    act.wait_ge(S["s_P"], 5 * hh + n)
                    nc.scalar.copy(PB[:, :, :], bank[0][:, :].rearrange("p (q n) -> p q n", q=4)).then_inc(S["s_Pc"], 1)
                act.wait_ge(S["s_uw"], hh + 1)
                nc.scalar.copy(uu[:, g], gp[1][:, 0:512].rearrange("p (d t n) -> p d t n", d=2, t=TT))
                nc.scalar.copy(wTs[:, g], gp[1][:, 512:1024].rearrange("p (d t n) -> p d t n", d=2, t=TT)).then_inc(S["s_uwc"], 1)
                if g == G - 1:
                    gr = hh // G
                    for s in range(2):
                        act.wait_ge(S["s_os"], 4 * gr + s + 1)
                        for d in range(2):
                            c = s if d == 0 else NCH - 1 - s
                            lo, tl = CHUNK * (c % 2), c // 2
                            a = nc.scalar.copy(oacc[lo:lo + CHUNK, tl, G * gr:G * gr + G, :],
                                               bank[1][lo:lo + CHUNK, :].rearrange("p (g n) -> p g n", g=G))
                        a.then_inc(S["s_oc"], 1)
            act.wait_ge(S["s_od"], 4)
            nc.scalar.activation(osq[:, :, :, :], oacc[:, :, :, :], ACT.Square).then_inc(S["s_or"], 1)
            act.wait_ge(S["s_ord"], 1)
            nc.scalar.activation(st8[:, 16:32], st8[:, 0:16], ACT.Sqrt).then_inc(S["s_or"], 1)
            turn_hi(TG["yb"], 4, a2h, 8)

            def to_mix(n, i, g, free):
                if n == 1:
                    act.wait_ge(S["s_mixa"], i + 1)
                    nc.scalar.copy(a1h[:, bass.ds(4 * i, 4), :], mixb[:, :].rearrange("p (m n) -> p m n", m=4)).then_inc(S["s_mixh"], 1)
            gemm(PH["mix"], to_mix)
            gemm(PH["out"], None)

            def wait_products(ph):
                wait_read_out(act, ph, ph.trips - 1, ph.nc - 2)
                wait_read_out(act, ph, ph.trips - 1, ph.nc - 1)

            wait_products(PH["out"])
            norm_stats("mlp")
            turn_hi(TG["mlp"], 8, a1h, 0, 1)

            def to_hidden(ph):
                def f(n, i, g, free):
                    nc.scalar.activation(ffr[:, :], g[:, :], ACT.Relu).then_inc(free, 1)
                    wait_read_out(act, ph, i, n)
                    chain(nc.scalar.activation(ffq[:, :], ffr[:, :], ACT.Square))
                    nc.scalar.copy(a2h[:, bass.ds(8 * i + 4 * n, 4), :], ffq[:, :].rearrange("p (m n) -> p m n", m=4)).then_inc(S["s_ffh"], 1)
                return f

            for k in range(2):
                gemm(PH[f"up{k}"], to_hidden(PH[f"up{k}"]), 2)
                gemm(PH[f"down{k}"], None)
            wait_products(PH["down1"])
            norm_stats("final")
            act.wait_ge(S["s_norm"], 1)
            norm_stats("norm1")
            turn_hi(TG["norm1"], 8, a1h, 0, 2)

            def to_lr(n, i, g, free):
                nc.scalar.copy(lrT[0:32, :], g[0:32, 0:SEQ]).then_inc(free, 1)

            def to_rows(dst, func=ACT.Copy):
                def f(n, i, g, free):
                    nc.scalar.activation(dst[:, :, n * 512:(n + 1) * 512], g[:, :].rearrange("p (t n) -> p t n", t=TT), func).then_inc(free, 1)
                return f

            def to_qkg(n, i, g, free):
                nc.scalar.copy(qkg[:, 4 * n:4 * n + 4, :], g[:, :].rearrange("p (m n) -> p m n", m=4)).then_inc(free, 1)

            gemm(PH["lr"], to_lr)
            gemm(PH["kv"], to_rows(kva))
            gemm(PH["qa"], to_rows(qa))
            gemm(PH["qkg"], to_qkg)
            gemm(PH["vg"], to_rows(vg))
            gemm(PH["gg"], to_rows(gg2, ACT.Silu))
            act.wait_ge(s_blk, last_block(PH["gg"]))
            chain(nc.scalar.activation(rtmp[:, :, :], qa[:, :, :], ACT.Square))
            nc.scalar.activation(rtmp2[:, :, 0:256], kva[:, :, 0:256], ACT.Square).then_inc(S["s_qr"], 1)
            act.wait_ge(S["s_qn"], 1)
            nc.scalar.activation(st8[:, 32:52], st8[:, 0:20], ACT.Sqrt).then_inc(S["s_qr"], 1)
            for g in range(5):
                act.wait_ge(S["s_q2T"], g + 1)
                nc.scalar.copy(qT2[:, 2 * g:2 * g + 2, :], bank[g % 4][:, :].rearrange("p (k n) -> p k n", k=2)).then_inc(S["s_q2c"], 1)
            attention(HEADS, asc2, apr2, apT2, True)
            act.wait_ge(S["s_al"], 2 * HEADS)
            for q in range(4):
                act.wait_ge(S["s_gt"], q + 1)
                a = nc.scalar.copy(gtok[:, q // 2, q % 2, :], bank[q][:, :])
            a.then_inc(S["s_gta"], 1)
            act.wait_ge(S["s_gtd"], 1)
            chain(nc.scalar.activation(eb4[:, :], eb4[:, :], ACT.Exp))
            nc.scalar.activation(eb4[:, :], eb4[:, :], ACT.Ln, bias=1.0).then_inc(S["s_gta"], 1)
            for d in range(2):
                last = CHUNK - 1 if d == 0 else 0
                act.wait_ge(S["s_bc"], d + 1)
                if d:
                    act.wait_ge(S["s_bE"], 3)
                    act.wait_ge(S["s_aTp"], 1)
                    act.wait_ge(S["s_oin"], 1)
                nc.scalar.activation(eb[:, :, :], gp[0][:, :].rearrange("p (h n) -> p h n", h=4), ACT.Copy, scale=1.0 / 16).then_inc(S["s_eb"], 1)
                act.wait_ge(S["s_eb"], d + 1)
                chain(nc.scalar.activation(st8[:, 0:16].rearrange("p (h c) -> p h c", h=4),
                                           eb[:, :, :].rearrange("p h (c n) -> p h c n", n=CHUNK)[:, :, :, last], ACT.Exp))
                nc.scalar.activation(qin[:, :, :], eb[:, :, :], ACT.Exp).then_inc(S["s_ea"], 1)
                act.wait_ge(S["s_bD"], 2 * d + 1)
                nc.scalar.activation(qga[:, :, :], eD[:, :, :], ACT.Exp)
                nc.scalar.activation(kga[:, :, :], eD[:, :, :], ACT.Exp, scale=-1.0).then_inc(S["s_ea"], 1)
                act.wait_ge(S["s_bD"], 2 * d + 2)
                nc.scalar.activation(kou[:, :, :], eE[:, :, :], ACT.Exp, scale=-1.0).then_inc(S["s_ea"], 1)
                act.wait_ge(S["s_kop"], d + 1)
                nc.scalar.copy(kot[:, :, :, :], gp[0][:, :].rearrange("p (h t n) -> p h t n", h=4, t=TT)).then_inc(S["s_koc"], 1)
            act.wait_ge(S["s_oin"], 2)
            for tt in range(TT):
                for k in range(2):
                    a = nc.scalar.copy(oo2[:, tt, 2 * k:2 * k + 2, :], bank[2 * tt + k][:, :].rearrange("p (h n) -> p h n", h=2))
            a.then_inc(S["s_oev"], 1)
            act.wait_ge(S["s_oev"], 1)
            nc.scalar.activation(oq2[:, :, :, :], oo2[:, :, :, :], ACT.Square).then_inc(S["s_or2"], 1)
            act.wait_ge(S["s_or2d"], 1)
            nc.scalar.activation(st8[:, 16:24], st8[:, 0:8], ACT.Sqrt).then_inc(S["s_or2"], 1)
            turn_hi(TG["cat"], 4, a2h, 8)
            gemm(PH["out2"], None)
            wait_products(PH["out2"])
            norm_stats("norm2")
            turn_hi(TG["norm2"], 8, a1h, 0, 3)

            def to_ff(count0):
                def f(n, i, g, free):
                    nc.scalar.copy(upad[:, n, :, 1:1 + SEQ], g[:, :].rearrange("p (m n) -> p m n", m=4)).then_inc(free, 1)
                    if n == 1:
                        act.wait_ge(S["s_cv2"], count0 + i + 1)
                        nc.scalar.activation(cg[:, 0, :], cg[:, 0, :], ACT.Silu).then_inc(S["s_sil"], 1)
                        act.wait_ge(S["s_prod"], count0 + i + 1)
                        nc.scalar.copy(a2h[:, bass.ds(4 * i, 4), :], cg[:, 1, :].rearrange("p (m n) -> p m n", m=4)).then_inc(S["s_ffh"], 1)
                return f
            gemm(PH["ff0"], to_ff(0))
            gemm(PH["dd0"], None)
            gemm(PH["ff1"], to_ff(6))
            gemm(PH["dd1"], None)

        @block.vector
        def _(dve):
            V = nc.vector
            chain = Chain(dve, s_dve)

            def split(idx, i, nb):
                if idx >= BLOCKS:
                    return
                dve.wait_ge(s_raw[idx % RAW_SLOTS], raw_value(idx, i, nb))
                dve.wait_ge(s_hi, idx + 1 + i * nb)
                if idx == 0:
                    V.tensor_tensor(wl[:, 0, 0, :], raw[:, 0, 0, :], wh[:, 0, 0, :].bitcast(F32), ALU.subtract).then_inc(s_lo, 1)
                else:
                    V.tensor_tensor(wl[:, idx % HL_SLOTS], raw[:, idx % RAW_SLOTS], wh[:, idx % HL_SLOTS].bitcast(F32),
                                    ALU.subtract).then_inc(s_lo, 1)

            def gemm(ph, read_out, per=0, waits=True):
                with Loop(dve, ph.trips, chain, per) as i:
                    for n, ch in enumerate(ph.body):
                        for j in range(ch.blocks):
                            split(ch.b + 2 + j, i, ph.nb)
                        if read_out is not None:
                            if waits:
                                dve.wait_ge(s_blk, ch.b + ch.blocks + i * ph.nb)
                            read_out(n, i, gp[ch.c % 2], s_free[ch.c % 2])

            def norm_rows(name, weights=None):
                k = NS[name]
                dve.wait_ge(S["s_ss"], k + 1)
                V.tensor_scalar(st[:, 2:4], st[:, 0:2], 1.0 / D, EPS, ALU.mult, ALU.add).then_inc(S["s_ms"], 1)
                dve.wait_ge(S["s_rt"], k + 1)
                chain(V.reciprocal(st[:, 6:8], st[:, 4:6]))
                for tt in range(TT):
                    if weights is None:
                        a = V.tensor_scalar(xs[:, tt, :], h[:, tt, :], st[:, 6 + tt:7 + tt], None, ALU.mult)
                    else:
                        a = V.scalar_tensor_tensor(h[:, tt, :], h[:, tt, :], st[:, 6 + tt:7 + tt], weights, ALU.mult, ALU.mult)
                a.then_inc(S["s_xs"] if weights is None else S["s_norm"], 1)

            def turn_lo(base, groups, hi, lo, kt0, w=None):
                for g in range(groups):
                    dve.wait_ge(S["s_trh"], base + g + 1)
                    if w is None:
                        sl = slice(kt0 + 2 * g, kt0 + 2 * g + 2)
                        a = V.tensor_tensor(lo[:, sl, :], bank[g % 4][:, :].rearrange("p (k n) -> p k n", k=2),
                                            hi[:, sl, :].bitcast(F32), ALU.subtract)
                    else:
                        for m in range(2):
                            kt = 2 * g + m
                            a = V.scalar_tensor_tensor(lo[:, kt0 + kt, :], bank[g % 4][:, m * SEQ:(m + 1) * SEQ], normw[:, w, kt:kt + 1],
                                                       hi[:, kt0 + kt, :].bitcast(F32), ALU.mult, ALU.subtract)
                    a.then_inc(S["s_trl"], 1)

            def attention(base, scores, probs, table, sink):
                for hh in range(HEADS + 2):
                    b = hh % 2
                    if hh < HEADS:
                        dve.wait_ge(S["s_qk"], base + hh + 1)
                        if hh >= 2:
                            dve.wait_ge(S["s_ex"], base + hh - 1)
                        V.scalar_tensor_tensor(scores[:, b].rearrange("p t n -> p (t n)"), bank[b][:, :], SCALE,
                                               table[:, :, :].rearrange("p t n -> p (t n)"), ALU.mult, ALU.add).then_inc(S["s_sc"], 1)
                        dve.wait_ge(S["s_sc"], base + hh + 1)
                        chain(V.tensor_reduce(amx[:, b, :], scores[:, b], AXX, ALU.max))
                        if sink:
                            chain(V.tensor_scalar(amx[:, b, :], amx[:, b, :], sink_bc[:, hh:hh + 1], None, ALU.max))
                        V.tensor_scalar(anm[:, b, :], amx[:, b, :], -1.0, None, ALU.mult).then_inc(S["s_mx"], 1)
                    if 1 <= hh <= HEADS:
                        k = (hh - 1) % 2
                        dve.wait_ge(S["s_ex"], base + hh)
                        if sink:
                            chain(V.tensor_tensor(asm[:, k, :], asm[:, k, :], aes[:, k, :], ALU.add))
                        chain(V.reciprocal(asm[:, k, :], asm[:, k, :]))
                        for tt in range(TT):
                            a = V.tensor_scalar(probs[:, k, tt, :], probs[:, k, tt, :], asm[:, k, tt:tt + 1], None, ALU.mult)
                        a.then_inc(S["s_p"], 1)
                    if hh >= 2:
                        k = hh - 2
                        dve.wait_ge(S["s_ah"], base + k + 1)
                        V.tensor_tensor(a2l[:, k, :], gp[0][:, (k % 2) * 512:(k % 2) * 512 + SEQ], a2h[:, k, :].bitcast(F32),
                                        ALU.subtract).then_inc(S["s_al"], 1)

            chain(V.memset(eps[:, :], EPS))
            V.memset(ones[:, :], 1.0)
            V.memset(cvin[:, :, :, 0:2], 0.0)
            V.memset(cvin[:, :, :, 2 + SEQ:4 + SEQ], 0.0).then_inc(S["s_set"], 1)
            norm_rows("mix")
            dve.wait_ge(S["s_const"], 16 * NCONST)
            turn_lo(TG["mix"], 8, a1h, a1l, 0, 0)
            split(0, 0, 0)
            split(1, 0, 0)

            def to_dn(n, i, g, free):
                ch = PH["dn"].body[n]
                wait_read_out(dve, PH["dn"], i, n)
                for tap in range(5):
                    for m in range(4):
                        wcol = cw1[:, tap, bass.ds(8 * i + 4 * n + m, 1)]
                        src = cvin[:, n, m, tap:tap + SEQ]
                        if tap == 0:
                            a = V.tensor_scalar(cvout[:, m, :], src, wcol, None, ALU.mult)
                        else:
                            a = V.scalar_tensor_tensor(cvout[:, m, :], src, wcol, cvout[:, m, :], ALU.mult, ALU.add)
                    if tap < 4:
                        chain(a)
                a.then_inc(S["s_cv"], 1)

            for name in ("ba", "lead", "v", "qk"):
                gemm(PH[name], None)
            gemm(PH["dn"], to_dn, 8, waits=False)
            gemm(PH["z"], None)
            gemm(PH["gates0"], None)
            gemm(PH["gates"], None)
            dve.wait_ge(S["s_wm"], 16)
            attention(0, asc, apr, wmask, False)

            bt, gg, gc, glc, bte, ekg = (sc32[n] for n in ("bt", "gg", "gc", "gl_c", "bte", "ekg"))
            ta, tb, tc = (tmp64[n] for n in ("ta", "tb", "tc"))
            hdt = dict(h=HEADS, d=2, t=TT)
            ta4, tc4 = (x[:, 0:32].rearrange("p (h d t) -> p h d t", **hdt) for x in (ta, tc))
            alpha = ba[:, :, 16:32].rearrange("p t (d h) -> p h d t", d=2)

            def per_head_dir(row):
                return row.rearrange("p (d h) -> p h d", d=2).unsqueeze(3).to_broadcast([P, HEADS, 2, TT])

            chain(V.tensor_tensor(ta4, alpha, per_head_dir(dtal[:, 0, :]), ALU.add))
            V.scalar_tensor_tensor(tb[:, 0:32], ta[:, 0:32], -1.0, ta[:, 0:32], ALU.mult, ALU.min).then_inc(S["s_gate"], 1)
            dve.wait_ge(S["s_bag"], 2)
            chain(V.scalar_tensor_tensor(tc[:, 0:32], ta[:, 0:32], 0.0, tc[:, 0:32], ALU.max, ALU.add))
            chain(V.tensor_scalar(tc[:, 0:32], tc[:, 0:32], -1.0, None, ALU.mult))
            chain(V.tensor_tensor(gg[:, :, :, :], tc4, per_head_dir(dtal[:, 1, :]), ALU.mult))
            for a in range(2):
                i_ = V.tensor_scalar(ghalf[:, a], gg[:, :, :, :], half[:, a:a + 1], None, ALU.mult)
            i_.then_inc(S["s_gate"], 1)
            dve.wait_ge(S["s_gcm"], 1)
            chain(V.tensor_copy(gc[:, :, :, :], bank[0][:, 0:32].rearrange("p (d h t) -> p h d t", d=2, h=HEADS)))
            V.tensor_tensor(glc[:, :, :, :], bank[1][:, 0:32].rearrange("p (h d t) -> p h d t", **hdt), gc[:, :, :, :],
                            ALU.subtract).then_inc(S["s_gcols"], 1)
            dve.wait_ge(S["s_bag"], 3)
            chain(V.tensor_tensor(bte[:, :, :, :], bte[:, :, :, :], bt[:, :, :, :], ALU.mult))
            for j in range(8):
                dve.wait_ge(S["s_lrt"], j + 1)
                chain(V.reciprocal(rtb[:, j % 2, :], rtb[:, j % 2, :]))
                x = dnT[:, 2 * j:2 * j + 2, :].rearrange("p k n -> p (k n)")
                V.scalar_tensor_tensor(x, x, SCALE if j < 4 else 1.0, rtb[:, j % 2, :], ALU.mult, ALU.mult).then_inc(S["s_lfree"], 1)
            dve.wait_ge(S["s_lfree"], 8)

            def over_dirs(x):
                return x.unsqueeze(1).to_broadcast([P, 2] + list(x.shape[1:]))

            def bank4(b, lo=0, hi=4):
                return b[:, lo * P:hi * P]

            for hh in range(HEADS):
                g, gr = hh % G, hh // G
                dve.wait_ge(S["s_r1"], hh + 1)
                for d in range(2):
                    for tt in range(TT):
                        q = d * 2 + tt
                        a = V.scalar_tensor_tensor(dec[:, d, tt, :], bank[0][:, q * P:(q + 1) * P], gc[:, hh, d, tt:tt + 1], neg[:, d, :],
                                                   ALU.subtract, ALU.add)
                a.then_inc(S["s_dm"], 1)
                V.tensor_tensor(kbT[:, :, :], bank[1][:, :].rearrange("p (d n) -> p d n", d=2), over_dirs(dnT[:, 8 + hh, :]),
                                ALU.mult).then_inc(S["s_kb"], 1)
                dve.wait_ge(S["s_r1a"], 2 * hh + 1)
                V.tensor_tensor(qgT[:, g], egr[:, :, :, :].rearrange("p d t n -> p d (t n)"), over_dirs(dnT[:, hh, :]), ALU.mult).then_inc(S["s_qg"], 1)
                dve.wait_ge(S["s_r1a"], 2 * hh + 2)
                dve.wait_ge(S["s_gram"], hh + 1)
                V.tensor_tensor(AT[:, :, :, :], bank[2][:, :].rearrange("p (d t n) -> p d t n", d=2, t=TT), dec[:, :, :, :], ALU.mult).then_inc(S["s_AT"], 1)
                V.tensor_tensor(qkT[:, g], over_dirs(bank[3][:, 0:256].rearrange("p (t n) -> p t n", t=TT)), dec[:, :, :, :], ALU.mult).then_inc(S["s_qks"], 1)
                dve.wait_ge(S["s_AT"], hh + 1)
                chain(V.tensor_tensor(PB[:, :, :].rearrange("p (d t) n -> p d t n", d=2), AT[:, :, :, :],
                                      level[:, :, 0, :].unsqueeze(2).to_broadcast([P, 2, TT, P]), ALU.mult))
                V.tensor_tensor(TB[:, 1, :, :], ident[:, :].unsqueeze(1).to_broadcast([P, 4, P]), PB[:, :, :], ALU.subtract).then_inc(S["s_t1d"], 1)
                dve.wait_ge(S["s_tok"], hh + 1)
                ktok = over_dirs(bank[1][:, 0:256].rearrange("p (t n) -> p t n", t=TT))
                vtok = over_dirs(bank[1][:, 256:512].rearrange("p (t n) -> p t n", t=TT))

                def rows(x):
                    return x[:, hh].unsqueeze(3).to_broadcast([P, 2, TT, P])
                V.tensor_tensor(kbg[:, :, :, :], ktok, rows(bte), ALU.mult)
                V.tensor_tensor(kgt[:, g], ktok, rows(ekg), ALU.mult)
                V.tensor_tensor(vb[:, :, :, :], vtok, rows(bt), ALU.mult).then_inc(S["s_tokd"], 1)
                for n in range(1, LEVELS):
                    dve.wait_ge(S["s_X"], 5 * hh + n)
                    if n == 1:
                        dve.wait_ge(S["s_t1"], hh + 1)
                    if n < LEVELS - 1:
                        V.tensor_tensor(TB[:, :, :, :].rearrange("p a q n -> p (a q n)"), TB[:, :, :, :].rearrange("p a q n -> p (a q n)"), gp[0][:, :],
                                        ALU.subtract).then_inc(S["s_TB"], 1)
                    else:
                        V.tensor_tensor(TB[:, 1, :, :].rearrange("p q n -> p (q n)"), TB[:, 1, :, :].rearrange("p q n -> p (q n)"), gp[0][:, 512:1024],
                                        ALU.subtract).then_inc(S["s_TB"], 1)
                    dve.wait_ge(S["s_TB"], 5 * hh + n)
                if g < G - 1:
                    continue
                for s in range(NCH):
                    step = NCH * gr + s
                    where = []
                    for d in range(2):
                        c = s if d == 0 else NCH - 1 - s
                        where.append((CHUNK * (c % 2), c // 2))
                    if s:
                        dve.wait_ge(S["s_ws"], 3 * gr + s)
                    else:
                        dve.wait_ge(S["s_uwc"], hh + 1)
                    if step:
                        dve.wait_ge(S["s_os"], step)
                    for d, (lo, tl) in enumerate(where):
                        u = uu[lo:lo + CHUNK, :, d, tl, :]
                        o = vn[lo:lo + CHUNK, :, :]
                        if s:
                            a = V.tensor_tensor(o, u, bank[0][lo:lo + CHUNK, :].rearrange("p (g n) -> p g n", g=G), ALU.subtract)
                        else:
                            a = V.tensor_copy(o, u)
                    a.then_inc(S["s_vn"], 1)
                    if s < NCH - 1:
                        dve.wait_ge(S["s_su"], 3 * gr + s + 1)
                        dve.wait_ge(S["s_os"], step + 1)
                        if s == 0:
                            a = V.tensor_copy(SS[:, :, :, :].rearrange("p d g n -> p (d g n)"), gp[0][:, :])
                        else:
                            for d, (lo, tl) in enumerate(where):
                                for k in range(G):
                                    o = (d * G + k) * P
                                    a = V.scalar_tensor_tensor(SS[:, d, k, :], SS[:, d, k, :],
                                                               glast[:, lo // CHUNK, G * gr + k, d, tl:tl + 1], gp[0][:, o:o + P],
                                                               ALU.mult, ALU.add)
                        a.then_inc(S["s_S"], 1)
                        dve.wait_ge(S["s_S"], 3 * gr + s + 1)
                    if s >= 2:
                        dve.wait_ge(S["s_os"], step + 1)
                        dve.wait_ge(S["s_oc"], 2 * gr + 2)
                        for d, (lo, tl) in enumerate(where):
                            x = oacc[lo:lo + CHUNK, tl, G * gr:G * gr + G, :].rearrange("p g n -> p (g n)")
                            a = V.tensor_tensor(x, x, bank[1][lo:lo + CHUNK, :], ALU.add)
                        a.then_inc(S["s_od"], 1)
            dve.wait_ge(S["s_or"], 1)
            chain(V.tensor_reduce(st8[:, 0:16], osq[:, :, :, :].rearrange("p t h n -> p (t h) n"), AXX, ALU.add))
            V.tensor_scalar(st8[:, 0:16], st8[:, 0:16], 1.0 / HD, EPS, ALU.mult, ALU.add).then_inc(S["s_ord"], 1)
            dve.wait_ge(S["s_or"], 2)
            chain(V.reciprocal(st8[:, 16:32], st8[:, 16:32]))
            o16 = oacc[:, :, :, :].rearrange("p t h n -> p (t h) n")
            chain(V.tensor_tensor(o16, o16, st8[:, 16:32].unsqueeze(2).to_broadcast([P, 16, HD]), ALU.mult))
            chain(V.tensor_tensor(o16, o16, onorm[:, :].unsqueeze(1).to_broadcast([P, 16, HD]), ALU.mult))
            oflat = oacc[:, :, :, :].rearrange("p t h n -> p (t h n)")
            V.tensor_tensor(oflat, oflat, zs[:, :, :].rearrange("p t n -> p (t n)"), ALU.mult).then_inc(S["s_ord"], 1)
            turn_lo(TG["yb"], 4, a2h, a2l, 8)

            def to_mix(n, i, g, free):
                dve.wait_ge(s_gld[n], 16 * i + 16)
                V.tensor_tensor((mixa, mixb)[n][:, :], g[:, :], gld[:, n, :], ALU.mult).then_inc(free, 1)
                if n == 1:
                    wait_read_out(dve, PH["mix"], i, 0)
                    wait_read_out(dve, PH["mix"], i, 1)
                    V.tensor_tensor(mixb[:, :], mixb[:, :], mixa[:, :], ALU.add).then_inc(S["s_mixa"], 1)
                    dve.wait_ge(S["s_mixh"], i + 1)
                    sl = bass.ds(4 * i, 4)
                    V.tensor_tensor(a1l[:, sl, :], mixb[:, :].rearrange("p (m n) -> p m n", m=4), a1h[:, sl, :].bitcast(F32),
                                    ALU.subtract).then_inc(S["s_mixl"], 1)

            def to_residual(ph):
                def f(n, i, g, free):
                    x = h[:, :, bass.ds(ph.step * i + 512 * n, 512)] if ph.trips > 1 else h[:, :, 512 * n:512 * (n + 1)]
                    V.tensor_tensor(x, g[:, :].rearrange("p (t n) -> p t n", t=TT), x, ALU.add).then_inc(free, 1)
                return f
            gemm(PH["mix"], to_mix)
            dve.wait_ge(S["s_hx"], 16)
            gemm(PH["out"], to_residual(PH["out"]))
            norm_rows("mlp")
            turn_lo(TG["mlp"], 8, a1h, a1l, 0, 1)

            def to_hidden(count0):
                def f(n, i, g, free):
                    dve.wait_ge(S["s_ffh"], count0 + 2 * i + n + 1)
                    sl = bass.ds(8 * i + 4 * n, 4)
                    V.tensor_tensor(a2l[:, sl, :], ffq[:, :].rearrange("p (m n) -> p m n", m=4), a2h[:, sl, :].bitcast(F32),
                                    ALU.subtract).then_inc(S["s_ffl"], 1)
                return f
            for k in range(2):
                gemm(PH[f"up{k}"], to_hidden(8 * k), waits=False)
                gemm(PH[f"down{k}"], to_residual(PH[f"down{k}"]))
            dve.wait_ge(S["s_wrow"], 16)
            norm_rows("final", wrow[:, :])
            norm_rows("norm1")
            turn_lo(TG["norm1"], 8, a1h, a1l, 0, 2)

            for name in ("lr", "kv", "qa", "qkg", "vg", "gg"):
                gemm(PH[name], None)
            dve.wait_ge(S["s_qr"], 1)
            chain(V.tensor_reduce(st8[:, 0:16], rtmp[:, :, :].rearrange("p t (h n) -> p (t h) n", h=HEADS), AXX, ALU.add))
            chain(V.tensor_reduce(st8[:, 16:20].rearrange("p (t h) -> p t h", t=TT), rtmp2[:, :, 0:256].rearrange("p t (h n) -> p t h n", h=2), AXX, ALU.add))
            V.tensor_scalar(st8[:, 0:20], st8[:, 0:20], 1.0 / HD, EPS, ALU.mult, ALU.add).then_inc(S["s_qn"], 1)
            dve.wait_ge(S["s_qr"], 2)
            chain(V.reciprocal(st8[:, 32:52], st8[:, 32:52]))
            dve.wait_ge(S["s_const2"], 16 * NCONST2)
            for x, nh, c0, w in ((qa[:, :, :], HEADS, 32, 0), (kva[:, :, 0:256], 2, 48, 1)):
                x4 = x.rearrange("p t (h n) -> p t h n", h=nh)
                chain(V.tensor_tensor(x4, x4, st8[:, c0:c0 + 2 * nh].rearrange("p (t h) -> p t h", t=TT).unsqueeze(3).to_broadcast([P, TT, nh, HD]), ALU.mult))
                chain(V.tensor_tensor(x4, x4, gq_bc[:, w, :].unsqueeze(1).unsqueeze(1).to_broadcast([P, TT, nh, HD]), ALU.mult))
                x5 = x.rearrange("p t (h c n) -> p t h c n", h=nh, c=2)
                f1, f2 = (r[:, :, 0:nh * HD].rearrange("p t (h c n) -> p t h c n", h=nh, c=2) for r in (rtmp, rtmp2))
                cos, sin = (rope_cs[:, k].unsqueeze(2).to_broadcast([P, TT, nh, HD // 2]) for k in range(2))
                V.tensor_tensor(f1[:, :, :, 0], x5[:, :, :, 0], cos, ALU.mult)
                V.tensor_tensor(f2[:, :, :, 0], x5[:, :, :, 1], sin, ALU.mult)
                V.tensor_tensor(f1[:, :, :, 1], x5[:, :, :, 1], cos, ALU.mult)
                chain(V.tensor_tensor(f2[:, :, :, 1], x5[:, :, :, 0], sin, ALU.mult))
                V.tensor_tensor(x5[:, :, :, 0], f1[:, :, :, 0], f2[:, :, :, 0], ALU.subtract)
                chain(V.tensor_tensor(x5[:, :, :, 1], f1[:, :, :, 1], f2[:, :, :, 1], ALU.add))
            V.memset(st8[:, 63:64], 0.0).then_inc(S["s_roped"], 1)
            dve.wait_ge(S["s_bm"], 16)
            attention(HEADS, asc2, apr2, bmask, True)

            dve.wait_ge(S["s_al"], 2 * HEADS)
            for z in (aTm[:, :, :, :].rearrange("p h t n -> p (h t n)"),):
                chain(V.memset(z, 0.0))
            dve.wait_ge(S["s_gta"], 1)
            gflat = gtok[:, :, :, :].rearrange("p d t n -> p (d t n)")
            V.scalar_tensor_tensor(eb4[:, :], gflat, -1.0, gflat, ALU.mult, ALU.min).then_inc(S["s_gtd"], 1)
            dve.wait_ge(S["s_gta"], 2)
            V.scalar_tensor_tensor(gflat, gflat, 0.0, eb4[:, :], ALU.min, ALU.subtract).then_inc(S["s_gtd"], 1)
            qf, kf = (qkg[:, 4 * k:4 * k + 4, :].rearrange("p h n -> p (h n)") for k in range(2))

            def flat(x):
                return x[:, :, :].rearrange("p h n -> p (h n)")
            for d in range(2):
                ref = CHUNK // 2 if d == 0 else CHUNK - 1 - CHUNK // 2
                last = CHUNK - 1 if d == 0 else 0
                ebc = eb[:, :, :].rearrange("p h (c n) -> p (h c) n", n=CHUNK)
                dve.wait_ge(S["s_eb"], d + 1)
                if d:
                    dve.wait_ge(S["s_kop"], 1)
                for k, (x, at_) in enumerate(((eD, ref), (eE, last))):
                    V.tensor_tensor(x[:, :, :].rearrange("p h (c n) -> p (h c) n", n=CHUNK), ebc, ebc[:, :, at_:at_ + 1].to_broadcast([P, 16, CHUNK]),
                                    ALU.subtract).then_inc(S["s_bD"], 1)
                dve.wait_ge(S["s_ea"], 3 * d + 1)
                V.scalar_tensor_tensor(flat(qin), flat(qin), SCALE, qf, ALU.mult, ALU.mult).then_inc(S["s_bE"], 1)
                dve.wait_ge(S["s_ea"], 3 * d + 2)
                V.scalar_tensor_tensor(flat(qga), flat(qga), SCALE, qf, ALU.mult, ALU.mult)
                V.tensor_tensor(flat(kga), flat(kga), kf, ALU.mult).then_inc(S["s_bE"], 1)
                dve.wait_ge(S["s_ea"], 3 * d + 3)
                V.tensor_tensor(flat(kou), flat(kou), kf, ALU.mult).then_inc(S["s_bE"], 1)
                dve.wait_ge(S["s_aTp"], d + 1)
                if d:
                    dve.wait_ge(S["s_oin"], 1)
                    chain(V.memset(aTm[:, :, :, :].rearrange("p h t n -> p (h t n)"), 0.0))
                V.copy_predicated(aTm[:, :, :, :].rearrange("p h t n -> p (h t) n"),
                                  causal[:, d, :].bitcast(U32).unsqueeze(1).to_broadcast([P, 8, P]),
                                  gp[1][:, :].rearrange("p (q n) -> p q n", q=8)).then_inc(S["s_aTm"], 1)
                for s in range(NCH - 1):
                    c = s if d == 0 else NCH - 1 - s
                    dve.wait_ge(S["s_kv2"], 3 * d + s + 1)
                    if 3 * d + s >= 2:
                        dve.wait_ge(S["s_oi"], 3 * d + s - 1)
                    src = gp[s % 2]
                    new = S2[:, s % 2]
                    if s == 0:
                        a = V.tensor_copy(new.rearrange("p h n -> p (h n)"), src[:, :])
                    else:
                        for k in range(4):
                            a = V.scalar_tensor_tensor(new[:, k, :], S2[:, (s + 1) % 2, k, :], st8[:, 4 * k + c:4 * k + c + 1],
                                                       src[:, k * 256:(k + 1) * 256], ALU.mult, ALU.add)
                    a.then_inc(S["s_S2"], 1)
                    dve.wait_ge(S["s_S2"], 3 * d + s + 1)
            dve.wait_ge(S["s_or2"], 1)
            chain(V.tensor_reduce(st8[:, 0:8], oq2[:, :, :, :].rearrange("p t h n -> p (t h) n"), AXX, ALU.add))
            V.tensor_scalar(st8[:, 0:8], st8[:, 0:8], 1.0 / GLA_DV, EPS, ALU.mult, ALU.add).then_inc(S["s_or2d"], 1)
            dve.wait_ge(S["s_or2"], 2)
            chain(V.reciprocal(st8[:, 16:24], st8[:, 16:24]))
            o8 = oo2[:, :, :, :].rearrange("p t h n -> p (t h) n")
            chain(V.tensor_tensor(o8, o8, st8[:, 16:24].unsqueeze(2).to_broadcast([P, 8, GLA_DV]), ALU.mult))
            chain(V.tensor_tensor(o8, o8, gout_bc[:, :].unsqueeze(1).to_broadcast([P, 8, GLA_DV]), ALU.mult))
            o2f = oo2[:, :, :, :].rearrange("p t h n -> p (t h n)")
            V.tensor_tensor(o2f, o2f, gg2[:, :, :].rearrange("p t n -> p (t n)"), ALU.mult).then_inc(S["s_or2d"], 1)
            turn_lo(TG["cat"], 4, a2h, a2l, 8)
            gemm(PH["out2"], to_residual(PH["out2"]))
            norm_rows("norm2")
            turn_lo(TG["norm2"], 8, a1h, a1l, 0, 3)

            def to_ff(ph, count0, tile0):
                def f(n, i, g, free):
                    wait_read_out(dve, ph, i, n)
                    base = tile0 + 44 * n
                    for tap in (1, 0, 2):
                        for m in range(4):
                            col = bass.ds(4 * i + base + m, 1)
                            src = upad[:, n, m, tap:tap + SEQ]
                            o = cg[:, n, m * SEQ:(m + 1) * SEQ]
                            if tap == 1:
                                a = V.tensor_scalar(o, src, cw2[:, tap, col], cb2[:, col], ALU.mult, ALU.add)
                            else:
                                a = V.scalar_tensor_tensor(o, src, cw2[:, tap, col], o, ALU.mult, ALU.add)
                        if not (tap == 2 and n == 0):
                            chain(a)
                    if n == 0:
                        a.then_inc(S["s_cv2"], 1)
                        return
                    dve.wait_ge(S["s_sil"], count0 + i + 1)
                    V.tensor_tensor(cg[:, 1, :], cg[:, 1, :], cg[:, 0, :], ALU.mult).then_inc(S["s_prod"], 1)
                    dve.wait_ge(S["s_ffh"], 16 + count0 + i + 1)
                    sl = bass.ds(4 * i, 4)
                    V.tensor_tensor(a2l[:, sl, :], cg[:, 1, :].rearrange("p (m n) -> p m n", m=4), a2h[:, sl, :].bitcast(F32),
                                    ALU.subtract).then_inc(S["s_ffl"], 1)
                return f
            V.memset(upad[:, :, :, 0:1], 0.0)
            chain(V.memset(upad[:, :, :, 1 + SEQ:2 + SEQ], 0.0))
            gemm(PH["ff0"], to_ff(PH["ff0"], 0, 0), 5, waits=False)
            gemm(PH["dd0"], to_residual(PH["dd0"]))
            gemm(PH["ff1"], to_ff(PH["ff1"], 6, 24), 5, waits=False)
            gemm(PH["dd1"], to_residual(PH["dd1"]))

        @block.tensor
        def _(pe):
            def gemm(ph, ready=()):
                for s, v in ready:
                    pe.wait_ge(s, v)
                ah, al = acts[ph.act]
                with Loop(pe, ph.trips) as i:
                    for ch in ph.body:
                        g = gp[ch.c % 2]
                        if ch.c >= 2:
                            pe.wait_ge(s_free[ch.c % 2], ch.c // 2 + i * (ph.nc // 2))
                        kts = BLK_KT if ch.n == BLK_N else KT
                        for j in range(ch.blocks):
                            idx = ch.b + j
                            sl = idx % HL_SLOTS
                            pe.wait_ge(s_hi, idx + 1 + i * ph.nb)
                            pe.wait_ge(s_lo, idx + 1 + i * ph.nb)
                            for k in range(kts):
                                kt = ch.kt0 + j * BLK_KT + k
                                first, last = j == 0 and k == 0, j == ch.blocks - 1 and k == kts - 1
                                if ch.n == BLK_N:
                                    hi, lo = wh[:, sl, k, :], wl[:, sl, k, :]
                                else:
                                    hi, lo = (w[:, sl, 0, k * ch.n:(k + 1) * ch.n] for w in (wh, wl))
                                if ch.kind == "up":
                                    for m in range((ch.n + P - 1) // P):
                                        cols = slice(m * P, min((m + 1) * P, ch.n))
                                        rows = min(P, ch.n)
                                        for q, (a, b) in enumerate(((hi, ah), (hi, al), (lo, ah))):
                                            mm = pe.matmul(g[0:rows, m * SEQ:(m + 1) * SEQ], a[:, cols], b[:, kt, :],
                                                           start=first and q == 0 and m % 2 == 0, stop=last and q == 2,
                                                           skip_group_check=True)
                                else:
                                    for tt in range(TT):
                                        rows = slice(tt * P, (tt + 1) * P)
                                        for q, (a, b) in enumerate(((ah, hi), (ah, lo), (al, hi))):
                                            mm = pe.matmul(g[:, tt * 512:tt * 512 + ch.n], a[:, kt, rows], b,
                                                           start=first and q == 0, stop=last and q == 2,
                                                           skip_group_check=True)
                            mm.then_inc(s_blk, 1)

            def turn(base, groups, src, after):
                pe.wait_ge(*after)
                for g in range(groups):
                    if g >= 4:
                        pe.wait_ge(S["s_trl"], base + g - 3)
                    for m in range(2):
                        for tt in range(TT):
                            mm = pe.transpose(bank[g % 4][:, m * SEQ + tt * P:m * SEQ + (tt + 1) * P], src(2 * g + m, tt), ident[:, :])
                    mm.then_inc(S["s_tr"], 1)

            def products_out(ph):
                wait_read_out(pe, ph, ph.trips - 1, ph.nc - 2)
                wait_read_out(pe, ph, ph.trips - 1, ph.nc - 1)

            def attention(base, q, k, v, position=None):
                def scores(hh):
                    if hh >= 2:
                        pe.wait_ge(S["s_sc"], base + hh - 1)
                    for tt in range(TT):
                        o = bank[hh % 2][:, tt * SEQ:(tt + 1) * SEQ]
                        mm = pe.matmul(o, q(hh)[:, tt * P:(tt + 1) * P], k(hh), start=True, stop=position is None)
                        if position is not None:
                            mm = pe.matmul(o, flip[:, :], position[:, hh, tt, :], start=False, stop=True)
                    mm.then_inc(S["s_qk"], 1)
                scores(0)
                for hh in range(HEADS):
                    if hh + 1 < HEADS:
                        scores(hh + 1)
                    pe.wait_ge(S["s_p"], base + hh + 1)
                    if hh >= 2:
                        pe.wait_ge(S["s_pT"], base + hh - 1)
                    for kt in range(TT):
                        for tt in range(TT):
                            mm = pe.transpose(bank[2 + hh % 2][:, kt * SEQ + tt * P:kt * SEQ + (tt + 1) * P],
                                              probs_[base][:, hh % 2, tt, kt * P:(kt + 1) * P], ident[:, :])
                    mm.then_inc(S["s_pt"], 1)
                    pe.wait_ge(S["s_pT"], base + hh + 1)
                    if hh >= 2:
                        pe.wait_ge(S["s_al"], base + hh - 1)
                    for kt in range(TT):
                        mm = pe.matmul(gp[0][:, (hh % 2) * 512:(hh % 2) * 512 + SEQ], v(hh, kt), probsT_[base][:, hh % 2, kt, :],
                                       start=kt == 0, stop=kt == TT - 1)
                    mm.then_inc(S["s_o"], 1)
            probs_ = {0: apr, HEADS: apr2}
            probsT_ = {0: apT, HEADS: apT2}

            pe.wait_ge(S["s_const"], 16 * NCONST)
            pe.wait_ge(S["s_set"], 1)
            turn(TG["mix"], 8, lambda kt, tt: xs[:, tt, kt * P:(kt + 1) * P], (S["s_xs"], 1))
            gemm(PH["ba"], [(S["s_trl"], TG["mix"] + 8)])
            for name in ("lead", "v", "qk", "dn", "z", "gates0", "gates"):
                gemm(PH[name])
            products_out(PH["gates"])
            pe.wait_ge(S["s_bias"], 16 * (4 * HEADS + 1))
            attention(0, lambda hh: attqk[:, hh, :], lambda hh: attqk[:, 8 + hh, :], lambda hh, kt: attv[:, kt, hh * P:(hh + 1) * P], bias)

            bt, gg = sc32["bt"], sc32["gg"]
            pe.wait_ge(S["s_gate"], 2)
            pe.wait_ge(S["s_bag"], 2)
            pe.wait_ge(S["s_sc"], HEADS)
            for d in range(2):
                pe.matmul(bank[0][:, d * 16:(d + 1) * 16], tri[:, d, :], gg[:, :, d, :], start=True, stop=True)
            pe.matmul(bank[1][:, 0:32], blockm[:, :], gg[:, :, :, :].rearrange("p h d t -> p (h d t)"), start=True, stop=True)
            pe.matmul(bank[1][:, 64:128], ones[:, :], ghalf[:, :, :, :, :].rearrange("p a h d t -> p (a h d t)"), start=True, stop=True).then_inc(S["s_gcm"], 1)
            pe.wait_ge(S["s_pT"], HEADS)
            for j in range(8):
                pe.wait_ge(S["s_lsq"], j + 1)
                if j >= 2:
                    pe.wait_ge(S["s_lrt"], j - 1)
                pe.matmul(bank[2 + j % 2][:, :], ones[:, :], sqb[:, j % 2, :], start=True, stop=True).then_inc(S["s_lsum"], 1)
            pe.wait_ge(S["s_bag"], 3)
            pe.wait_ge(S["s_gcols"], 1)
            pe.wait_ge(S["s_lfree"], 8)
            pe.wait_ge(S["s_al"], HEADS)
            for hh in range(HEADS):
                g, gr = hh % G, hh // G
                qT, kT, vT = dnT[:, hh, :], dnT[:, 8 + hh, :], dnT[:, 16 + hh, :]
                if hh:
                    pe.wait_ge(S["s_Pc"], 5 * hh)
                    pe.wait_ge(S["s_tokd"], hh)
                if g == 0 and gr:
                    pe.wait_ge(S["s_od"], 2 * gr)
                for d in range(2):
                    for tt in range(TT):
                        q = d * 2 + tt
                        pe.matmul(bank[0][:, q * P:(q + 1) * P], gg[:, hh, d, tt:tt + 1].to_broadcast([P, P]), tri[:, d, :], start=True, stop=True)
                        mm = pe.matmul(bank[1][:, q * P:(q + 1) * P], bt[:, hh, d, tt:tt + 1].to_broadcast([P, P]), ident[:, :], start=True, stop=True)
                mm.then_inc(S["s_r1"], 1)
                pe.wait_ge(S["s_kb"], hh + 1)
                if hh:
                    pe.wait_ge(S["s_qks"], hh)
                for tt in range(TT):
                    c = slice(tt * P, (tt + 1) * P)
                    for d in range(2):
                        q = d * 2 + tt
                        pe.matmul(bank[2][:, q * P:(q + 1) * P], kT[:, c], kbT[:, d, c], start=True, stop=True)
                    mm = pe.matmul(bank[3][:, c], kT[:, c], qT[:, c], start=True, stop=True)
                mm.then_inc(S["s_gram"], 1)
                for tt in range(TT):
                    c = slice(tt * P, (tt + 1) * P)
                    pe.transpose(bank[1][:, c], kT[:, c], ident[:, :])
                    mm = pe.transpose(bank[1][:, 256 + tt * P:256 + (tt + 1) * P], vT[:, c], ident[:, :])
                mm.then_inc(S["s_tok"], 1)
                pe.wait_ge(S["s_t1d"], hh + 1)
                pe.wait_ge(S["s_r1a"], 2 * hh + 1)
                for q in range(4):
                    mm = pe.transpose(bank[0][:, q * P:(q + 1) * P], TB[:, 1, q, :], ident[:, :])
                mm.then_inc(S["s_t1p"], 1)
                pe.wait_ge(S["s_ATl"], hh + 1)
                for n in range(1, LEVELS):
                    if n == 1:
                        pe.wait_ge(S["s_t1"], hh + 1)
                    else:
                        pe.wait_ge(S["s_TB"], 5 * hh + n - 1)
                    for q in range(4):
                        mm = pe.matmul(bank[0][:, q * P:(q + 1) * P], ATl[:, q // 2, q % 2, n - 1, :], TB[:, 0, q, :], start=True, stop=True)
                    mm.then_inc(S["s_P"], 1)
                    pe.wait_ge(S["s_Pc"], 5 * hh + n)
                    for q in range(4):
                        if n < LEVELS - 1:
                            pe.matmul(gp[0][:, q * P:(q + 1) * P], TB[:, 1, q, :], PB[:, q, :], start=True, stop=True)
                        mm = pe.matmul(gp[0][:, 512 + q * P:512 + (q + 1) * P], PB[:, q, :], TB[:, 1, q, :], start=True, stop=True)
                    mm.then_inc(S["s_X"], 1)
                pe.wait_ge(S["s_TB"], 5 * hh + 5)
                pe.wait_ge(S["s_tokd"], hh + 1)
                if hh:
                    pe.wait_ge(S["s_uwc"], hh)
                for q in range(4):
                    pe.matmul(gp[1][:, q * P:(q + 1) * P], TB[:, 1, q, :], vb[:, q // 2, q % 2, :], start=True, stop=True)
                    mm = pe.matmul(gp[1][:, 512 + q * P:512 + (q + 1) * P], kbg[:, q // 2, q % 2, :], TB[:, 1, q, :], start=True, stop=True)
                mm.then_inc(S["s_uw"], 1)
                if g < G - 1:
                    continue
                pe.wait_ge(S["s_uwc"], hh + 1)
                pe.wait_ge(S["s_qg"], hh + 1)
                for s in range(NCH):
                    step = NCH * gr + s
                    where = []
                    for d in range(2):
                        c = s if d == 0 else NCH - 1 - s
                        where.append((CHUNK * (c % 2), c // 2))
                    if s:
                        pe.wait_ge(S["s_S"], 3 * gr + s)
                        for d, (lo, tl) in enumerate(where):
                            for k in range(G):
                                mm = pe.matmul(bank[0][lo:lo + CHUNK, k * P:(k + 1) * P], wTs[:, k, d, tl, lo:lo + CHUNK], SS[:, d, k, :],
                                               start=True, stop=True)
                        mm.then_inc(S["s_ws"], 1)
                    pe.wait_ge(S["s_vn"], step + 1)
                    if s < NCH - 1:
                        for d, (lo, tl) in enumerate(where):
                            for k in range(G):
                                o = (d * G + k) * P
                                mm = pe.matmul(gp[0][:, o:o + P], kgt[lo:lo + CHUNK, k, d, tl, :], vn[lo:lo + CHUNK, k, :], start=True, stop=True)
                        mm.then_inc(S["s_su"], 1)
                    if s in (1, 2):
                        pe.wait_ge(S["s_oc"], 2 * gr + s)
                    elif s == 3:
                        pe.wait_ge(S["s_od"], 2 * gr + 1)
                    for d, (lo, tl) in enumerate(where):
                        rows = slice(lo, lo + CHUNK)
                        for k in range(G):
                            o = bank[1][rows, k * P:(k + 1) * P]
                            if s:
                                pe.matmul(o, qgT[:, k, d, tl * P + lo:tl * P + lo + CHUNK], SS[:, d, k, :], start=True, stop=False)
                            mm = pe.matmul(o, qkT[rows, k, d, tl, lo:lo + CHUNK], vn[rows, k, :], start=s == 0, stop=True)
                    mm.then_inc(S["s_os"], 1)
            turn(TG["yb"], 4, lambda kt, tt: oacc[:, tt, kt, :], (S["s_ord"], 2))
            gemm(PH["mix"], [(S["s_trl"], TG["yb"] + 4)])
            gemm(PH["out"], [(S["s_mixl"], 4)])
            turn(TG["mlp"], 8, lambda kt, tt: xs[:, tt, kt * P:(kt + 1) * P], (S["s_xs"], 2))
            gemm(PH["up0"], [(S["s_trl"], TG["mlp"] + 8)])
            gemm(PH["down0"], [(S["s_ffl"], 8)])
            gemm(PH["up1"])
            gemm(PH["down1"], [(S["s_ffl"], 16)])
            turn(TG["norm1"], 8, lambda kt, tt: xs[:, tt, kt * P:(kt + 1) * P], (S["s_xs"], 3))
            gemm(PH["lr"], [(S["s_trl"], TG["norm1"] + 8)])
            for name in ("kv", "qa", "qkg", "vg", "gg"):
                gemm(PH[name])
            products_out(PH["gg"])
            pe.wait_ge(S["s_roped"], 1)
            for g in range(5):
                if g == 4:
                    pe.wait_ge(S["s_q2c"], 1)
                for m in range(2):
                    for tt in range(TT):
                        hd = 2 * g + m
                        src = qa[:, tt, hd * P:(hd + 1) * P] if g < 4 else kva[:, tt, m * P:(m + 1) * P]
                        mm = pe.transpose(bank[g % 4][:, m * SEQ + tt * P:m * SEQ + (tt + 1) * P], src, ident[:, :])
                mm.then_inc(S["s_q2T"], 1)
            pe.wait_ge(S["s_q2c"], 5)
            attention(HEADS, lambda hh: qT2[:, hh, :], lambda hh: qT2[:, 8 + hh // 4, :],
                      lambda hh, kt: kva[:, kt, 256 + (hh // 4) * P:256 + (hh // 4 + 1) * P])
            pe.wait_ge(S["s_al"], 2 * HEADS)
            pe.wait_ge(S["s_wa"], 1)
            for q in range(4):
                d, tt = q // 2, q % 2
                pe.matmul(bank[q][:, :], lrT[0:33, tt * P:(tt + 1) * P], wa2[0:33, d, :], start=True, stop=True).then_inc(S["s_gt"], 1)
            pe.wait_ge(S["s_gtd"], 2)
            for d in range(2):
                if d:
                    pe.wait_ge(S["s_S2"], 3)
                for hh in range(4):
                    for tt in range(TT):
                        mm = pe.matmul(gp[0][:, hh * SEQ + tt * P:hh * SEQ + (tt + 1) * P], gtok[:, d, tt, hh * P:(hh + 1) * P], tri[:, d, :],
                                       start=True, stop=True)
                mm.then_inc(S["s_bc"], 1)
                pe.wait_ge(S["s_bE"], 3 * d + 2)
                for hh in range(4):
                    for tt in range(TT):
                        c = slice(tt * P, (tt + 1) * P)
                        mm = pe.matmul(gp[1][:, (hh * 2 + tt) * P:(hh * 2 + tt + 1) * P], kga[:, hh, c], qga[:, hh, c], start=True, stop=True)
                mm.then_inc(S["s_aTp"], 1)
                pe.wait_ge(S["s_bE"], 3 * d + 3)
                pe.wait_ge(S["s_eb"], d + 1)
                for hh in range(4):
                    for tt in range(TT):
                        mm = pe.transpose(gp[0][:, (hh * 2 + tt) * P:(hh * 2 + tt + 1) * P], kou[:, hh, tt * P:(tt + 1) * P], ident[:, :])
                mm.then_inc(S["s_kop"], 1)
                pe.wait_ge(S["s_aTm"], d + 1)
                for tt in range(TT):
                    for hh in range(4):
                        mm = pe.matmul(bank[2 * tt + hh // 2][:, (hh % 2) * 256:(hh % 2 + 1) * 256], aTm[:, hh, tt, :],
                                       vg[:, tt, hh * 256:(hh + 1) * 256], start=d == 0 and hh % 2 == 0, stop=False, skip_group_check=True)
                pe.wait_ge(S["s_koc"], d + 1)
                for s in range(NCH):
                    c = s if d == 0 else NCH - 1 - s
                    lo, tl = CHUNK * (c % 2), c // 2
                    rows = slice(lo, lo + CHUNK)
                    if s < NCH - 1:
                        if s >= 2:
                            pe.wait_ge(S["s_S2"], 3 * d + s - 1)
                        for hh in range(4):
                            mm = pe.matmul(gp[s % 2][:, hh * 256:(hh + 1) * 256], kot[rows, hh, tl, :], vg[rows, tl, hh * 256:(hh + 1) * 256],
                                           start=True, stop=True)
                        mm.then_inc(S["s_kv2"], 1)
                    if s:
                        pe.wait_ge(S["s_S2"], 3 * d + s)
                        for hh in range(4):
                            mm = pe.matmul(bank[2 * tl + hh // 2][rows, (hh % 2) * 256:(hh % 2 + 1) * 256], qin[:, hh, c * CHUNK:(c + 1) * CHUNK],
                                           S2[:, (s - 1) % 2, hh, :], start=False, stop=d == 1 and s == NCH - 1, skip_group_check=True)
                        if s < NCH - 1:
                            mm.then_inc(S["s_oi"], 1)
                        else:
                            mm.then_inc(S["s_oin"], 1)
            turn(TG["cat"], 4, lambda kt, tt: oo2[:, tt, kt // 2, (kt % 2) * P:(kt % 2 + 1) * P], (S["s_or2d"], 2))
            gemm(PH["out2"], [(S["s_trl"], TG["cat"] + 4)])
            turn(TG["norm2"], 8, lambda kt, tt: xs[:, tt, kt * P:(kt + 1) * P], (S["s_xs"], 4))
            gemm(PH["ff0"], [(S["s_trl"], TG["norm2"] + 8)])
            gemm(PH["dd0"], [(S["s_ffl"], 16 + 6)])
            gemm(PH["ff1"])
            gemm(PH["dd1"], [(S["s_ffl"], 16 + 11)])

        @block.gpsimd
        def _(pool):
            G_ = nc.gpsimd

            def load(dst, src, s, slow=False):
                pool.dma_start(dst, src).then_inc(s, 16)

            for dst, name in ((ident[:, :], "ident"), (tri[:, :, :], "tri"), (blockm[:, :], "block"), (neg[:, :, :], "neg"),
                              (half[:, :], "half"), (level[:, :, :, :], "level")):
                load(dst, t[name], S["s_const"])
            with nc.allow_non_contiguous_dma(reason="small per-feature tables"):
                for k, name in enumerate(("norm_mix_w", "norm_mlp_w")):
                    load(normw[:, k, :], t[name].rearrange("(k p) -> p k", p=P), S["s_const"])
                for k, name in enumerate(("norm1_g_2", "norm2_g_2")):
                    load(normw[:, 2 + k, :], t[name][0].rearrange("(k p) -> p k", p=P), S["s_const"])
                for tap in range(5):
                    load(cw1[:, tap, :], t["conv_w"][tap].rearrange("(k p) -> p k", p=P), S["s_const"])
                load(dtal[:, 0, :], t["dt_bias"].rearrange("d h -> (d h)").partition_broadcast(P), S["s_const"])
                load(dtal[:, 1, :], t["a_log"].rearrange("d h -> (d h)").partition_broadcast(P), S["s_const"])
                load(onorm[:, :], t["onorm_w"].partition_broadcast(P), S["s_const"])
            for ph, row in ((PH["gates0"], 0), (PH["gates"], 2)):
                with Loop(pool, ph.trips) as i:
                    for n in range(2):
                        wait_read_out(pool, ph, i, n)
                        dst = gates_dram[bass.ds(2 * i + row + n, 1)] if ph.trips > 1 else gates_dram[row + n:row + n + 1]
                        load(dst.rearrange("o p n -> p (o n)"), gstage[:, n, :], s_gst[n])
            pool.wait_ge(s_blk, last_block(PH["gates"]))
            load(wmask[:, :, :], t["window"].rearrange("p (t k) -> p t k", t=TT), S["s_wm"])
            load(flip[:, :], t["flip"], S["s_bias"])
            for hh in range(HEADS):
                for row in range(SEQ // GRID_W):
                    lo, tl = GRID_W * (row % 2), row // 2
                    first = hh * 15 * 31 + (7 - row) * 31 + 15 - (GRID_W - 1)
                    src = bass.AP(t["rpb"].tensor, first, [[1, GRID_W], [31, SEQ // GRID_W], [1, GRID_W]])
                    load(bias[lo:lo + GRID_W, hh, tl, :].rearrange("p (r c) -> p r c", c=GRID_W), src, S["s_bias"])
            for hh in range(HEADS):
                pool.wait_ge(S["s_AT"], hh + 1)
                if hh:
                    pool.wait_ge(S["s_P"], 5 * hh)
                for d in range(2):
                    a = G_.tensor_tensor(ATl[:, d], AT[:, d].unsqueeze(2).to_broadcast([P, TT, LEVELS - 1, P]),
                                         level[:, d, 1:LEVELS, :].unsqueeze(1).to_broadcast([P, TT, LEVELS - 1, P]), ALU.mult)
                a.then_inc(S["s_ATl"], 1)
            pool.wait_ge(S["s_trl"], TG["yb"] + 4)
            load(h[:, :, :], t["x"][0].rearrange("(t p) n -> p t n", p=P), S["s_hx"])
            ph = PH["mix"]
            for n in range(2):
                load(gld[:, n, :], gates_dram[4 * n], s_gld[n])
            for i in range(1, 4):
                for n in range(2):
                    wait_read_out(pool, ph, i - 1, n)
                    load(gld[:, n, :], gates_dram[4 * n + i], s_gld[n])
            load(causal[:, :, :], t["causal"].rearrange("p (d n) -> p d n", d=2), S["s_const2"])
            for k, name in enumerate(("cos", "sin")):
                load(rope_cs[:, k], t[name].rearrange("p (t n) -> p t n", t=TT), S["s_const2"])
            with nc.allow_non_contiguous_dma(reason="small per-feature tables"):
                for tap in range(3):
                    load(cw2[:, tap, :], t["conv_w_2"][0, tap].rearrange("(k p) -> p k", p=P), S["s_const2"])
                load(cb2[:, :], t["conv_b_2"][0].rearrange("(k p) -> p k", p=P), S["s_const2"])
                load(gq_bc[:, 0, :], t["attn_q_norm_g_2"][0].partition_broadcast(P), S["s_const2"])
                load(gq_bc[:, 1, :], t["attn_k_norm_g_2"][0].partition_broadcast(P), S["s_const2"])
                load(gout_bc[:, :], t["gla_out_norm_g_2"][0].partition_broadcast(P), S["s_const2"])
                load(sink_bc[:, :], t["attn_sink_2"][0].partition_broadcast(P), S["s_const2"])
            pool.wait_ge(s_blk, last_block(PH["down1"]))
            load(wrow[:, :], t["norm_final_w"].partition_broadcast(P), S["s_wrow"])
            wait_read_out(pool, PH["lr"], 0, 0)
            G_.memset(lrT[32:33, :], 1.0)
            G_.memset(wa2[0:32, :, :], 0.0).then_inc(S["s_waz"], 1)
            pool.wait_ge(S["s_waz"], 1)
            for d, s in enumerate(("fwd", "bwd")):
                load(wa2[16 * d:16 * d + 16, d, :], t[f"gla_wa2_{s}_2"][0], S["s_wal"])
                load(wa2[32:33, d, :], t[f"gla_ba_{s}_2"], S["s_wal"])
            pool.wait_ge(S["s_wal"], 64)
            G_.memset(pdum[:, 0:1], 0.0).then_inc(S["s_wa"], 1)
            pool.wait_ge(s_blk, last_block(PH["gg"]))
            load(bmask[:, :, :], t["band"].rearrange("p (t k) -> p t k", t=TT), S["s_bm"])


_INS = ['x', 'norm_mix_w', 'w_in', 'conv_w', 'a_log', 'dt_bias', 'onorm_w', 'rpb', 'w_proj_a', 'w_proj_b', 'w_out',
        'norm_mlp_w', 'w_mlp_up', 'w_mlp_down', 'norm_final_w', 'norm1_g_2', 'w_in_2', 'attn_q_norm_g_2',
        'attn_k_norm_g_2', 'attn_sink_2', 'gla_wa2_fwd_2', 'gla_ba_fwd_2', 'gla_wa2_bwd_2', 'gla_ba_bwd_2',
        'gla_out_norm_g_2', 'w_out_2', 'norm2_g_2', 'w_up_2', 'conv_w_2', 'conv_b_2', 'w_down_2']
_SQUEEZED = ('w_in_2', 'w_out_2', 'w_up_2', 'w_down_2')


def program(nc, shapes):
    t = {}
    for name, (shape, dtype) in shapes.items():
        ap = nc.dram_tensor(f"in_{name}", shape, dtype, kind="ExternalInput").ap()
        t[name] = ap[0] if name in _SQUEEZED else ap
    t["out"] = nc.dram_tensor("out_0", (1, SEQ, D), F32, kind="ExternalOutput").ap()
    return t


def kernel(**inputs):
    import concourse.bacc as _bacc
    from concourse.bass_utils import run_bass_kernel_spmd as _run

    nc = _bacc.Bacc("TRN2", target_bir_lowering=False, num_devices=1)
    arrays = {n: np.ascontiguousarray(inputs[n]) for n in _INS}
    arrays.update(constants())
    t = program(nc, {n: (a.shape, mybir.dt.from_np(a.dtype)) for n, a in arrays.items()})
    build(nc, t)
    r = _run(nc, [{f"in_{n}": a for n, a in arrays.items()}], core_ids=[0])
    return r.results[0]["out_0"]
```

```python
from contextlib import ExitStack

import numpy as np
import concourse.bass as bass
from concourse import mybir

ALU = mybir.AluOpType
ACT = mybir.ActivationFunctionType
F32 = mybir.dt.float32
F32R = mybir.dt.float32r
U32 = mybir.dt.uint32
AXX = mybir.AxisListType.X

P = 128
SEQ = 256
TT = SEQ // P
D = 2048
KT = D // P
DFF = 4 * D
DFF2 = 5632
HEADS = 8
HD = 128
CHUNK = 64
NCH = SEQ // CHUNK
GRID_W, WIN_C = 64, 16
GLA_H, GLA_DV = 4, 256
LEVELS = 6
EPS = 1e-6
NEG = -1e30
SCALE = float(HD) ** -0.5
BLK_KT = 2
BLK_N = 512
RAW_SLOTS = 8
HL_SLOTS = 4

C_QK, C_V, C_DN, C_Z, C_BA, C_GATES = 0, 2048, 3072, 6144, 7168, 7200
D_QA, D_KV, D_QKG, D_VG, D_GG, D_LR = 0, 1024, 1536, 2560, 3584, 4608


def constants():
    p = np.arange(P)
    j, i = p[:, None], p[None, :]
    same = (j // CHUNK) == (i // CHUNK)
    fwd, bwd = same & (j <= i), same & (j >= i)
    out = {"ident": np.eye(P), "tri": np.stack([fwd, bwd], 1), "block": same,
           "neg": np.stack([np.where(m, 0, NEG) for m in (fwd, bwd)], 1),
           "half": np.stack([p < CHUNK, p >= CHUNK], 1)}
    level = np.zeros((P, 2, LEVELS, P))
    for n in range(LEVELS):
        s = 1 << n
        pair = (j // (2 * s)) == (i // (2 * s))
        level[:, 0, n] = pair & (j // s < i // s)
        level[:, 1, n] = pair & (j // s > i // s)
    out["level"] = level
    out["causal"] = np.stack([fwd, same & (j > i)], 1)
    out["flip"] = (same & (j % GRID_W + i % GRID_W == GRID_W - 1)) / SCALE
    cs, kc = np.clip(j % GRID_W - WIN_C // 2, 0, GRID_W - WIN_C), np.arange(GRID_W)
    out["window"] = np.where((kc >= cs) & (kc < cs + WIN_C), 0, NEG)
    q = p[:, None] + P * np.arange(TT)[None, :]
    k = np.arange(SEQ)
    out["band"] = np.where(np.abs(k - q[..., None]) <= P, 0, NEG)
    half = HD // 2
    inv = (1.0 / (np.float32(10000.0) ** (np.arange(half, dtype=np.float32) / np.float32(half)))).astype(np.float32)
    ang = q.astype(np.float32)[..., None] * inv
    out["cos"], out["sin"] = np.cos(ang), np.sin(ang)
    return {n: np.ascontiguousarray(a, dtype=np.float32).reshape(P, -1) for n, a in out.items()}


CONST_SHAPES = {"ident": (P,), "tri": (2, P), "block": (P,), "neg": (2, P), "half": (2,), "level": (2, LEVELS, P),
                "causal": (2, P), "window": (GRID_W,), "band": (TT, SEQ), "cos": (TT, HD // 2),
                "sin": (TT, HD // 2)}


def span(first, n):
    return slice(first, first + n) if isinstance(first, int) else bass.ds(first, n)


class Chunk:
    def __init__(self, w, row, col, blocks, kind, kt0=0, n=BLK_N):
        self.w, self.row, self.col, self.blocks, self.kind, self.kt0, self.n = w, row, col, blocks, kind, kt0, n


class Phase:
    def __init__(self, body, trips, step, act):
        self.body, self.trips, self.step, self.act = body, trips, step, act
        self.nb = sum(c.blocks for c in body)
        self.nc = len(body)


def number(phases):
    b = c = 0
    for ph in phases:
        ph.b0, ph.c0 = b, c
        for ch in ph.body:
            ch.b, ch.c = b, c
            b += ch.blocks
            c += 1
        b = ph.b0 + ph.nb * ph.trips
        c = ph.c0 + ph.nc * ph.trips
        assert ph.trips == 1 or (ph.nb % RAW_SLOTS == 0 and ph.nc % 2 == 0)
    return b


class Chain:
    def __init__(self, eng, sem):
        self.eng, self.sem, self.n, self.reg = eng, sem, 0, 0

    def __call__(self, ins):
        ins.then_inc(self.sem, 1)
        self.n += 1
        self.eng.wait_ge(self.sem, self.reg + self.n)
        return ins


class Loop:
    def __init__(self, eng, trips, chain=None, per=0):
        self.eng, self.trips, self.chain, self.per = eng, trips, chain, per

    def __enter__(self):
        if self.chain is not None:
            self.n0 = self.chain.n
        if self.trips == 1:
            return 0
        self.ctx = self.eng.Fori(0, self.trips)
        i = self.ctx.__enter__()
        if self.chain is not None:
            self.chain.reg = i * self.per
        return i

    def __exit__(self, *e):
        if self.trips > 1:
            self.ctx.__exit__(*e)
        if self.chain is not None and e[0] is None:
            if self.trips > 1:
                assert self.chain.n - self.n0 == self.per, (self.chain.n - self.n0, self.per)
                self.chain.n = self.n0 + self.per * self.trips
            self.chain.reg = 0


def build(nc, t):
    ctx = ExitStack()
    with ctx:
        def sem(name):
            return ctx.enter_context(nc.semaphore(name))

        BASE = 16512
        RAW0 = BASE
        SLOT = BLK_KT * BLK_N * 4
        WH0 = RAW0 + RAW_SLOTS * SLOT
        WL0 = WH0 + HL_SLOTS * SLOT
        A0 = WL0 + HL_SLOTS * SLOT
        R0 = A0 + 32768
        H0 = R0 + 65536
        T0 = H0 + 16384
        K = 1024

        def at(name, shape, off, dt=F32):
            return nc.alloc_sbuf_tensor_at(name, [P] + list(shape), dt, offset=off)

        raw = at("raw", [RAW_SLOTS, BLK_KT, BLK_N], RAW0)
        wh = at("wh", [HL_SLOTS, BLK_KT, BLK_N], WH0, F32R)
        wl = at("wl", [HL_SLOTS, BLK_KT, BLK_N], WL0, F32R)
        a1h = at("a1h", [KT, SEQ], A0, F32R)
        a1l = at("a1l", [KT, SEQ], A0 + 16 * K, F32R)
        a2h = at("a2h", [32, SEQ], R0, F32R)
        a2l = at("a2l", [32, SEQ], R0 + 32 * K, F32R)
        h = at("h", [TT, D], H0)

        tpos = [T0]

        def small(name, shape, dt=F32):
            n = int(np.prod(shape)) * 4
            x = at(name, shape, tpos[0], dt)
            tpos[0] += (n + 31) // 32 * 32
            return x

        ident = small("ident", [P])
        tri = small("tri", [2, P])
        blockm = small("block", [P])
        neg = small("neg", [2, P])
        half = small("half", [2])
        wmask = small("wmask", [GRID_W])
        ones = small("ones", [P])
        LV0 = tpos[0]
        level = small("level", [2, LEVELS, P])
        causal = at("causal", [2, P], LV0)
        rope_cs = at("rope_cs", [2, TT, HD // 2], LV0 + 1024)
        cw2 = at("cw2", [3, 88], LV0 + 2048)
        cb2 = at("cb2", [88], LV0 + 3136)
        gq_bc = at("gq_bc", [2, HD], LV0 + 3520)
        gout_bc = at("gout_bc", [GLA_DV], LV0 + 4544)
        sink_bc = at("sink_bc", [HEADS], LV0 + 5568)
        normw = small("normw", [4, KT])
        cw1 = small("cw1", [5, 24])
        dtal = small("dtal", [2, 16])
        onorm = small("onorm", [HD])
        ba = small("ba", [TT, 32])
        sc32 = {n: small(n, [HEADS, 2, TT]) for n in ("bt", "gg", "gc", "gl_c", "bte", "ekg")}
        tmp64 = {n: small(n, [64]) for n in ("ta", "tb", "tc")}
        ghalf = small("ghalf", [2, HEADS, 2, TT])
        glast = small("glast", [2, HEADS, 2, TT])
        st = small("st", [8])
        st8 = small("st8", [64])
        eps = small("eps", [1])
        pdum = small("pdum", [1])
        amx = small("amx", [2, TT]); asm = small("asm", [2, TT]); anm = small("anm", [2, TT]); aes = small("aes", [2, TT])
        S0 = tpos[0]
        assert 229368 - S0 >= 17 * K, 229368 - S0

        dnT = at("dnT", [24, SEQ], R0 + 40 * K)
        attqk = at("attqk", [16, SEQ], R0 + 16 * K)
        attv = at("attv", [TT, 1024], R0 + 8 * K)
        zs = at("zs", [TT, 1024], H0)
        gstage = at("gstage", [2, 1024], H0 + 8 * K)
        cvin = at("cvin", [2, 4, 260], S0)
        cvout = at("cvout", [2, 4, SEQ], S0 + 8352)
        bias = at("bias", [HEADS, TT, SEQ], S0)
        flip = at("flip", [P], S0 + 16 * K)
        asc = at("asc", [2, TT, SEQ], A0 + 16 * K)
        apr = at("apr", [2, TT, SEQ], A0 + 20 * K)
        apT = at("apT", [2, TT, SEQ], A0 + 24 * K)
        G = 4
        qgT = at("qgT", [G, 2, SEQ], A0)
        kgt = at("kgt", [G, 2, TT, HD], A0 + 8 * K)
        wTs = at("wTs", [G, 2, TT, P], A0 + 16 * K)
        uu = at("uu", [G, 2, TT, HD], A0 + 24 * K)
        qkT = at("qkT", [G, 2, TT, P], R0 + 16 * K)
        kbT, kbg, vb, egr, dec, AT, TB, PB, ATl, SS = ([] for _ in range(10))
        for n, (b0, b1, b2) in enumerate(((R0 + 24 * K, R0 + 8 * K, S0), (RAW0, RAW0 + 8 * K, RAW0 + 16 * K))):
            kbT.append(at(f"kbT{n}", [2, SEQ], b0))
            kbg.append(at(f"kbg{n}", [2, TT, HD], b0))
            vb.append(at(f"vb{n}", [2, TT, HD], b0 + 2 * K))
            egr.append(at(f"egr{n}", [2, TT, P], b0 + 4 * K))
            dec.append(at(f"dec{n}", [2, TT, P], b0 + 6 * K))
            AT.append(at(f"AT{n}", [2, TT, P], b1))
            TB.append(at(f"TB{n}", [2, 4, P], b1 + 2 * K))
            PB.append(at(f"PB{n}", [4, P], b1 + 6 * K))
            ATl.append(at(f"ATl{n}", [2, TT, LEVELS - 1, P], b2))
            SS.append(at(f"SS{n}", [2, G, HD], b2 + 10 * K))
        vn = at("vn", [G, HD], S0 + 14 * K)
        oacc = at("oacc", [TT, HEADS, HD], H0 + 8 * K)
        sqb = at("sqb", [2, 512], S0)
        rtb = at("rtb", [2, 512], S0 + 4 * K)
        osq = at("osq", [TT, HEADS, HD], A0)
        gld = at("gld", [2, 1024], R0 + 16 * K)
        mixa = at("mixa", [1024], R0 + 48 * K)
        mixb = at("mixb", [1024], R0 + 52 * K)
        xs = at("xs", [TT, D], R0)
        junk = at("junk", [D], R0 + 16 * K)
        wrow = at("wrow", [D], R0 + 24 * K)
        ffr = at("ffr", [1024], S0)
        ffq = at("ffq", [1024], S0 + 4 * K)
        qa = at("qa", [TT, 1024], R0 + 16 * K)
        kva = at("kva", [TT, 512], R0 + 24 * K)
        qkg = at("qkg", [8, SEQ], R0 + 48 * K)
        vg = at("vg", [TT, 1024], R0 + 56 * K)
        gg2 = at("gg2", [TT, 1024], S0)
        lrT = at("lrT", [SEQ], S0 + 8 * K)
        wa2 = at("wa2", [2, 512], S0 + 9 * K)
        gtok = at("gtok", [2, TT, 512], R0 + 24 * K)
        rtmp = at("rtmp", [TT, 1024], A0)
        rtmp2 = at("rtmp2", [TT, 1024], A0 + 8 * K)
        qT2 = at("qT2", [10, SEQ], A0 + 16 * K)
        bmask = at("bmask", [TT, SEQ], A0 + 26 * K)
        asc2 = at("asc2", [2, TT, SEQ], A0)
        apr2 = at("apr2", [2, TT, SEQ], A0 + 4 * K)
        apT2 = at("apT2", [2, TT, SEQ], A0 + 8 * K)
        eb = at("eb", [4, SEQ], A0)
        eD = at("eD", [4, SEQ], A0 + 4 * K)
        eE = at("eE", [4, SEQ], A0 + 8 * K)
        qga = at("qga", [4, SEQ], A0 + 12 * K)
        kga = at("kga", [4, SEQ], A0 + 16 * K)
        qin = at("qin", [4, SEQ], A0 + 20 * K)
        kou = at("kou", [4, SEQ], A0 + 24 * K)
        kot = at("kot", [4, TT, P], A0 + 28 * K)
        eb4 = at("eb4", [2048], A0 + 8 * K)
        aTm = at("aTm", [4, TT, P], S0 + 13 * K)
        S2 = at("S2", [2, 4, GLA_DV], R0 + 16 * K)
        oo2 = at("oo2", [TT, 4, GLA_DV], A0)
        oq2 = at("oq2", [TT, 4, GLA_DV], A0 + 8 * K)
        upad = at("upad", [2, 4, 258], S0)
        cg = at("cg", [2, 1024], S0 + 8320)

        bank = [ctx.enter_context(nc.psum_tensor(f"bank{n}", [P, 512], F32)) for n in range(4)]
        gp = [ctx.enter_context(nc.psum_tensor(f"gp{n}", [P, 1024], F32)) for n in range(2)]
        gates_dram = nc.dram_tensor("gates_dram", [8, P, 1024], F32, kind="Internal").ap()

        W1, W2 = t["w_in"], t["w_in_2"]
        acts = {"x1": (a1h, a1l), "hid": (a2h, a2l)}
        full = KT // BLK_KT
        PH = {}
        PH["ba"] = Phase([Chunk(W1, 0, C_BA, 1, "down", n=32)], 1, 0, "x1")
        PH["lead"] = Phase([Chunk(W1, 0, C_V, full, "down")], 1, 0, "x1")
        PH["v"] = Phase([Chunk(W1, 0, C_V + 512, full, "down")], 1, 0, "x1")
        PH["qk"] = Phase([Chunk(W1, 0, C_QK + 512 * n, full, "up") for n in range(2)], 2, 1024, "x1")
        PH["dn0"] = Phase([Chunk(W1, 0, C_DN + 512 * n, full, "up") for n in range(2)], 1, 0, "x1")
        PH["dn"] = Phase([Chunk(W1, 0, C_DN + 1024 + 512 * n, full, "up") for n in range(2)], 2, 1024, "x1")
        PH["z"] = Phase([Chunk(W1, 0, C_Z + 512 * n, full, "down") for n in range(2)], 1, 0, "x1")
        PH["gates0"] = Phase([Chunk(W1, 0, C_GATES + 512 * n, full, "up") for n in range(2)], 1, 0, "x1")
        PH["gates"] = Phase([Chunk(W1, 0, C_GATES + 1024 + 512 * n, full, "up") for n in range(2)], 3, 1024, "x1")
        PH["mix"] = Phase([Chunk(t["w_proj_a"], 0, 0, full // 2, "up", 0), Chunk(t["w_proj_b"], 0, 0, full // 2, "up", 8)], 4, 512, "hid")
        PH["out"] = Phase([Chunk(t["w_out"], 0, 512 * n, full, "down") for n in range(2)], 2, 1024, "x1")
        for g in range(2):
            PH[f"up{g}"] = Phase([Chunk(t["w_mlp_up"], 0, 4096 * g + 512 * n, full, "up") for n in range(2)], 4, 1024, "x1")
            PH[f"down{g}"] = Phase([Chunk(t["w_mlp_down"], 4096 * g, 512 * n, 32 // BLK_KT, "down") for n in range(2)], 2, 1024, "hid")
        PH["lr"] = Phase([Chunk(W2, 0, D_LR, 1, "up", n=32)], 1, 0, "x1")
        PH["kv"] = Phase([Chunk(W2, 0, D_KV, full, "down")], 1, 0, "x1")
        PH["qa"] = Phase([Chunk(W2, 0, D_QA + 512 * n, full, "down") for n in range(2)], 1, 0, "x1")
        PH["qkg"] = Phase([Chunk(W2, 0, D_QKG + 512 * n, full, "up") for n in range(2)], 1, 0, "x1")
        PH["vg"] = Phase([Chunk(W2, 0, D_VG + 512 * n, full, "down") for n in range(2)], 1, 0, "x1")
        PH["gg"] = Phase([Chunk(W2, 0, D_GG + 512 * n, full, "down") for n in range(2)], 1, 0, "x1")
        PH["out2"] = Phase([Chunk(t["w_out_2"], 0, 512 * n, full, "down") for n in range(2)], 2, 1024, "hid")
        for g, (n0, n1) in enumerate(((0, 6), (6, 11))):
            PH[f"ffa{g}"] = Phase([Chunk(t["w_up_2"], 0, base + 512 * n0, full, "up") for base in (0, DFF2)], 1, 0, "x1")
            PH[f"ff{g}"] = Phase([Chunk(t["w_up_2"], 0, base + 512 * (n0 + 1), full, "up") for base in (0, DFF2)],
                                 n1 - n0 - 1, 512, "x1")
            nk = (n1 - n0)
            PH[f"dd{g}"] = Phase([Chunk(t["w_down_2"], 512 * n0, 512 * n, 4 * nk // BLK_KT, "down") for n in range(4)], 1, 0, "hid")
        order = ["ba", "lead", "v", "qk", "dn0", "dn", "z", "gates0", "gates", "mix", "out", "up0", "down0", "up1", "down1",
                 "lr", "kv", "qa", "qkg", "vg", "gg", "out2", "ffa0", "ff0", "dd0", "ffa1", "ff1", "dd1"]
        phases = [PH[n] for n in order]
        BLOCKS = number(phases)

        s_raw = [sem(f"s_raw{n}") for n in range(RAW_SLOTS)]
        s_hi, s_lo = sem("s_hi"), sem("s_lo")
        s_blk = sem("s_blk")
        s_free = [sem(f"s_free{n}") for n in range(2)]
        s_act, s_dve = sem("s_act"), sem("s_dve")
        names = ("s_const s_const2 s_x s_hx s_ss s_ms s_rt s_xs s_tr s_trh s_trl s_cvo "
                 "  s_bias s_qk s_sc s_mx s_ex s_p s_pt s_pT s_o s_ah s_al  s_bag  s_lsq s_lsum s_lrt s_lfree "
                 "s_gate s_gcm s_gcols   s_r1 s_r1a  s_gram s_dm s_AT s_ATl s_t1p s_t1 s_P s_Pc s_X s_TB s_tok s_tokd "
                 "s_uw s_uwc s_ws s_vn s_os s_oc s_su s_S s_or s_ord s_mixa s_mixh s_mixl  s_ffh s_ffl  s_norm  "
                 " s_qr  s_qn s_q2T s_q2c s_gt s_gta s_gtd s_bm s_bc s_bD s_bE  s_aTp s_aTm s_kop s_koc "
                 "s_kv2 s_S2  s_oev s_or2 s_or2d s_cv  s_store s_od s_qg s_kb s_qks s_t1d s_eb s_ea s_oin s_oi s_sil s_prod s_cv2 "
                 "s_wrow s_roped s_wa s_waz s_wal s_wm s_set").split()
        s_gst = [sem(f"s_gst{n}") for n in range(2)]
        s_gld = [sem(f"s_gld{n}") for n in range(2)]
        S = {n: sem(n) for n in names}

        def raw_value(idx, i, nb):
            return 16 * (idx // RAW_SLOTS + 1) + i * (16 * nb // RAW_SLOTS)

        def last_block(ph):
            return ph.b0 + ph.nb * ph.trips

        NCONST = 18
        NCONST2 = 11
        TG = {"mix": 0, "yb": 8, "mlp": 12, "norm1": 20, "cat": 28, "norm2": 32}
        NS = {"mix": 0, "mlp": 1, "final": 2, "norm1": 3, "norm2": 4}

        def wait_read_out(eng, ph, trip, n):
            ch = ph.body[n]
            eng.wait_ge(s_free[ch.c % 2], ch.c // 2 + 1 + trip * (ph.nc // 2))

        LV = LEVELS - 1

        def pair_count(hh, n=1, rounds=1):
            return 2 * rounds * (hh // 2) + 2 * (n - 1) + hh % 2 + 1

        block = ctx.enter_context(nc.Block())

        @block.sync
        def _(sp):
            def stream(ph):
                with Loop(sp, ph.trips) as i:
                    for n, ch in enumerate(ph.body):
                        for j in range(ch.blocks):
                            idx = ch.b + j
                            slot = idx % RAW_SLOTS
                            if ph is PH["mix"] and j == 0 and n == 1:
                                sp.wait_ge(S["s_od"], 4)
                            if idx >= RAW_SLOTS:
                                sp.wait_ge(s_hi, idx - RAW_SLOTS + 1 + i * ph.nb)
                                sp.wait_ge(s_lo, idx - RAW_SLOTS + 1 + i * ph.nb)
                            if ch.n == BLK_N:
                                rows = ch.w[ch.row + j * BLK_KT * P:ch.row + (j + 1) * BLK_KT * P, :]
                                src = rows.rearrange("(t p) n -> p t n", p=P)[:, :, bass.ds(ch.col + i * ph.step, BLK_N)] \
                                    if ph.trips > 1 else rows.rearrange("(t p) n -> p t n", p=P)[:, :, ch.col:ch.col + BLK_N]
                                sp.dma_start(raw[:, slot], src).then_inc(s_raw[slot], 16)
                            else:
                                src = ch.w.rearrange("(t p) n -> p t n", p=P)[:, :, ch.col:ch.col + ch.n]
                                dst = raw[:, slot, 0, :].rearrange("p (t n) -> p t n", n=ch.n)
                                sp.dma_start(dst, src).then_inc(s_raw[slot], 16)
            sp.dma_start(h[:, :, :], t["x"][0].rearrange("(t p) n -> p t n", p=P)).then_inc(S["s_x"], 16)
            for name in order:
                stream(PH[name])
            wait_read_out(sp, PH["dd1"], 0, 2)
            wait_read_out(sp, PH["dd1"], 0, 3)
            sp.dma_start(t["out"][0].rearrange("(t p) n -> p t n", p=P), h[:, :, :]).then_inc(S["s_store"], 16)
            sp.wait_ge(S["s_store"], 16)

        @block.scalar
        def _(act):
            chain = Chain(act, s_act)

            def split(idx, i, nb):
                if idx >= BLOCKS:
                    return
                act.wait_ge(s_raw[idx % RAW_SLOTS], raw_value(idx, i, nb))
                if idx >= HL_SLOTS:
                    act.wait_ge(s_blk, idx - HL_SLOTS + 1 + i * nb)
                if idx == 0:
                    nc.scalar.copy(wh[:, 0, 0, :], raw[:, 0, 0, :]).then_inc(s_hi, 1)
                else:
                    nc.scalar.copy(wh[:, idx % HL_SLOTS], raw[:, idx % RAW_SLOTS]).then_inc(s_hi, 1)

            def gemm(ph, read_out, per=0):
                with Loop(act, ph.trips, chain, per) as i:
                    for n, ch in enumerate(ph.body):
                        for j in range(ch.blocks):
                            split(ch.b + HL_SLOTS + j, i, ph.nb)
                        if read_out is not None:
                            act.wait_ge(s_blk, ch.b + ch.blocks + i * ph.nb)
                            read_out(n, i, gp[ch.c % 2], s_free[ch.c % 2])

            def norm_stats(name):
                k = NS[name]
                for tt in range(TT):
                    a = nc.scalar.activation(junk[:, :], h[:, tt, :], ACT.Square, accum_out=st[:, tt:tt + 1])
                    if tt == 0:
                        chain(a)
                    else:
                        a.then_inc(S["s_ss"], 1)
                act.wait_ge(S["s_ms"], k + 1)
                nc.scalar.activation(st[:, 4:6], st[:, 2:4], ACT.Sqrt).then_inc(S["s_rt"], 1)

            def turn_hi(base, groups, dst, kt0, w=None):
                for g in range(groups):
                    act.wait_ge(S["s_tr"], base + g + 1)
                    if w is None:
                        a = nc.scalar.copy(dst[:, kt0 + 2 * g:kt0 + 2 * g + 2, :], bank[g % 4][:, :].rearrange("p (k n) -> p k n", k=2))
                    else:
                        for m in range(2):
                            kt = 2 * g + m
                            a = nc.scalar.activation(dst[:, kt0 + kt, :], bank[g % 4][:, m * SEQ:(m + 1) * SEQ], ACT.Copy,
                                                     scale=normw[:, w, kt:kt + 1])
                    a.then_inc(S["s_trh"], 1)

            def attention(base, scores, probs, probsT, sink):
                for hh in range(HEADS + 2):
                    if hh < HEADS:
                        act.wait_ge(S["s_mx"], base + hh + 1)
                        if hh >= 2:
                            act.wait_ge(S["s_pt"], base + hh - 1)
                        b = hh % 2
                        for tt in range(TT):
                            a = nc.scalar.activation(probs[:, b, tt, :], scores[:, b, tt, :], ACT.Exp,
                                                     bias=anm[:, b, tt:tt + 1], accum_out=asm[:, b, tt:tt + 1])
                        if sink:
                            a = nc.scalar.activation(aes[:, b, :], anm[:, b, :], ACT.Exp, bias=sink_bc[:, hh:hh + 1])
                        a.then_inc(S["s_ex"], 1)
                    if 1 <= hh <= HEADS:
                        k = hh - 1
                        act.wait_ge(S["s_pt"], base + k + 1)
                        if k >= 2:
                            act.wait_ge(S["s_o"], base + k - 1)
                        nc.scalar.copy(probsT[:, k % 2], bank[2 + k % 2][:, :].rearrange("p (k n) -> p k n", k=2)).then_inc(S["s_pT"], 1)
                    if hh >= 2:
                        k = hh - 2
                        act.wait_ge(S["s_o"], base + k + 1)
                        nc.scalar.copy(a2h[:, k, :], gp[0][:, (k % 2) * 512:(k % 2) * 512 + SEQ]).then_inc(S["s_ah"], 1)

            act.wait_ge(S["s_x"], 16)
            norm_stats("mix")
            act.wait_ge(S["s_const"], 16 * NCONST)
            turn_hi(TG["mix"], 8, a1h, 0, 0)
            for n in range(HL_SLOTS):
                split(n, 0, 0)

            def to_ba(n, i, g, free):
                nc.scalar.copy(ba[:, :, :], g[:, :].rearrange("p (t n) -> p t n", t=TT)[:, :, 0:32]).then_inc(free, 1)

            def to_v(col):
                def f(n, i, g, free):
                    nc.scalar.copy(attv[:, :, col:col + 512], g[:, :].rearrange("p (t n) -> p t n", t=TT)).then_inc(free, 1)
                return f

            def to_qk(n, i, g, free):
                nc.scalar.copy(attqk[:, bass.ds(8 * i + 4 * n, 4), :], g[:, :].rearrange("p (m n) -> p m n", m=4)).then_inc(free, 1)

            def activate_dn(q, n):
                act.wait_ge(S["s_cv"], q + 1)
                nc.scalar.activation(dnT[:, span(4 * q, 4), :], cvout[:, n, :, :], ACT.Silu).then_inc(S["s_cvo"], 1)

            def to_dn(q0):
                def f(n, i, g, free):
                    q = 2 * i + q0 + n
                    if q0 or n:
                        activate_dn(q - 1, 1 - n)
                        act.wait_ge(S["s_cvo"], q)
                    for m in range(4):
                        nc.scalar.activation(cvout[:, n, m, :], g[:, m * SEQ:(m + 1) * SEQ], ACT.Copy,
                                             scale=cw1[:, 2, span(4 * q + m, 1)])
                    nc.scalar.copy(cvin[:, n, :, 2:2 + SEQ], g[:, :].rearrange("p (m n) -> p m n", m=4)).then_inc(free, 1)
                return f

            def to_z(n, i, g, free):
                nc.scalar.activation(zs[:, :, n * 512:(n + 1) * 512], g[:, :].rearrange("p (t n) -> p t n", t=TT),
                                     ACT.Silu).then_inc(free, 1)

            def to_gates0(n, i, g, free):
                nc.scalar.activation(gstage[:, n, :], g[:, :], ACT.Sigmoid).then_inc(free, 1)

            def to_gates(n, i, g, free):
                act.wait_ge(s_gst[n], 16 * i + 16)
                nc.scalar.activation(gstage[:, n, :], g[:, :], ACT.Sigmoid).then_inc(free, 1)

            gemm(PH["ba"], to_ba)
            gemm(PH["lead"], to_v(0))
            gemm(PH["v"], to_v(512))
            gemm(PH["qk"], to_qk)
            gemm(PH["dn0"], to_dn(0))
            gemm(PH["dn"], to_dn(2))
            activate_dn(5, 1)
            gemm(PH["z"], to_z)
            gemm(PH["gates0"], to_gates0)
            gemm(PH["gates"], to_gates)
            attention(0, asc, apr, apT, False)

            tb, tc = tmp64["tb"], tmp64["tc"]
            beta_in = ba[:, :, 0:16].rearrange("p t (d h) -> p h d t", d=2)
            nc.scalar.activation(sc32["bt"][:, :, :, :], beta_in, ACT.Sigmoid).then_inc(S["s_bag"], 1)
            chain(nc.scalar.activation(dtal[:, 1, :], dtal[:, 1, :], ACT.Exp))
            act.wait_ge(S["s_gate"], 1)
            chain(nc.scalar.activation(tc[:, 0:32], tb[:, 0:32], ACT.Exp))
            nc.scalar.activation(tc[:, 0:32], tc[:, 0:32], ACT.Ln, bias=1.0).then_inc(S["s_bag"], 1)
            act.wait_ge(S["s_gcols"], 1)
            nc.scalar.activation(sc32["ekg"][:, :, :, :], sc32["gl_c"][:, :, :, :], ACT.Exp)
            nc.scalar.activation(sc32["bte"][:, :, :, :], sc32["gc"][:, :, :, :], ACT.Exp)
            nc.scalar.activation(glast[:, :, :, :, :], bank[1][:, 64:128].rearrange("p (a h d t) -> p a h d t", a=2, h=8, d=2),
                                 ACT.Exp).then_inc(S["s_bag"], 1)
            for j in range(9):
                if j < 8:
                    if j >= 2:
                        act.wait_ge(S["s_lsum"], j - 1)
                    nc.scalar.activation(sqb[:, j % 2, :], dnT[:, 2 * j:2 * j + 2, :].rearrange("p k n -> p (k n)"), ACT.Square).then_inc(S["s_lsq"], 1)
                if j >= 1:
                    k = j - 1
                    act.wait_ge(S["s_lsum"], k + 1)
                    if k >= 2:
                        act.wait_ge(S["s_lfree"], k - 1)
                    nc.scalar.activation(rtb[:, k % 2, :], bank[2 + k % 2][:, :], ACT.Sqrt, bias=eps[:, 0:1]).then_inc(S["s_lrt"], 1)
            for n in range(2):
                act.wait_ge(s_gst[n], 16 * 4)
            for h0 in range(0, HEADS, 2):
                pair = (h0, h0 + 1)
                for hh in pair:
                    act.wait_ge(S["s_dm"], hh + 1)
                    x = dec[hh % 2][:, :, :, :]
                    nc.scalar.activation(x, x, ACT.Exp).then_inc(S["s_r1a"], 1)
                for hh in pair:
                    if hh >= 2:
                        act.wait_ge(S["s_qg"], hh - 1)
                    nc.scalar.activation(egr[hh % 2][:, :, :, :], bank[2 * (hh % 2)][:, :].rearrange("p (d t n) -> p d t n", d=2, t=TT),
                                         ACT.Exp).then_inc(S["s_r1a"], 1)
                for hh in pair:
                    act.wait_ge(S["s_t1p"], hh + 1)
                    nc.scalar.copy(TB[hh % 2][:, 0, :, :], bank[2 * (hh % 2)][:, :].rearrange("p (q n) -> p q n", q=4)).then_inc(S["s_t1"], 1)
                for n in range(1, LEVELS):
                    for hh in pair:
                        act.wait_ge(S["s_P"], pair_count(hh, n, LV))
                        nc.scalar.copy(PB[hh % 2][:, :, :], bank[2 * (hh % 2)][:, :].rearrange("p (q n) -> p q n", q=4)).then_inc(S["s_Pc"], 1)
                for hh in pair:
                    act.wait_ge(S["s_uw"], hh + 1)
                    nc.scalar.copy(uu[:, hh % G], gp[hh % 2][:, 0:512].rearrange("p (d t n) -> p d t n", d=2, t=TT))
                    nc.scalar.copy(wTs[:, hh % G], gp[hh % 2][:, 512:1024].rearrange("p (d t n) -> p d t n", d=2, t=TT)).then_inc(S["s_uwc"], 1)
                g = hh % G
                if g == G - 1:
                    gr = hh // G
                    for s in range(2):
                        act.wait_ge(S["s_os"], 4 * gr + s + 1)
                        for d in range(2):
                            c = s if d == 0 else NCH - 1 - s
                            lo, tl = CHUNK * (c % 2), c // 2
                            a = nc.scalar.copy(oacc[lo:lo + CHUNK, tl, G * gr:G * gr + G, :],
                                               bank[1][lo:lo + CHUNK, :].rearrange("p (g n) -> p g n", g=G))
                        a.then_inc(S["s_oc"], 1)
            act.wait_ge(S["s_od"], 4)
            nc.scalar.activation(osq[:, :, :, :], oacc[:, :, :, :], ACT.Square).then_inc(S["s_or"], 1)
            act.wait_ge(S["s_ord"], 1)
            nc.scalar.activation(st8[:, 16:32], st8[:, 0:16], ACT.Sqrt).then_inc(S["s_or"], 1)
            turn_hi(TG["yb"], 4, a2h, 8)

            def to_mix(n, i, g, free):
                if n == 1:
                    act.wait_ge(S["s_mixa"], i + 1)
                    nc.scalar.copy(a1h[:, bass.ds(4 * i, 4), :], mixb[:, :].rearrange("p (m n) -> p m n", m=4)).then_inc(S["s_mixh"], 1)
            gemm(PH["mix"], to_mix)
            gemm(PH["out"], None)

            def wait_products(ph):
                wait_read_out(act, ph, ph.trips - 1, ph.nc - 2)
                wait_read_out(act, ph, ph.trips - 1, ph.nc - 1)

            wait_products(PH["out"])
            norm_stats("mlp")
            turn_hi(TG["mlp"], 8, a1h, 0, 1)

            def to_hidden(ph):
                def f(n, i, g, free):
                    nc.scalar.activation(ffr[:, :], g[:, :], ACT.Relu).then_inc(free, 1)
                    wait_read_out(act, ph, i, n)
                    chain(nc.scalar.activation(ffq[:, :], ffr[:, :], ACT.Square))
                    nc.scalar.copy(a2h[:, bass.ds(8 * i + 4 * n, 4), :], ffq[:, :].rearrange("p (m n) -> p m n", m=4)).then_inc(S["s_ffh"], 1)
                return f

            for k in range(2):
                gemm(PH[f"up{k}"], to_hidden(PH[f"up{k}"]), 2)
                gemm(PH[f"down{k}"], None)
            wait_products(PH["down1"])
            norm_stats("final")
            act.wait_ge(S["s_norm"], 1)
            norm_stats("norm1")
            turn_hi(TG["norm1"], 8, a1h, 0, 2)

            def to_lr(n, i, g, free):
                nc.scalar.copy(lrT[0:32, :], g[0:32, 0:SEQ]).then_inc(free, 1)

            def to_rows(dst, func=ACT.Copy):
                def f(n, i, g, free):
                    nc.scalar.activation(dst[:, :, n * 512:(n + 1) * 512], g[:, :].rearrange("p (t n) -> p t n", t=TT), func).then_inc(free, 1)
                return f

            def to_qkg(n, i, g, free):
                nc.scalar.copy(qkg[:, 4 * n:4 * n + 4, :], g[:, :].rearrange("p (m n) -> p m n", m=4)).then_inc(free, 1)

            gemm(PH["lr"], to_lr)
            gemm(PH["kv"], to_rows(kva))
            gemm(PH["qa"], to_rows(qa))
            gemm(PH["qkg"], to_qkg)
            gemm(PH["vg"], to_rows(vg))
            gemm(PH["gg"], to_rows(gg2, ACT.Silu))
            act.wait_ge(s_blk, last_block(PH["gg"]))
            chain(nc.scalar.activation(rtmp[:, :, :], qa[:, :, :], ACT.Square))
            nc.scalar.activation(rtmp2[:, :, 0:256], kva[:, :, 0:256], ACT.Square).then_inc(S["s_qr"], 1)
            act.wait_ge(S["s_qn"], 1)
            nc.scalar.activation(st8[:, 32:52], st8[:, 0:20], ACT.Sqrt).then_inc(S["s_qr"], 1)
            for g in range(5):
                act.wait_ge(S["s_q2T"], g + 1)
                nc.scalar.copy(qT2[:, 2 * g:2 * g + 2, :], bank[g % 4][:, :].rearrange("p (k n) -> p k n", k=2)).then_inc(S["s_q2c"], 1)
            attention(HEADS, asc2, apr2, apT2, True)
            act.wait_ge(S["s_al"], 2 * HEADS)
            for q in range(4):
                act.wait_ge(S["s_gt"], q + 1)
                a = nc.scalar.copy(gtok[:, q // 2, q % 2, :], bank[q][:, :])
            a.then_inc(S["s_gta"], 1)
            act.wait_ge(S["s_gtd"], 1)
            chain(nc.scalar.activation(eb4[:, :], eb4[:, :], ACT.Exp))
            nc.scalar.activation(eb4[:, :], eb4[:, :], ACT.Ln, bias=1.0).then_inc(S["s_gta"], 1)
            for d in range(2):
                last = CHUNK - 1 if d == 0 else 0
                act.wait_ge(S["s_bc"], d + 1)
                if d:
                    act.wait_ge(S["s_bE"], 3)
                    act.wait_ge(S["s_aTp"], 1)
                    act.wait_ge(S["s_oin"], 1)
                nc.scalar.activation(eb[:, :, :], gp[0][:, :].rearrange("p (h n) -> p h n", h=4), ACT.Copy, scale=1.0 / 16).then_inc(S["s_eb"], 1)
                act.wait_ge(S["s_eb"], d + 1)
                chain(nc.scalar.activation(st8[:, 0:16].rearrange("p (h c) -> p h c", h=4),
                                           eb[:, :, :].rearrange("p h (c n) -> p h c n", n=CHUNK)[:, :, :, last], ACT.Exp))
                nc.scalar.activation(qin[:, :, :], eb[:, :, :], ACT.Exp).then_inc(S["s_ea"], 1)
                act.wait_ge(S["s_bD"], 2 * d + 1)
                nc.scalar.activation(qga[:, :, :], eD[:, :, :], ACT.Exp)
                nc.scalar.activation(kga[:, :, :], eD[:, :, :], ACT.Exp, scale=-1.0).then_inc(S["s_ea"], 1)
                act.wait_ge(S["s_bD"], 2 * d + 2)
                nc.scalar.activation(kou[:, :, :], eE[:, :, :], ACT.Exp, scale=-1.0).then_inc(S["s_ea"], 1)
                act.wait_ge(S["s_kop"], d + 1)
                nc.scalar.copy(kot[:, :, :, :], gp[0][:, :].rearrange("p (h t n) -> p h t n", h=4, t=TT)).then_inc(S["s_koc"], 1)
            act.wait_ge(S["s_oin"], 2)
            for tt in range(TT):
                for k in range(2):
                    a = nc.scalar.copy(oo2[:, tt, 2 * k:2 * k + 2, :], bank[2 * tt + k][:, :].rearrange("p (h n) -> p h n", h=2))
            a.then_inc(S["s_oev"], 1)
            act.wait_ge(S["s_oev"], 1)
            nc.scalar.activation(oq2[:, :, :, :], oo2[:, :, :, :], ACT.Square).then_inc(S["s_or2"], 1)
            act.wait_ge(S["s_or2d"], 1)
            nc.scalar.activation(st8[:, 16:24], st8[:, 0:8], ACT.Sqrt).then_inc(S["s_or2"], 1)
            turn_hi(TG["cat"], 4, a2h, 8)
            gemm(PH["out2"], None)
            wait_products(PH["out2"])
            norm_stats("norm2")
            turn_hi(TG["norm2"], 8, a1h, 0, 3)

            def hidden_hi(q, tile):
                act.wait_ge(S["s_prod"], q + 1)
                nc.scalar.copy(a2h[:, span(tile, 4), :], cg[:, 1, :].rearrange("p (m n) -> p m n", m=4)).then_inc(S["s_ffh"], 1)

            def to_ff(q0, after):
                def f(n, i, g, free):
                    q = i + q0
                    if n == 0 and after:
                        hidden_hi(q - 1, 4 * i)
                        act.wait_ge(S["s_ffh"], 16 + q)
                    if n == 1 and after:
                        act.wait_ge(S["s_ffl"], 16 + q)
                    for m in range(4):
                        col = span(4 * q + 44 * n + m, 1)
                        nc.scalar.activation(cg[:, n, m * SEQ:(m + 1) * SEQ], g[:, m * SEQ:(m + 1) * SEQ], ACT.Identity,
                                             scale=cw2[:, 1, col], bias=cb2[:, col])
                    nc.scalar.copy(upad[:, n, :, 1:1 + SEQ], g[:, :].rearrange("p (m n) -> p m n", m=4)).then_inc(free, 1)
                    if n == 1:
                        act.wait_ge(S["s_cv2"], q + 1)
                        nc.scalar.activation(cg[:, 0, :], cg[:, 0, :], ACT.Silu).then_inc(S["s_sil"], 1)
                return f
            gemm(PH["ffa0"], to_ff(0, False))
            gemm(PH["ff0"], to_ff(1, True))
            hidden_hi(5, 20)
            gemm(PH["dd0"], None)
            gemm(PH["ffa1"], to_ff(6, False))
            gemm(PH["ff1"], to_ff(7, True))
            hidden_hi(10, 16)
            gemm(PH["dd1"], None)

        @block.vector
        def _(dve):
            V = nc.vector
            chain = Chain(dve, s_dve)

            def split(idx, i, nb):
                if idx >= BLOCKS:
                    return
                dve.wait_ge(s_raw[idx % RAW_SLOTS], raw_value(idx, i, nb))
                dve.wait_ge(s_hi, idx + 1 + i * nb)
                if idx == 0:
                    V.tensor_tensor(wl[:, 0, 0, :], raw[:, 0, 0, :], wh[:, 0, 0, :].bitcast(F32), ALU.subtract).then_inc(s_lo, 1)
                else:
                    V.tensor_tensor(wl[:, idx % HL_SLOTS], raw[:, idx % RAW_SLOTS], wh[:, idx % HL_SLOTS].bitcast(F32),
                                    ALU.subtract).then_inc(s_lo, 1)

            def gemm(ph, read_out, per=0, waits=True):
                with Loop(dve, ph.trips, chain, per) as i:
                    for n, ch in enumerate(ph.body):
                        for j in range(ch.blocks):
                            split(ch.b + HL_SLOTS + j, i, ph.nb)
                        if read_out is not None:
                            if waits:
                                dve.wait_ge(s_blk, ch.b + ch.blocks + i * ph.nb)
                            read_out(n, i, gp[ch.c % 2], s_free[ch.c % 2])

            def norm_rows(name, weights=None):
                k = NS[name]
                dve.wait_ge(S["s_ss"], k + 1)
                V.tensor_scalar(st[:, 2:4], st[:, 0:2], 1.0 / D, EPS, ALU.mult, ALU.add).then_inc(S["s_ms"], 1)
                dve.wait_ge(S["s_rt"], k + 1)
                chain(V.reciprocal(st[:, 6:8], st[:, 4:6]))
                for tt in range(TT):
                    if weights is None:
                        a = V.tensor_scalar(xs[:, tt, :], h[:, tt, :], st[:, 6 + tt:7 + tt], None, ALU.mult)
                    else:
                        a = V.scalar_tensor_tensor(h[:, tt, :], h[:, tt, :], st[:, 6 + tt:7 + tt], weights, ALU.mult, ALU.mult)
                a.then_inc(S["s_xs"] if weights is None else S["s_norm"], 1)

            def turn_lo(base, groups, hi, lo, kt0, w=None):
                for g in range(groups):
                    dve.wait_ge(S["s_trh"], base + g + 1)
                    if w is None:
                        sl = slice(kt0 + 2 * g, kt0 + 2 * g + 2)
                        a = V.tensor_tensor(lo[:, sl, :], bank[g % 4][:, :].rearrange("p (k n) -> p k n", k=2),
                                            hi[:, sl, :].bitcast(F32), ALU.subtract)
                    else:
                        for m in range(2):
                            kt = 2 * g + m
                            a = V.scalar_tensor_tensor(lo[:, kt0 + kt, :], bank[g % 4][:, m * SEQ:(m + 1) * SEQ], normw[:, w, kt:kt + 1],
                                                       hi[:, kt0 + kt, :].bitcast(F32), ALU.mult, ALU.subtract)
                    a.then_inc(S["s_trl"], 1)

            def attention(base, scores, probs, mask, sink):
                for hh in range(HEADS + 2):
                    b = hh % 2
                    if hh < HEADS:
                        dve.wait_ge(S["s_qk"], base + hh + 1)
                        if hh >= 2:
                            dve.wait_ge(S["s_ex"], base + hh - 1)
                        V.scalar_tensor_tensor(scores[:, b].rearrange("p t (r c) -> p (t r) c", c=mask.shape[2]),
                                               bank[b][:, :].rearrange("p (r c) -> p r c", c=mask.shape[2]), SCALE, mask, ALU.mult, ALU.add).then_inc(S["s_sc"], 1)
                        dve.wait_ge(S["s_sc"], base + hh + 1)
                        chain(V.tensor_reduce(amx[:, b, :], scores[:, b], AXX, ALU.max))
                        if sink:
                            chain(V.tensor_scalar(amx[:, b, :], amx[:, b, :], sink_bc[:, hh:hh + 1], None, ALU.max))
                        V.tensor_scalar(anm[:, b, :], amx[:, b, :], -1.0, None, ALU.mult).then_inc(S["s_mx"], 1)
                    if 1 <= hh <= HEADS:
                        k = (hh - 1) % 2
                        dve.wait_ge(S["s_ex"], base + hh)
                        if sink:
                            chain(V.tensor_tensor(asm[:, k, :], asm[:, k, :], aes[:, k, :], ALU.add))
                        chain(V.reciprocal(asm[:, k, :], asm[:, k, :]))
                        for tt in range(TT):
                            a = V.tensor_scalar(probs[:, k, tt, :], probs[:, k, tt, :], asm[:, k, tt:tt + 1], None, ALU.mult)
                        a.then_inc(S["s_p"], 1)
                    if hh >= 2:
                        k = hh - 2
                        dve.wait_ge(S["s_ah"], base + k + 1)
                        V.tensor_tensor(a2l[:, k, :], gp[0][:, (k % 2) * 512:(k % 2) * 512 + SEQ], a2h[:, k, :].bitcast(F32),
                                        ALU.subtract).then_inc(S["s_al"], 1)

            chain(V.memset(eps[:, :], EPS))
            V.memset(ones[:, :], 1.0)
            V.memset(cvin[:, :, :, 0:2], 0.0)
            V.memset(cvin[:, :, :, 2 + SEQ:4 + SEQ], 0.0).then_inc(S["s_set"], 1)
            norm_rows("mix")
            dve.wait_ge(S["s_const"], 16 * NCONST)
            turn_lo(TG["mix"], 8, a1h, a1l, 0, 0)
            for n in range(HL_SLOTS):
                split(n, 0, 0)

            def to_dn(q0):
                def f(n, i, g, free):
                    q = 2 * i + q0 + n
                    wait_read_out(dve, PH["dn" if q0 else "dn0"], i, n)
                    for tap in (0, 1, 3, 4):
                        for m in range(4):
                            o = cvout[:, n, m, :]
                            a = V.scalar_tensor_tensor(o, cvin[:, n, m, tap:tap + SEQ], cw1[:, tap, span(4 * q + m, 1)], o,
                                                       ALU.mult, ALU.add)
                        if tap < 4:
                            chain(a)
                    a.then_inc(S["s_cv"], 1)
                return f

            for name in ("ba", "lead", "v", "qk"):
                gemm(PH[name], None)
            gemm(PH["dn0"], to_dn(0), 6, waits=False)
            gemm(PH["dn"], to_dn(2), 6, waits=False)
            for name in ("z", "gates0", "gates"):
                gemm(PH[name], None)
            dve.wait_ge(S["s_wm"], 16)
            attention(0, asc, apr, wmask[:, :].unsqueeze(1).to_broadcast([P, 8, GRID_W]), False)

            bt, gg, gc, glc, bte, ekg = (sc32[n] for n in ("bt", "gg", "gc", "gl_c", "bte", "ekg"))
            ta, tb, tc = (tmp64[n] for n in ("ta", "tb", "tc"))
            hdt = dict(h=HEADS, d=2, t=TT)
            ta4, tc4 = (x[:, 0:32].rearrange("p (h d t) -> p h d t", **hdt) for x in (ta, tc))
            alpha = ba[:, :, 16:32].rearrange("p t (d h) -> p h d t", d=2)

            def per_head_dir(row):
                return row.rearrange("p (d h) -> p h d", d=2).unsqueeze(3).to_broadcast([P, HEADS, 2, TT])

            chain(V.tensor_tensor(ta4, alpha, per_head_dir(dtal[:, 0, :]), ALU.add))
            V.scalar_tensor_tensor(tb[:, 0:32], ta[:, 0:32], -1.0, ta[:, 0:32], ALU.mult, ALU.min).then_inc(S["s_gate"], 1)
            dve.wait_ge(S["s_bag"], 2)
            chain(V.scalar_tensor_tensor(tc[:, 0:32], ta[:, 0:32], 0.0, tc[:, 0:32], ALU.max, ALU.add))
            chain(V.tensor_scalar(tc[:, 0:32], tc[:, 0:32], -1.0, None, ALU.mult))
            chain(V.tensor_tensor(gg[:, :, :, :], tc4, per_head_dir(dtal[:, 1, :]), ALU.mult))
            for a in range(2):
                i_ = V.tensor_scalar(ghalf[:, a], gg[:, :, :, :], half[:, a:a + 1], None, ALU.mult)
            i_.then_inc(S["s_gate"], 1)
            dve.wait_ge(S["s_gcm"], 1)
            chain(V.tensor_copy(gc[:, :, :, :], bank[0][:, 0:32].rearrange("p (d h t) -> p h d t", d=2, h=HEADS)))
            V.tensor_tensor(glc[:, :, :, :], bank[1][:, 0:32].rearrange("p (h d t) -> p h d t", **hdt), gc[:, :, :, :],
                            ALU.subtract).then_inc(S["s_gcols"], 1)
            dve.wait_ge(S["s_bag"], 3)
            chain(V.tensor_tensor(bte[:, :, :, :], bte[:, :, :, :], bt[:, :, :, :], ALU.mult))
            for j in range(8):
                dve.wait_ge(S["s_lrt"], j + 1)
                chain(V.reciprocal(rtb[:, j % 2, :], rtb[:, j % 2, :]))
                x = dnT[:, 2 * j:2 * j + 2, :].rearrange("p k n -> p (k n)")
                V.scalar_tensor_tensor(x, x, SCALE if j < 4 else 1.0, rtb[:, j % 2, :], ALU.mult, ALU.mult).then_inc(S["s_lfree"], 1)
            dve.wait_ge(S["s_lfree"], 8)

            def over_dirs(x):
                return x.unsqueeze(1).to_broadcast([P, 2] + list(x.shape[1:]))

            def rows(x, hh):
                return x[:, hh].unsqueeze(3).to_broadcast([P, 2, TT, P])

            for h0 in range(0, HEADS, 2):
                pair = (h0, h0 + 1)
                for hh in pair:
                    b = hh % 2
                    dve.wait_ge(S["s_r1"], hh + 1)
                    for d in range(2):
                        for tt in range(TT):
                            q = d * 2 + tt
                            a = V.scalar_tensor_tensor(dec[b][:, d, tt, :], bank[2 * b][:, q * P:(q + 1) * P], gc[:, hh, d, tt:tt + 1],
                                                       neg[:, d, :], ALU.subtract, ALU.add)
                    a.then_inc(S["s_dm"], 1)
                    V.tensor_tensor(kbT[b][:, :, :], bank[2 * b + 1][:, :].rearrange("p (d n) -> p d n", d=2), over_dirs(dnT[:, 8 + hh, :]),
                                    ALU.mult).then_inc(S["s_kb"], 1)
                for hh in pair:
                    b, g = hh % 2, hh % G
                    dve.wait_ge(S["s_r1a"], pair_count(hh, 1, 2))
                    dve.wait_ge(S["s_gram"], hh + 1)
                    V.tensor_tensor(AT[b][:, :, :, :], gp[b][:, 0:512].rearrange("p (d t n) -> p d t n", d=2, t=TT), dec[b][:, :, :, :],
                                    ALU.mult).then_inc(S["s_AT"], 1)
                    V.tensor_tensor(qkT[:, g], over_dirs(gp[b][:, 512:768].rearrange("p (t n) -> p t n", t=TT)), dec[b][:, :, :, :],
                                    ALU.mult).then_inc(S["s_qks"], 1)
                    dve.wait_ge(S["s_AT"], hh + 1)
                    chain(V.tensor_tensor(PB[b][:, :, :].rearrange("p (d t) n -> p d t n", d=2), AT[b][:, :, :, :],
                                          level[:, :, 0, :].unsqueeze(2).to_broadcast([P, 2, TT, P]), ALU.mult))
                    V.tensor_tensor(TB[b][:, 1, :, :], ident[:, :].unsqueeze(1).to_broadcast([P, 4, P]), PB[b][:, :, :],
                                    ALU.subtract).then_inc(S["s_t1d"], 1)
                for hh in pair:
                    b, g = hh % 2, hh % G
                    dve.wait_ge(S["s_r1a"], pair_count(hh, 2, 2))
                    V.tensor_tensor(qgT[:, g], egr[b][:, :, :, :].rearrange("p d t n -> p d (t n)"), over_dirs(dnT[:, hh, :]),
                                    ALU.mult).then_inc(S["s_qg"], 1)
                    dve.wait_ge(S["s_tok"], hh + 1)
                    ktok = over_dirs(bank[2 * b + 1][:, 0:256].rearrange("p (t n) -> p t n", t=TT))
                    vtok = over_dirs(bank[2 * b + 1][:, 256:512].rearrange("p (t n) -> p t n", t=TT))
                    V.tensor_tensor(kbg[b][:, :, :, :], ktok, rows(bte, hh), ALU.mult)
                    V.tensor_tensor(kgt[:, g], ktok, rows(ekg, hh), ALU.mult)
                    V.tensor_tensor(vb[b][:, :, :, :], vtok, rows(bt, hh), ALU.mult).then_inc(S["s_tokd"], 1)
                for n in range(1, LEVELS):
                    for hh in pair:
                        b = hh % 2
                        dve.wait_ge(S["s_X"], pair_count(hh, n, LV))
                        if n == 1:
                            dve.wait_ge(S["s_t1"], hh + 1)
                        else:
                            dve.wait_ge(S["s_TB"], pair_count(hh, n - 1, LV))
                        half_ = slice(0, 2) if n < LV else slice(1, 2)
                        x = TB[b][:, half_, :, :].rearrange("p a q n -> p (a q n)")
                        V.tensor_tensor(x, x, gp[b][:, 512 * half_.start:1024], ALU.subtract).then_inc(S["s_TB"], 1)
                g, gr = hh % G, hh // G
                if g < G - 1:
                    continue
                for s in range(NCH):
                    step = NCH * gr + s
                    where = []
                    for d in range(2):
                        c = s if d == 0 else NCH - 1 - s
                        where.append((CHUNK * (c % 2), c // 2))
                    if s:
                        dve.wait_ge(S["s_ws"], 3 * gr + s)
                    else:
                        dve.wait_ge(S["s_uwc"], hh + 1)
                    if step:
                        dve.wait_ge(S["s_os"], step)
                    for d, (lo, tl) in enumerate(where):
                        u = uu[lo:lo + CHUNK, :, d, tl, :]
                        o = vn[lo:lo + CHUNK, :, :]
                        if s:
                            a = V.tensor_tensor(o, u, bank[0][lo:lo + CHUNK, :].rearrange("p (g n) -> p g n", g=G), ALU.subtract)
                        else:
                            a = V.tensor_copy(o, u)
                    a.then_inc(S["s_vn"], 1)
                    if s < NCH - 1:
                        dve.wait_ge(S["s_su"], 3 * gr + s + 1)
                        old, new = SS[(s + 1) % 2], SS[s % 2]
                        if s == 0:
                            a = V.tensor_copy(new[:, :, :, :].rearrange("p d g n -> p (d g n)"), gp[0][:, :])
                        else:
                            for d, (lo, tl) in enumerate(where):
                                for k in range(G):
                                    o = (d * G + k) * P
                                    a = V.scalar_tensor_tensor(new[:, d, k, :], old[:, d, k, :],
                                                               glast[:, lo // CHUNK, G * gr + k, d, tl:tl + 1], gp[0][:, o:o + P],
                                                               ALU.mult, ALU.add)
                        a.then_inc(S["s_S"], 1)
                        dve.wait_ge(S["s_S"], 3 * gr + s + 1)
                    if s >= 2:
                        dve.wait_ge(S["s_os"], step + 1)
                        dve.wait_ge(S["s_oc"], 2 * gr + 2)
                        for d, (lo, tl) in enumerate(where):
                            x = oacc[lo:lo + CHUNK, tl, G * gr:G * gr + G, :].rearrange("p g n -> p (g n)")
                            a = V.tensor_tensor(x, x, bank[1][lo:lo + CHUNK, :], ALU.add)
                        a.then_inc(S["s_od"], 1)
            dve.wait_ge(S["s_or"], 1)
            chain(V.tensor_reduce(st8[:, 0:16], osq[:, :, :, :].rearrange("p t h n -> p (t h) n"), AXX, ALU.add))
            V.tensor_scalar(st8[:, 0:16], st8[:, 0:16], 1.0 / HD, EPS, ALU.mult, ALU.add).then_inc(S["s_ord"], 1)
            dve.wait_ge(S["s_or"], 2)
            chain(V.reciprocal(st8[:, 16:32], st8[:, 16:32]))
            o16 = oacc[:, :, :, :].rearrange("p t h n -> p (t h) n")
            chain(V.tensor_tensor(o16, o16, st8[:, 16:32].unsqueeze(2).to_broadcast([P, 16, HD]), ALU.mult))
            chain(V.tensor_tensor(o16, o16, onorm[:, :].unsqueeze(1).to_broadcast([P, 16, HD]), ALU.mult))
            oflat = oacc[:, :, :, :].rearrange("p t h n -> p (t h n)")
            V.tensor_tensor(oflat, oflat, zs[:, :, :].rearrange("p t n -> p (t n)"), ALU.mult).then_inc(S["s_ord"], 1)
            turn_lo(TG["yb"], 4, a2h, a2l, 8)

            def to_mix(n, i, g, free):
                dve.wait_ge(s_gld[n], 16 * i + 16)
                V.tensor_tensor((mixa, mixb)[n][:, :], g[:, :], gld[:, n, :], ALU.mult).then_inc(free, 1)
                if n == 1:
                    wait_read_out(dve, PH["mix"], i, 0)
                    wait_read_out(dve, PH["mix"], i, 1)
                    V.tensor_tensor(mixb[:, :], mixb[:, :], mixa[:, :], ALU.add).then_inc(S["s_mixa"], 1)
                    dve.wait_ge(S["s_mixh"], i + 1)
                    sl = bass.ds(4 * i, 4)
                    V.tensor_tensor(a1l[:, sl, :], mixb[:, :].rearrange("p (m n) -> p m n", m=4), a1h[:, sl, :].bitcast(F32),
                                    ALU.subtract).then_inc(S["s_mixl"], 1)

            def to_residual(ph):
                def f(n, i, g, free):
                    x = h[:, :, bass.ds(ph.step * i + 512 * n, 512)] if ph.trips > 1 else h[:, :, 512 * n:512 * (n + 1)]
                    V.tensor_tensor(x, g[:, :].rearrange("p (t n) -> p t n", t=TT), x, ALU.add).then_inc(free, 1)
                return f
            gemm(PH["mix"], to_mix)
            dve.wait_ge(S["s_hx"], 16)
            gemm(PH["out"], to_residual(PH["out"]))
            norm_rows("mlp")
            turn_lo(TG["mlp"], 8, a1h, a1l, 0, 1)

            def to_hidden(count0):
                def f(n, i, g, free):
                    dve.wait_ge(S["s_ffh"], count0 + 2 * i + n + 1)
                    sl = bass.ds(8 * i + 4 * n, 4)
                    V.tensor_tensor(a2l[:, sl, :], ffq[:, :].rearrange("p (m n) -> p m n", m=4), a2h[:, sl, :].bitcast(F32),
                                    ALU.subtract).then_inc(S["s_ffl"], 1)
                return f
            for k in range(2):
                gemm(PH[f"up{k}"], to_hidden(8 * k), waits=False)
                gemm(PH[f"down{k}"], to_residual(PH[f"down{k}"]))
            dve.wait_ge(S["s_wrow"], 16)
            norm_rows("final", wrow[:, :])
            norm_rows("norm1")
            turn_lo(TG["norm1"], 8, a1h, a1l, 0, 2)

            for name in ("lr", "kv", "qa", "qkg", "vg", "gg"):
                gemm(PH[name], None)
            dve.wait_ge(S["s_qr"], 1)
            chain(V.tensor_reduce(st8[:, 0:16], rtmp[:, :, :].rearrange("p t (h n) -> p (t h) n", h=HEADS), AXX, ALU.add))
            chain(V.tensor_reduce(st8[:, 16:20].rearrange("p (t h) -> p t h", t=TT), rtmp2[:, :, 0:256].rearrange("p t (h n) -> p t h n", h=2), AXX, ALU.add))
            V.tensor_scalar(st8[:, 0:20], st8[:, 0:20], 1.0 / HD, EPS, ALU.mult, ALU.add).then_inc(S["s_qn"], 1)
            dve.wait_ge(S["s_qr"], 2)
            chain(V.reciprocal(st8[:, 32:52], st8[:, 32:52]))
            dve.wait_ge(S["s_const2"], 16 * NCONST2)
            for x, nh, c0, w in ((qa[:, :, :], HEADS, 32, 0), (kva[:, :, 0:256], 2, 48, 1)):
                x4 = x.rearrange("p t (h n) -> p t h n", h=nh)
                chain(V.tensor_tensor(x4, x4, st8[:, c0:c0 + 2 * nh].rearrange("p (t h) -> p t h", t=TT).unsqueeze(3).to_broadcast([P, TT, nh, HD]), ALU.mult))
                chain(V.tensor_tensor(x4, x4, gq_bc[:, w, :].unsqueeze(1).unsqueeze(1).to_broadcast([P, TT, nh, HD]), ALU.mult))
                x5 = x.rearrange("p t (h c n) -> p t h c n", h=nh, c=2)
                f1, f2 = (r[:, :, 0:nh * HD].rearrange("p t (h c n) -> p t h c n", h=nh, c=2) for r in (rtmp, rtmp2))
                cos, sin = (rope_cs[:, k].unsqueeze(2).to_broadcast([P, TT, nh, HD // 2]) for k in range(2))
                V.tensor_tensor(f1[:, :, :, 0], x5[:, :, :, 0], cos, ALU.mult)
                V.tensor_tensor(f2[:, :, :, 0], x5[:, :, :, 1], sin, ALU.mult)
                V.tensor_tensor(f1[:, :, :, 1], x5[:, :, :, 1], cos, ALU.mult)
                chain(V.tensor_tensor(f2[:, :, :, 1], x5[:, :, :, 0], sin, ALU.mult))
                V.tensor_tensor(x5[:, :, :, 0], f1[:, :, :, 0], f2[:, :, :, 0], ALU.subtract)
                chain(V.tensor_tensor(x5[:, :, :, 1], f1[:, :, :, 1], f2[:, :, :, 1], ALU.add))
            V.memset(st8[:, 63:64], 0.0).then_inc(S["s_roped"], 1)
            dve.wait_ge(S["s_bm"], 16)
            attention(HEADS, asc2, apr2, bmask[:, :, :], True)

            dve.wait_ge(S["s_al"], 2 * HEADS)
            for z in (aTm[:, :, :, :].rearrange("p h t n -> p (h t n)"),):
                chain(V.memset(z, 0.0))
            dve.wait_ge(S["s_gta"], 1)
            gflat = gtok[:, :, :, :].rearrange("p d t n -> p (d t n)")
            V.scalar_tensor_tensor(eb4[:, :], gflat, -1.0, gflat, ALU.mult, ALU.min).then_inc(S["s_gtd"], 1)
            dve.wait_ge(S["s_gta"], 2)
            V.scalar_tensor_tensor(gflat, gflat, 0.0, eb4[:, :], ALU.min, ALU.subtract).then_inc(S["s_gtd"], 1)
            qf, kf = (qkg[:, 4 * k:4 * k + 4, :].rearrange("p h n -> p (h n)") for k in range(2))

            def flat(x):
                return x[:, :, :].rearrange("p h n -> p (h n)")
            for d in range(2):
                ref = CHUNK // 2 if d == 0 else CHUNK - 1 - CHUNK // 2
                last = CHUNK - 1 if d == 0 else 0
                ebc = eb[:, :, :].rearrange("p h (c n) -> p (h c) n", n=CHUNK)
                dve.wait_ge(S["s_eb"], d + 1)
                if d:
                    dve.wait_ge(S["s_kop"], 1)
                for k, (x, at_) in enumerate(((eD, ref), (eE, last))):
                    V.tensor_tensor(x[:, :, :].rearrange("p h (c n) -> p (h c) n", n=CHUNK), ebc, ebc[:, :, at_:at_ + 1].to_broadcast([P, 16, CHUNK]),
                                    ALU.subtract).then_inc(S["s_bD"], 1)
                dve.wait_ge(S["s_ea"], 3 * d + 1)
                V.scalar_tensor_tensor(flat(qin), flat(qin), SCALE, qf, ALU.mult, ALU.mult).then_inc(S["s_bE"], 1)
                dve.wait_ge(S["s_ea"], 3 * d + 2)
                V.scalar_tensor_tensor(flat(qga), flat(qga), SCALE, qf, ALU.mult, ALU.mult)
                V.tensor_tensor(flat(kga), flat(kga), kf, ALU.mult).then_inc(S["s_bE"], 1)
                dve.wait_ge(S["s_ea"], 3 * d + 3)
                V.tensor_tensor(flat(kou), flat(kou), kf, ALU.mult).then_inc(S["s_bE"], 1)
                dve.wait_ge(S["s_aTp"], d + 1)
                if d:
                    dve.wait_ge(S["s_oin"], 1)
                    chain(V.memset(aTm[:, :, :, :].rearrange("p h t n -> p (h t n)"), 0.0))
                V.copy_predicated(aTm[:, :, :, :].rearrange("p h t n -> p (h t) n"),
                                  causal[:, d, :].bitcast(U32).unsqueeze(1).to_broadcast([P, 8, P]),
                                  gp[1][:, :].rearrange("p (q n) -> p q n", q=8)).then_inc(S["s_aTm"], 1)
                for s in range(NCH - 1):
                    c = s if d == 0 else NCH - 1 - s
                    dve.wait_ge(S["s_kv2"], 3 * d + s + 1)
                    if 3 * d + s >= 2:
                        dve.wait_ge(S["s_oi"], 3 * d + s - 1)
                    src = gp[s % 2]
                    new = S2[:, s % 2]
                    if s == 0:
                        a = V.tensor_copy(new.rearrange("p h n -> p (h n)"), src[:, :])
                    else:
                        for k in range(4):
                            a = V.scalar_tensor_tensor(new[:, k, :], S2[:, (s + 1) % 2, k, :], st8[:, 4 * k + c:4 * k + c + 1],
                                                       src[:, k * 256:(k + 1) * 256], ALU.mult, ALU.add)
                    a.then_inc(S["s_S2"], 1)
                    dve.wait_ge(S["s_S2"], 3 * d + s + 1)
            dve.wait_ge(S["s_or2"], 1)
            chain(V.tensor_reduce(st8[:, 0:8], oq2[:, :, :, :].rearrange("p t h n -> p (t h) n"), AXX, ALU.add))
            V.tensor_scalar(st8[:, 0:8], st8[:, 0:8], 1.0 / GLA_DV, EPS, ALU.mult, ALU.add).then_inc(S["s_or2d"], 1)
            dve.wait_ge(S["s_or2"], 2)
            chain(V.reciprocal(st8[:, 16:24], st8[:, 16:24]))
            o8 = oo2[:, :, :, :].rearrange("p t h n -> p (t h) n")
            chain(V.tensor_tensor(o8, o8, st8[:, 16:24].unsqueeze(2).to_broadcast([P, 8, GLA_DV]), ALU.mult))
            chain(V.tensor_tensor(o8, o8, gout_bc[:, :].unsqueeze(1).to_broadcast([P, 8, GLA_DV]), ALU.mult))
            o2f = oo2[:, :, :, :].rearrange("p t h n -> p (t h n)")
            V.tensor_tensor(o2f, o2f, gg2[:, :, :].rearrange("p t n -> p (t n)"), ALU.mult).then_inc(S["s_or2d"], 1)
            turn_lo(TG["cat"], 4, a2h, a2l, 8)
            gemm(PH["out2"], to_residual(PH["out2"]))
            norm_rows("norm2")
            turn_lo(TG["norm2"], 8, a1h, a1l, 0, 3)

            def hidden_lo(q, tile):
                dve.wait_ge(S["s_ffh"], 16 + q + 1)
                sl = span(tile, 4)
                V.tensor_tensor(a2l[:, sl, :], cg[:, 1, :].rearrange("p (m n) -> p m n", m=4), a2h[:, sl, :].bitcast(F32),
                                ALU.subtract).then_inc(S["s_ffl"], 1)

            def to_ff(ph, q0, after):
                def f(n, i, g, free):
                    q = i + q0
                    if n == 0 and after:
                        hidden_lo(q - 1, 4 * i)
                    wait_read_out(dve, ph, i, n)
                    for tap in (0, 2):
                        for m in range(4):
                            o = cg[:, n, m * SEQ:(m + 1) * SEQ]
                            a = V.scalar_tensor_tensor(o, upad[:, n, m, tap:tap + SEQ], cw2[:, tap, span(4 * q + 44 * n + m, 1)], o,
                                                       ALU.mult, ALU.add)
                        if tap == 0 or n == 1:
                            chain(a)
                    if n == 0:
                        a.then_inc(S["s_cv2"], 1)
                        return
                    dve.wait_ge(S["s_sil"], q + 1)
                    V.tensor_tensor(cg[:, 1, :], cg[:, 1, :], cg[:, 0, :], ALU.mult).then_inc(S["s_prod"], 1)
                return f
            V.memset(upad[:, :, :, 0:1], 0.0)
            V.memset(upad[:, :, :, 1 + SEQ:2 + SEQ], 0.0).then_inc(S["s_set"], 1)
            for g, (q0, q1) in enumerate(((0, 6), (6, 11))):
                gemm(PH[f"ffa{g}"], to_ff(PH[f"ffa{g}"], q0, False), 3, waits=False)
                gemm(PH[f"ff{g}"], to_ff(PH[f"ff{g}"], q0 + 1, True), 3, waits=False)
                hidden_lo(q1 - 1, 4 * (q1 - q0 - 1))
                gemm(PH[f"dd{g}"], to_residual(PH[f"dd{g}"]))

        @block.tensor
        def _(pe):
            def gemm(ph, ready=(), ready_last=None):
                for s, v in ready:
                    pe.wait_ge(s, v)
                ah, al = acts[ph.act]
                with Loop(pe, ph.trips) as i:
                    for ch in ph.body:
                        g = gp[ch.c % 2]
                        if ch.c >= 2:
                            pe.wait_ge(s_free[ch.c % 2], ch.c // 2 + i * (ph.nc // 2))
                        kts = BLK_KT if ch.n == BLK_N else KT
                        for j in range(ch.blocks):
                            idx = ch.b + j
                            sl = idx % HL_SLOTS
                            pe.wait_ge(s_hi, idx + 1 + i * ph.nb)
                            pe.wait_ge(s_lo, idx + 1 + i * ph.nb)
                            if ready_last is not None and ch is ph.body[0] and j == ch.blocks - 4 // BLK_KT:
                                pe.wait_ge(*ready_last)
                            for k in range(kts):
                                kt = ch.kt0 + j * BLK_KT + k
                                first, last = j == 0 and k == 0, j == ch.blocks - 1 and k == kts - 1
                                if ch.n == BLK_N:
                                    hi, lo = wh[:, sl, k, :], wl[:, sl, k, :]
                                else:
                                    hi, lo = (w[:, sl, 0, k * ch.n:(k + 1) * ch.n] for w in (wh, wl))
                                if ch.kind == "up":
                                    for m in range((ch.n + P - 1) // P):
                                        cols = slice(m * P, min((m + 1) * P, ch.n))
                                        rows = min(P, ch.n)
                                        for q, (a, b) in enumerate(((hi, ah), (hi, al), (lo, ah))):
                                            mm = pe.matmul(g[0:rows, m * SEQ:(m + 1) * SEQ], a[:, cols], b[:, kt, :],
                                                           start=first and q == 0 and m % 2 == 0, stop=last and q == 2,
                                                           skip_group_check=True)
                                else:
                                    for tt in range(TT):
                                        rows = slice(tt * P, (tt + 1) * P)
                                        for q, (a, b) in enumerate(((ah, hi), (ah, lo), (al, hi))):
                                            mm = pe.matmul(g[:, tt * 512:tt * 512 + ch.n], a[:, kt, rows], b,
                                                           start=first and q == 0, stop=last and q == 2,
                                                           skip_group_check=True)
                            mm.then_inc(s_blk, 1)

            def turn(base, groups, src, after):
                pe.wait_ge(*after)
                for g in range(groups):
                    if g >= 4:
                        pe.wait_ge(S["s_trl"], base + g - 3)
                    for m in range(2):
                        for tt in range(TT):
                            mm = pe.transpose(bank[g % 4][:, m * SEQ + tt * P:m * SEQ + (tt + 1) * P], src(2 * g + m, tt), ident[:, :])
                    mm.then_inc(S["s_tr"], 1)

            def products_out(ph):
                wait_read_out(pe, ph, ph.trips - 1, ph.nc - 2)
                wait_read_out(pe, ph, ph.trips - 1, ph.nc - 1)

            def attention(base, q, k, v, position=None):
                def scores(hh):
                    if hh >= 2:
                        pe.wait_ge(S["s_sc"], base + hh - 1)
                    for tt in range(TT):
                        o = bank[hh % 2][:, tt * SEQ:(tt + 1) * SEQ]
                        mm = pe.matmul(o, q(hh)[:, tt * P:(tt + 1) * P], k(hh), start=True, stop=position is None)
                        if position is not None:
                            mm = pe.matmul(o, flip[:, :], position[:, hh, tt, :], start=False, stop=True)
                    mm.then_inc(S["s_qk"], 1)
                scores(0)
                for hh in range(HEADS):
                    if hh + 1 < HEADS:
                        scores(hh + 1)
                    pe.wait_ge(S["s_p"], base + hh + 1)
                    if hh >= 2:
                        pe.wait_ge(S["s_pT"], base + hh - 1)
                    for kt in range(TT):
                        for tt in range(TT):
                            mm = pe.transpose(bank[2 + hh % 2][:, kt * SEQ + tt * P:kt * SEQ + (tt + 1) * P],
                                              probs_[base][:, hh % 2, tt, kt * P:(kt + 1) * P], ident[:, :])
                    mm.then_inc(S["s_pt"], 1)
                    pe.wait_ge(S["s_pT"], base + hh + 1)
                    if hh >= 2:
                        pe.wait_ge(S["s_al"], base + hh - 1)
                    for kt in range(TT):
                        mm = pe.matmul(gp[0][:, (hh % 2) * 512:(hh % 2) * 512 + SEQ], v(hh, kt), probsT_[base][:, hh % 2, kt, :],
                                       start=kt == 0, stop=kt == TT - 1)
                    mm.then_inc(S["s_o"], 1)
            probs_ = {0: apr, HEADS: apr2}
            probsT_ = {0: apT, HEADS: apT2}

            pe.wait_ge(S["s_const"], 16 * NCONST)
            pe.wait_ge(S["s_set"], 1)
            turn(TG["mix"], 8, lambda kt, tt: xs[:, tt, kt * P:(kt + 1) * P], (S["s_xs"], 1))
            gemm(PH["ba"], [(S["s_trl"], TG["mix"] + 8)])
            for name in ("lead", "v", "qk", "dn0", "dn", "z", "gates0", "gates"):
                gemm(PH[name])
            products_out(PH["gates"])
            pe.wait_ge(S["s_bias"], 16 * (4 * HEADS + 1))
            attention(0, lambda hh: attqk[:, hh, :], lambda hh: attqk[:, 8 + hh, :], lambda hh, kt: attv[:, kt, hh * P:(hh + 1) * P], bias)

            bt, gg = sc32["bt"], sc32["gg"]
            pe.wait_ge(S["s_gate"], 2)
            pe.wait_ge(S["s_bag"], 2)
            pe.wait_ge(S["s_sc"], HEADS)
            for d in range(2):
                pe.matmul(bank[0][:, d * 16:(d + 1) * 16], tri[:, d, :], gg[:, :, d, :], start=True, stop=True)
            pe.matmul(bank[1][:, 0:32], blockm[:, :], gg[:, :, :, :].rearrange("p h d t -> p (h d t)"), start=True, stop=True)
            pe.matmul(bank[1][:, 64:128], ones[:, :], ghalf[:, :, :, :, :].rearrange("p a h d t -> p (a h d t)"), start=True, stop=True).then_inc(S["s_gcm"], 1)
            pe.wait_ge(S["s_pT"], HEADS)
            for j in range(8):
                pe.wait_ge(S["s_lsq"], j + 1)
                if j >= 2:
                    pe.wait_ge(S["s_lrt"], j - 1)
                pe.matmul(bank[2 + j % 2][:, :], ones[:, :], sqb[:, j % 2, :], start=True, stop=True).then_inc(S["s_lsum"], 1)
            pe.wait_ge(S["s_bag"], 3)
            pe.wait_ge(S["s_gcols"], 1)
            pe.wait_ge(S["s_lfree"], 8)
            pe.wait_ge(S["s_al"], HEADS)
            for h0 in range(0, HEADS, 2):
                pair = (h0, h0 + 1)
                if h0 == G:
                    pe.wait_ge(S["s_od"], 2)
                for hh in pair:
                    b = hh % 2
                    if hh >= 2:
                        pe.wait_ge(S["s_Pc"], pair_count(hh - 2, LV, LV))
                        pe.wait_ge(S["s_tokd"], hh - 1)
                    for d in range(2):
                        for tt in range(TT):
                            q = d * 2 + tt
                            pe.matmul(bank[2 * b][:, q * P:(q + 1) * P], gg[:, hh, d, tt:tt + 1].to_broadcast([P, P]), tri[:, d, :],
                                      start=True, stop=True)
                            mm = pe.matmul(bank[2 * b + 1][:, q * P:(q + 1) * P], bt[:, hh, d, tt:tt + 1].to_broadcast([P, P]), ident[:, :],
                                           start=True, stop=True)
                    mm.then_inc(S["s_r1"], 1)
                for hh in pair:
                    b = hh % 2
                    qT, kT, vT = dnT[:, hh, :], dnT[:, 8 + hh, :], dnT[:, 16 + hh, :]
                    pe.wait_ge(S["s_kb"], hh + 1)
                    if hh >= 2:
                        pe.wait_ge(S["s_uwc"], hh - 1)
                    for tt in range(TT):
                        c = slice(tt * P, (tt + 1) * P)
                        for d in range(2):
                            q = d * 2 + tt
                            pe.matmul(gp[b][:, q * P:(q + 1) * P], kT[:, c], kbT[b][:, d, c], start=True, stop=True)
                        mm = pe.matmul(gp[b][:, 512 + tt * P:512 + (tt + 1) * P], kT[:, c], qT[:, c], start=True, stop=True)
                    mm.then_inc(S["s_gram"], 1)
                    for tt in range(TT):
                        c = slice(tt * P, (tt + 1) * P)
                        pe.transpose(bank[2 * b + 1][:, c], kT[:, c], ident[:, :])
                        mm = pe.transpose(bank[2 * b + 1][:, 256 + tt * P:256 + (tt + 1) * P], vT[:, c], ident[:, :])
                    mm.then_inc(S["s_tok"], 1)
                for hh in pair:
                    b = hh % 2
                    pe.wait_ge(S["s_t1d"], hh + 1)
                    pe.wait_ge(S["s_r1a"], pair_count(hh, 2, 2))
                    for q in range(4):
                        mm = pe.transpose(bank[2 * b][:, q * P:(q + 1) * P], TB[b][:, 1, q, :], ident[:, :])
                    mm.then_inc(S["s_t1p"], 1)
                for n in range(1, LEVELS):
                    for hh in pair:
                        b = hh % 2
                        pe.wait_ge(S["s_ATl"], pair_count(hh, n, LV))
                        if n == 1:
                            pe.wait_ge(S["s_t1"], hh + 1)
                        else:
                            pe.wait_ge(S["s_TB"], pair_count(hh, n - 1, LV))
                        for q in range(4):
                            mm = pe.matmul(bank[2 * b][:, q * P:(q + 1) * P], ATl[b][:, q // 2, q % 2, n - 1, :], TB[b][:, 0, q, :],
                                           start=True, stop=True)
                        mm.then_inc(S["s_P"], 1)
                    for hh in pair:
                        b = hh % 2
                        pe.wait_ge(S["s_Pc"], pair_count(hh, n, LV))
                        if n == 1:
                            pe.wait_ge(S["s_qks"], hh + 1)
                        for q in range(4):
                            if n < LV:
                                pe.matmul(gp[b][:, q * P:(q + 1) * P], TB[b][:, 1, q, :], PB[b][:, q, :], start=True, stop=True)
                            mm = pe.matmul(gp[b][:, 512 + q * P:512 + (q + 1) * P], PB[b][:, q, :], TB[b][:, 1, q, :], start=True, stop=True)
                        mm.then_inc(S["s_X"], 1)
                for hh in pair:
                    b = hh % 2
                    pe.wait_ge(S["s_TB"], pair_count(hh, LV, LV))
                    pe.wait_ge(S["s_tokd"], hh + 1)
                    for q in range(4):
                        pe.matmul(gp[b][:, q * P:(q + 1) * P], TB[b][:, 1, q, :], vb[b][:, q // 2, q % 2, :], start=True, stop=True)
                        mm = pe.matmul(gp[b][:, 512 + q * P:512 + (q + 1) * P], kbg[b][:, q // 2, q % 2, :], TB[b][:, 1, q, :],
                                       start=True, stop=True)
                    mm.then_inc(S["s_uw"], 1)
                g, gr = hh % G, hh // G
                if g < G - 1:
                    continue
                pe.wait_ge(S["s_uwc"], hh + 1)
                pe.wait_ge(S["s_qg"], hh + 1)
                for s in range(NCH):
                    step = NCH * gr + s
                    where = []
                    for d in range(2):
                        c = s if d == 0 else NCH - 1 - s
                        where.append((CHUNK * (c % 2), c // 2))
                    if s:
                        pe.wait_ge(S["s_S"], 3 * gr + s)
                        for d, (lo, tl) in enumerate(where):
                            for k in range(G):
                                mm = pe.matmul(bank[0][lo:lo + CHUNK, k * P:(k + 1) * P], wTs[:, k, d, tl, lo:lo + CHUNK], SS[(s - 1) % 2][:, d, k, :],
                                               start=True, stop=True)
                        mm.then_inc(S["s_ws"], 1)
                    pe.wait_ge(S["s_vn"], step + 1)
                    if s < NCH - 1:
                        for d, (lo, tl) in enumerate(where):
                            for k in range(G):
                                o = (d * G + k) * P
                                mm = pe.matmul(gp[0][:, o:o + P], kgt[lo:lo + CHUNK, k, d, tl, :], vn[lo:lo + CHUNK, k, :], start=True, stop=True)
                        mm.then_inc(S["s_su"], 1)
                    if s in (1, 2):
                        pe.wait_ge(S["s_oc"], 2 * gr + s)
                    elif s == 3:
                        pe.wait_ge(S["s_od"], 2 * gr + 1)
                    for d, (lo, tl) in enumerate(where):
                        rows = slice(lo, lo + CHUNK)
                        for k in range(G):
                            o = bank[1][rows, k * P:(k + 1) * P]
                            if s:
                                pe.matmul(o, qgT[:, k, d, tl * P + lo:tl * P + lo + CHUNK], SS[(s - 1) % 2][:, d, k, :], start=True, stop=False)
                            mm = pe.matmul(o, qkT[rows, k, d, tl, lo:lo + CHUNK], vn[rows, k, :], start=s == 0, stop=True)
                    mm.then_inc(S["s_os"], 1)
            turn(TG["yb"], 4, lambda kt, tt: oacc[:, tt, kt, :], (S["s_ord"], 2))
            gemm(PH["mix"], [(S["s_trl"], TG["yb"] + 4)])
            gemm(PH["out"], [(S["s_mixl"], 3)], (S["s_mixl"], 4))
            turn(TG["mlp"], 8, lambda kt, tt: xs[:, tt, kt * P:(kt + 1) * P], (S["s_xs"], 2))
            gemm(PH["up0"], [(S["s_trl"], TG["mlp"] + 8)])
            gemm(PH["down0"], [(S["s_ffl"], 7)], (S["s_ffl"], 8))
            gemm(PH["up1"])
            gemm(PH["down1"], [(S["s_ffl"], 15)], (S["s_ffl"], 16))
            turn(TG["norm1"], 8, lambda kt, tt: xs[:, tt, kt * P:(kt + 1) * P], (S["s_xs"], 3))
            gemm(PH["lr"], [(S["s_trl"], TG["norm1"] + 8)])
            for name in ("kv", "qa", "qkg", "vg", "gg"):
                gemm(PH[name])
            products_out(PH["gg"])
            pe.wait_ge(S["s_roped"], 1)
            for g in range(5):
                if g == 4:
                    pe.wait_ge(S["s_q2c"], 1)
                for m in range(2):
                    for tt in range(TT):
                        hd = 2 * g + m
                        src = qa[:, tt, hd * P:(hd + 1) * P] if g < 4 else kva[:, tt, m * P:(m + 1) * P]
                        mm = pe.transpose(bank[g % 4][:, m * SEQ + tt * P:m * SEQ + (tt + 1) * P], src, ident[:, :])
                mm.then_inc(S["s_q2T"], 1)
            pe.wait_ge(S["s_q2c"], 5)
            attention(HEADS, lambda hh: qT2[:, hh, :], lambda hh: qT2[:, 8 + hh // 4, :],
                      lambda hh, kt: kva[:, kt, 256 + (hh // 4) * P:256 + (hh // 4 + 1) * P])
            pe.wait_ge(S["s_al"], 2 * HEADS)
            pe.wait_ge(S["s_wa"], 1)
            for q in range(4):
                d, tt = q // 2, q % 2
                pe.matmul(bank[q][:, :], lrT[0:33, tt * P:(tt + 1) * P], wa2[0:33, d, :], start=True, stop=True).then_inc(S["s_gt"], 1)
            pe.wait_ge(S["s_gtd"], 2)
            for d in range(2):
                if d:
                    pe.wait_ge(S["s_S2"], 3)
                for hh in range(4):
                    for tt in range(TT):
                        mm = pe.matmul(gp[0][:, hh * SEQ + tt * P:hh * SEQ + (tt + 1) * P], gtok[:, d, tt, hh * P:(hh + 1) * P], tri[:, d, :],
                                       start=True, stop=True)
                mm.then_inc(S["s_bc"], 1)
                pe.wait_ge(S["s_bE"], 3 * d + 2)
                for hh in range(4):
                    for tt in range(TT):
                        c = slice(tt * P, (tt + 1) * P)
                        mm = pe.matmul(gp[1][:, (hh * 2 + tt) * P:(hh * 2 + tt + 1) * P], kga[:, hh, c], qga[:, hh, c], start=True, stop=True)
                mm.then_inc(S["s_aTp"], 1)
                pe.wait_ge(S["s_bE"], 3 * d + 3)
                pe.wait_ge(S["s_eb"], d + 1)
                for hh in range(4):
                    for tt in range(TT):
                        mm = pe.transpose(gp[0][:, (hh * 2 + tt) * P:(hh * 2 + tt + 1) * P], kou[:, hh, tt * P:(tt + 1) * P], ident[:, :])
                mm.then_inc(S["s_kop"], 1)
                pe.wait_ge(S["s_aTm"], d + 1)
                for tt in range(TT):
                    for hh in range(4):
                        mm = pe.matmul(bank[2 * tt + hh // 2][:, (hh % 2) * 256:(hh % 2 + 1) * 256], aTm[:, hh, tt, :],
                                       vg[:, tt, hh * 256:(hh + 1) * 256], start=d == 0 and hh % 2 == 0, stop=False, skip_group_check=True)
                pe.wait_ge(S["s_koc"], d + 1)
                for s in range(NCH):
                    c = s if d == 0 else NCH - 1 - s
                    lo, tl = CHUNK * (c % 2), c // 2
                    rows = slice(lo, lo + CHUNK)
                    if s < NCH - 1:
                        if s >= 2:
                            pe.wait_ge(S["s_S2"], 3 * d + s - 1)
                        for hh in range(4):
                            mm = pe.matmul(gp[s % 2][:, hh * 256:(hh + 1) * 256], kot[rows, hh, tl, :], vg[rows, tl, hh * 256:(hh + 1) * 256],
                                           start=True, stop=True)
                        mm.then_inc(S["s_kv2"], 1)
                    if s:
                        pe.wait_ge(S["s_S2"], 3 * d + s)
                        for hh in range(4):
                            mm = pe.matmul(bank[2 * tl + hh // 2][rows, (hh % 2) * 256:(hh % 2 + 1) * 256], qin[:, hh, c * CHUNK:(c + 1) * CHUNK],
                                           S2[:, (s - 1) % 2, hh, :], start=False, stop=d == 1 and s == NCH - 1, skip_group_check=True)
                        if s < NCH - 1:
                            mm.then_inc(S["s_oi"], 1)
                        else:
                            mm.then_inc(S["s_oin"], 1)
            turn(TG["cat"], 4, lambda kt, tt: oo2[:, tt, kt // 2, (kt % 2) * P:(kt % 2 + 1) * P], (S["s_or2d"], 2))
            gemm(PH["out2"], [(S["s_trl"], TG["cat"] + 4)])
            turn(TG["norm2"], 8, lambda kt, tt: xs[:, tt, kt * P:(kt + 1) * P], (S["s_xs"], 4))
            gemm(PH["ffa0"], [(S["s_trl"], TG["norm2"] + 8)])
            gemm(PH["ff0"])
            gemm(PH["dd0"], [(S["s_ffl"], 16 + 5)], (S["s_ffl"], 16 + 6))
            gemm(PH["ffa1"])
            gemm(PH["ff1"])
            gemm(PH["dd1"], [(S["s_ffl"], 16 + 10)], (S["s_ffl"], 16 + 11))

        @block.gpsimd
        def _(pool):
            G_ = nc.gpsimd

            def load(dst, src, s, slow=False):
                pool.dma_start(dst, src).then_inc(s, 16)

            for dst, name in ((ident[:, :], "ident"), (tri[:, :, :], "tri"), (blockm[:, :], "block"), (neg[:, :, :], "neg"),
                              (half[:, :], "half"), (level[:, :, :, :], "level")):
                load(dst, t[name], S["s_const"])
            with nc.allow_non_contiguous_dma(reason="small per-feature tables"):
                for k, name in enumerate(("norm_mix_w", "norm_mlp_w")):
                    load(normw[:, k, :], t[name].rearrange("(k p) -> p k", p=P), S["s_const"])
                for k, name in enumerate(("norm1_g_2", "norm2_g_2")):
                    load(normw[:, 2 + k, :], t[name][0].rearrange("(k p) -> p k", p=P), S["s_const"])
                for tap in range(5):
                    load(cw1[:, tap, :], t["conv_w"][tap].rearrange("(k p) -> p k", p=P), S["s_const"])
                load(dtal[:, 0, :], t["dt_bias"].rearrange("d h -> (d h)").partition_broadcast(P), S["s_const"])
                load(dtal[:, 1, :], t["a_log"].rearrange("d h -> (d h)").partition_broadcast(P), S["s_const"])
                load(onorm[:, :], t["onorm_w"].partition_broadcast(P), S["s_const"])
            pool.wait_ge(S["s_cvo"], 6)
            load(wmask[:, :], t["window"], S["s_wm"])
            load(flip[:, :], t["flip"], S["s_bias"])
            for hh in range(HEADS):
                for row in range(SEQ // GRID_W):
                    lo, tl = GRID_W * (row % 2), row // 2
                    first = hh * 15 * 31 + (7 - row) * 31 + 15 - (GRID_W - 1)
                    src = bass.AP(t["rpb"].tensor, first, [[1, GRID_W], [31, SEQ // GRID_W], [1, GRID_W]])
                    load(bias[lo:lo + GRID_W, hh, tl, :].rearrange("p (r c) -> p r c", c=GRID_W), src, S["s_bias"])
            for ph, row in ((PH["gates0"], 0), (PH["gates"], 2)):
                with Loop(pool, ph.trips) as i:
                    for n in range(2):
                        wait_read_out(pool, ph, i, n)
                        dst = gates_dram[bass.ds(2 * i + row + n, 1)] if ph.trips > 1 else gates_dram[row + n:row + n + 1]
                        load(dst.rearrange("o p n -> p (o n)"), gstage[:, n, :], s_gst[n])
            for h0 in range(0, HEADS, 2):
                for n in range(1, LEVELS):
                    for hh in (h0, h0 + 1):
                        if n == 1:
                            pool.wait_ge(S["s_AT"], hh + 1)
                            if hh >= 2:
                                pool.wait_ge(S["s_P"], pair_count(hh - 2, LV, LV))
                        G_.tensor_tensor(ATl[hh % 2][:, :, :, n - 1, :], AT[hh % 2][:, :, :, :],
                                         level[:, :, n, :].unsqueeze(2).to_broadcast([P, 2, TT, P]), ALU.mult).then_inc(S["s_ATl"], 1)
            pool.wait_ge(S["s_trl"], TG["yb"] + 4)
            load(h[:, :, :], t["x"][0].rearrange("(t p) n -> p t n", p=P), S["s_hx"])
            ph = PH["mix"]
            for n in range(2):
                pool.wait_ge(s_gst[n], 16 * 4)
            for n in range(2):
                load(gld[:, n, :], gates_dram[4 * n], s_gld[n])
            for i in range(1, 4):
                for n in range(2):
                    wait_read_out(pool, ph, i - 1, n)
                    load(gld[:, n, :], gates_dram[4 * n + i], s_gld[n])
            load(causal[:, :, :], t["causal"].rearrange("p (d n) -> p d n", d=2), S["s_const2"])
            for k, name in enumerate(("cos", "sin")):
                load(rope_cs[:, k], t[name].rearrange("p (t n) -> p t n", t=TT), S["s_const2"])
            with nc.allow_non_contiguous_dma(reason="small per-feature tables"):
                for tap in range(3):
                    load(cw2[:, tap, :], t["conv_w_2"][0, tap].rearrange("(k p) -> p k", p=P), S["s_const2"])
                load(cb2[:, :], t["conv_b_2"][0].rearrange("(k p) -> p k", p=P), S["s_const2"])
                load(gq_bc[:, 0, :], t["attn_q_norm_g_2"][0].partition_broadcast(P), S["s_const2"])
                load(gq_bc[:, 1, :], t["attn_k_norm_g_2"][0].partition_broadcast(P), S["s_const2"])
                load(gout_bc[:, :], t["gla_out_norm_g_2"][0].partition_broadcast(P), S["s_const2"])
                load(sink_bc[:, :], t["attn_sink_2"][0].partition_broadcast(P), S["s_const2"])
            pool.wait_ge(s_blk, last_block(PH["down1"]))
            load(wrow[:, :], t["norm_final_w"].partition_broadcast(P), S["s_wrow"])
            wait_read_out(pool, PH["lr"], 0, 0)
            G_.memset(lrT[32:33, :], 1.0)
            G_.memset(wa2[0:32, :, :], 0.0).then_inc(S["s_waz"], 1)
            pool.wait_ge(S["s_waz"], 1)
            for d, s in enumerate(("fwd", "bwd")):
                load(wa2[16 * d:16 * d + 16, d, :], t[f"gla_wa2_{s}_2"][0], S["s_wal"])
                load(wa2[32:33, d, :], t[f"gla_ba_{s}_2"], S["s_wal"])
            pool.wait_ge(S["s_wal"], 64)
            G_.memset(pdum[:, 0:1], 0.0).then_inc(S["s_wa"], 1)
            pool.wait_ge(s_blk, last_block(PH["gg"]))
            load(bmask[:, :, :], t["band"].rearrange("p (t k) -> p t k", t=TT), S["s_bm"])


_INS = ['x', 'norm_mix_w', 'w_in', 'conv_w', 'a_log', 'dt_bias', 'onorm_w', 'rpb', 'w_proj_a', 'w_proj_b', 'w_out',
        'norm_mlp_w', 'w_mlp_up', 'w_mlp_down', 'norm_final_w', 'norm1_g_2', 'w_in_2', 'attn_q_norm_g_2',
        'attn_k_norm_g_2', 'attn_sink_2', 'gla_wa2_fwd_2', 'gla_ba_fwd_2', 'gla_wa2_bwd_2', 'gla_ba_bwd_2',
        'gla_out_norm_g_2', 'w_out_2', 'norm2_g_2', 'w_up_2', 'conv_w_2', 'conv_b_2', 'w_down_2']
_SQUEEZED = ('w_in_2', 'w_out_2', 'w_up_2', 'w_down_2')


def program(nc, shapes):
    t = {}
    for name, (shape, dtype) in shapes.items():
        ap = nc.dram_tensor(f"in_{name}", shape, dtype, kind="ExternalInput").ap()
        t[name] = ap[0] if name in _SQUEEZED else ap
    t["out"] = nc.dram_tensor("out_0", (1, SEQ, D), F32, kind="ExternalOutput").ap()
    return t


def kernel(**inputs):
    import concourse.bacc as _bacc
    from concourse.bass_utils import run_bass_kernel_spmd as _run

    nc = _bacc.Bacc("TRN2", target_bir_lowering=False, num_devices=1)
    arrays = {n: np.ascontiguousarray(inputs[n]) for n in _INS}
    arrays.update(constants())
    t = program(nc, {n: (a.shape, mybir.dt.from_np(a.dtype)) for n, a in arrays.items()})
    build(nc, t)
    r = _run(nc, [{f"in_{n}": a for n, a in arrays.items()}], core_ids=[0])
    return r.results[0]["out_0"]
```

```python
from contextlib import ExitStack

import numpy as np
import concourse.bass as bass
from concourse import mybir

ALU = mybir.AluOpType
ACT = mybir.ActivationFunctionType
F32 = mybir.dt.float32
F32R = mybir.dt.float32r
U32 = mybir.dt.uint32
AXX = mybir.AxisListType.X

P = 128
SEQ = 256
TT = SEQ // P
D = 2048
KT = D // P
DFF = 4 * D
DFF2 = 5632
HEADS = 8
HD = 128
CHUNK = 64
NCH = SEQ // CHUNK
GRID_W, WIN_C = 64, 16
GLA_H, GLA_DV = 4, 256
LEVELS = 6
EPS = 1e-6
NEG = -1e30
SCALE = float(HD) ** -0.5
BLK_KT = 2
BLK_N = 512
RAW_SLOTS = 8
HL_SLOTS = 4

C_QK, C_V, C_DN, C_Z, C_BA, C_GATES = 0, 2048, 3072, 6144, 7168, 7200
D_QA, D_KV, D_QKG, D_VG, D_GG, D_LR = 0, 1024, 1536, 2560, 3584, 4608


def constants():
    p = np.arange(P)
    j, i = p[:, None], p[None, :]
    same = (j // CHUNK) == (i // CHUNK)
    fwd, bwd = same & (j <= i), same & (j >= i)
    out = {"ident": np.eye(P), "tri": np.stack([fwd, bwd], 1), "block": same,
           "neg": np.stack([np.where(m, 0, NEG) for m in (fwd, bwd)], 1),
           "half": np.stack([p < CHUNK, p >= CHUNK], 1)}
    level = np.zeros((P, 2, LEVELS, P))
    for n in range(LEVELS):
        s = 1 << n
        pair = (j // (2 * s)) == (i // (2 * s))
        level[:, 0, n] = pair & (j // s < i // s)
        level[:, 1, n] = pair & (j // s > i // s)
    out["level"] = level
    out["causal"] = np.stack([fwd, same & (j > i)], 1)
    out["flip"] = (same & (j % GRID_W + i % GRID_W == GRID_W - 1)) / SCALE
    cs, kc = np.clip(j % GRID_W - WIN_C // 2, 0, GRID_W - WIN_C), np.arange(GRID_W)
    out["window"] = np.where((kc >= cs) & (kc < cs + WIN_C), 0, NEG)
    q = p[:, None] + P * np.arange(TT)[None, :]
    k = np.arange(SEQ)
    out["band"] = np.where(np.abs(k - q[..., None]) <= P, 0, NEG)
    half = HD // 2
    inv = (1.0 / (np.float32(10000.0) ** (np.arange(half, dtype=np.float32) / np.float32(half)))).astype(np.float32)
    ang = q.astype(np.float32)[..., None] * inv
    out["cos"], out["sin"] = np.cos(ang), np.sin(ang)
    return {n: np.ascontiguousarray(a, dtype=np.float32).reshape(P, -1) for n, a in out.items()}


CONST_SHAPES = {"ident": (P,), "tri": (2, P), "block": (P,), "neg": (2, P), "half": (2,), "level": (2, LEVELS, P),
                "causal": (2, P), "window": (GRID_W,), "band": (TT, SEQ), "cos": (TT, HD // 2),
                "sin": (TT, HD // 2)}


def span(first, n):
    return slice(first, first + n) if isinstance(first, int) else bass.ds(first, n)


class Chunk:
    def __init__(self, w, row, col, blocks, kind, kt0=0, n=BLK_N):
        self.w, self.row, self.col, self.blocks, self.kind, self.kt0, self.n = w, row, col, blocks, kind, kt0, n


class Phase:
    def __init__(self, body, trips, step, act):
        self.body, self.trips, self.step, self.act = body, trips, step, act
        self.nb = sum(c.blocks for c in body)
        self.nc = len(body)


def number(phases):
    b = c = 0
    for ph in phases:
        ph.b0, ph.c0 = b, c
        for ch in ph.body:
            ch.b, ch.c = b, c
            b += ch.blocks
            c += 1
        b = ph.b0 + ph.nb * ph.trips
        c = ph.c0 + ph.nc * ph.trips
        assert ph.trips == 1 or (ph.nb % RAW_SLOTS == 0 and ph.nc % 2 == 0)
    return b


class Chain:
    def __init__(self, eng, sem):
        self.eng, self.sem, self.n, self.reg = eng, sem, 0, 0

    def __call__(self, ins):
        ins.then_inc(self.sem, 1)
        self.n += 1
        self.eng.wait_ge(self.sem, self.reg + self.n)
        return ins


class Loop:
    def __init__(self, eng, trips, chain=None, per=0):
        self.eng, self.trips, self.chain, self.per = eng, trips, chain, per

    def __enter__(self):
        if self.chain is not None:
            self.n0 = self.chain.n
        if self.trips == 1:
            return 0
        self.ctx = self.eng.Fori(0, self.trips)
        i = self.ctx.__enter__()
        if self.chain is not None:
            self.chain.reg = i * self.per
        return i

    def __exit__(self, *e):
        if self.trips > 1:
            self.ctx.__exit__(*e)
        if self.chain is not None and e[0] is None:
            if self.trips > 1:
                assert self.chain.n - self.n0 == self.per, (self.chain.n - self.n0, self.per)
                self.chain.n = self.n0 + self.per * self.trips
            self.chain.reg = 0


def build(nc, t):
    ctx = ExitStack()
    with ctx:
        def sem(name):
            return ctx.enter_context(nc.semaphore(name))

        BASE = 16512
        RAW0 = BASE
        SLOT = BLK_KT * BLK_N * 4
        WH0 = RAW0 + RAW_SLOTS * SLOT
        WL0 = WH0 + HL_SLOTS * SLOT
        A0 = WL0 + HL_SLOTS * SLOT
        R0 = A0 + 32768
        H0 = R0 + 65536
        T0 = H0 + 16384
        K = 1024

        def at(name, shape, off, dt=F32):
            return nc.alloc_sbuf_tensor_at(name, [P] + list(shape), dt, offset=off)

        raw = at("raw", [RAW_SLOTS, BLK_KT, BLK_N], RAW0)
        wh = at("wh", [HL_SLOTS, BLK_KT, BLK_N], WH0, F32R)
        wl = at("wl", [HL_SLOTS, BLK_KT, BLK_N], WL0, F32R)
        a1h = at("a1h", [KT, SEQ], A0, F32R)
        a1l = at("a1l", [KT, SEQ], A0 + 16 * K, F32R)
        a2h = at("a2h", [32, SEQ], R0, F32R)
        a2l = at("a2l", [32, SEQ], R0 + 32 * K, F32R)
        h = at("h", [TT, D], H0)

        tpos = [T0]

        def small(name, shape, dt=F32):
            n = int(np.prod(shape)) * 4
            x = at(name, shape, tpos[0], dt)
            tpos[0] += (n + 31) // 32 * 32
            return x

        ident = small("ident", [P])
        tri = small("tri", [2, P])
        blockm = small("block", [P])
        neg = small("neg", [2, P])
        half = small("half", [2])
        wmask = small("wmask", [GRID_W])
        ones = small("ones", [P])
        LV0 = tpos[0]
        level = small("level", [2, LEVELS, P])
        causal = at("causal", [2, P], LV0)
        rope_cs = at("rope_cs", [2, TT, HD // 2], LV0 + 1024)
        conv2_w = at("conv2_w", [3, 88], LV0 + 2048)
        conv2_b = at("conv2_b", [88], LV0 + 3136)
        gq_bc = at("gq_bc", [2, HD], LV0 + 3520)
        gout_bc = at("gout_bc", [GLA_DV], LV0 + 4544)
        sink_bc = at("sink_bc", [HEADS], LV0 + 5568)
        normw = small("normw", [4, KT])
        conv1_w = small("conv1_w", [5, 24])
        dtal = small("dtal", [2, 16])
        onorm = small("onorm", [HD])
        ba = small("ba", [TT, 32])
        sc32 = {n: small(n, [HEADS, 2, TT]) for n in ("bt", "gg", "gc", "gl_c", "bte", "ekg")}
        tmp64 = {n: small(n, [64]) for n in ("ta", "tb", "tc")}
        ghalf = small("ghalf", [2, HEADS, 2, TT])
        glast = small("glast", [2, HEADS, 2, TT])
        st = small("st", [8])
        stp = small("stp", [TT, 4])
        st8 = small("st8", [64])
        eps = small("eps", [1])
        pdum = small("pdum", [1])
        amx, anm, asm, aes = (small(n, [2, TT]) for n in ("amx", "anm", "asm", "aes"))
        S0 = tpos[0]
        assert 229368 - S0 >= 17 * K, 229368 - S0

        dnT = at("dnT", [24, SEQ], R0 + 40 * K)
        attqk = at("attqk", [16, SEQ], R0 + 16 * K)
        attv = at("attv", [TT, 1024], R0 + 8 * K)
        z_silu = at("z_silu", [TT, 1024], H0)
        gates_out = at("gates_out", [2, 1024], H0 + 8 * K)
        conv_pad = at("conv_pad", [2, 4, 260], S0)
        conv_out = at("conv_out", [2, 4, SEQ], S0 + 8352)
        bias = at("bias", [4, TT, SEQ], S0)
        flip = at("flip", [P], S0 + 16 * K)
        att_scores = at("att_scores", [2, TT, SEQ], S0 + 8 * K)
        att_probsT = at("att_probsT", [2, TT, SEQ], S0 + 12 * K)
        baT = at("baT", [SEQ], S0 + 16 * K + 512)
        G = 4
        q_decayT = at("q_decayT", [G, 2, SEQ], A0)
        k_decay = at("k_decay", [G, 2, TT, HD], A0 + 8 * K)
        w_T = at("w_T", [G, 2, TT, P], A0 + 16 * K)
        u_rows = at("u_rows", [G, 2, TT, HD], A0 + 24 * K)
        qkT = at("qkT", [G, 2, TT, P], R0 + 16 * K)
        k_betaT, k_beta_decay, v_beta, exp_rows, decays_, triT, inverse, level_prod, tri_levels, states = ([] for _ in range(10))
        for n, (b0, b1, b2) in enumerate(((R0 + 24 * K, R0 + 8 * K, S0), (RAW0, RAW0 + 8 * K, RAW0 + 16 * K))):
            k_betaT.append(at(f"k_betaT{n}", [2, SEQ], b0))
            k_beta_decay.append(at(f"k_beta_decay{n}", [2, TT, HD], b0))
            v_beta.append(at(f"v_beta{n}", [2, TT, HD], b0 + 2 * K))
            exp_rows.append(at(f"exp_rows{n}", [2, TT, P], b0 + 4 * K))
            decays_.append(at(f"decays_{n}", [2, TT, P], b0 + 6 * K))
            triT.append(at(f"triT{n}", [2, TT, P], b1))
            inverse.append(at(f"inverse{n}", [2, 4, P], b1 + 2 * K))
            level_prod.append(at(f"level_prod{n}", [4, P], b1 + 6 * K))
            tri_levels.append(at(f"tri_levels{n}", [2, TT, LEVELS - 1, P], b2))
            states.append(at(f"states{n}", [2, G, HD], b2 + 10 * K))
        v_new = at("v_new", [G, HD], S0 + 14 * K)
        delta_out = at("delta_out", [TT, HEADS, HD], H0 + 8 * K)
        sq_buf = at("sq_buf", [2, 512], S0)
        root_buf = at("root_buf", [2, 512], S0 + 4 * K)
        delta_sq = at("delta_sq", [TT, HEADS, HD], A0)
        gates_in = at("gates_in", [2, 1024], R0 + 16 * K)
        mixa = at("mixa", [1024], R0 + 48 * K)
        mixb = at("mixb", [1024], R0 + 52 * K)
        rows_scaled = at("rows_scaled", [TT, D], R0)
        junk = at("junk", [D], R0 + 16 * K)
        junk_part = at("junk_part", [BLK_N], S0)
        wrow = at("wrow", [D], R0 + 24 * K)
        relu_buf = at("relu_buf", [1024], S0)
        relu_sq = at("relu_sq", [1024], S0 + 4 * K)
        qa = at("qa", [TT, 1024], R0 + 16 * K)
        kva = at("kva", [TT, 512], R0 + 24 * K)
        qkg = at("qkg", [8, SEQ], R0 + 48 * K)
        vg = at("vg", [TT, 1024], R0 + 56 * K)
        gg2 = at("gg2", [TT, 1024], S0)
        lrT = at("lrT", [SEQ], S0 + 8 * K)
        decay_w = at("decay_w", [2, 512], S0 + 9 * K)
        log_decay = at("log_decay", [2, TT, 512], R0 + 16 * K)
        rot_a = at("rot_a", [TT, 1024], R0 + 8 * K)
        rot_b = at("rot_b", [TT, 1024], R0 + 40 * K)
        qT2 = at("qT2", [8, SEQ], R0 + 8 * K)
        kT2 = at("kT2", [2, SEQ], R0 + 28 * K)
        bmask = at("bmask", [TT, SEQ], R0 + 30 * K)
        att2_scores = at("att2_scores", [2, TT, SEQ], R0 + 40 * K)
        att2_probsT = at("att2_probsT", [2, TT, SEQ], R0 + 44 * K)
        cum = at("cum", [4, SEQ], A0)
        cum_ref = at("cum_ref", [4, SEQ], A0 + 4 * K)
        cum_last = at("cum_last", [4, SEQ], A0 + 8 * K)
        qga = at("qga", [4, SEQ], A0 + 12 * K)
        kga = at("kga", [4, SEQ], A0 + 16 * K)
        q_in = at("q_in", [4, SEQ], A0 + 20 * K)
        k_out = at("k_out", [4, SEQ], A0 + 24 * K)
        k_outT = at("k_outT", [4, TT, P], A0 + 28 * K)
        softplus_buf = at("softplus_buf", [2048], S0)
        gla_scoresT = at("gla_scoresT", [4, TT, P], S0 + 13 * K)
        gla_state = at("gla_state", [2, 4, GLA_DV], R0 + 24 * K)
        gla_out = at("gla_out", [TT, 4, GLA_DV], A0)
        gla_sq = at("gla_sq", [TT, 4, GLA_DV], A0 + 8 * K)
        ffn_pad = at("ffn_pad", [2, 4, 258], S0)
        ffn_conv = at("ffn_conv", [2, 1024], S0 + 8320)

        bank = [ctx.enter_context(nc.psum_tensor(f"bank{n}", [P, 512], F32)) for n in range(4)]
        product = [ctx.enter_context(nc.psum_tensor(f"product{n}", [P, 1024], F32)) for n in range(2)]
        gates_dram = nc.dram_tensor("gates_dram", [8, P, 1024], F32, kind="Internal").ap()

        W1, W2 = t["w_in"], t["w_in_2"]
        acts = {"x1": (a1h, a1l), "hid": (a2h, a2l)}
        full = KT // BLK_KT
        PH = {}
        PH["ba"] = Phase([Chunk(W1, 0, C_BA, 1, "up", n=32)], 1, 0, "x1")
        PH["lead"] = Phase([Chunk(W1, 0, C_V, full, "down")], 1, 0, "x1")
        PH["v"] = Phase([Chunk(W1, 0, C_V + 512, full, "down")], 1, 0, "x1")
        PH["qk"] = Phase([Chunk(W1, 0, C_QK + 512 * n, full, "up") for n in range(2)], 2, 1024, "x1")
        PH["dn0"] = Phase([Chunk(W1, 0, C_DN + 512 * n, full, "up") for n in range(2)], 1, 0, "x1")
        PH["dn"] = Phase([Chunk(W1, 0, C_DN + 1024 + 512 * n, full, "up") for n in range(2)], 2, 1024, "x1")
        PH["z"] = Phase([Chunk(W1, 0, C_Z + 512 * n, full, "down") for n in range(2)], 1, 0, "x1")
        PH["gates"] = Phase([Chunk(W1, 0, C_GATES + 512 * n, full, "up") for n in range(8)], 1, 0, "x1")
        for name, col, trips in (("mix0", 0, 1), ("mix", 512, 3)):
            PH[name] = Phase([Chunk(t["w_proj_a"], 0, col, full // 2, "up", 0), Chunk(t["w_proj_b"], 0, col, full // 2, "up", 8)],
                             trips, 512, "hid")
        PH["out"] = Phase([Chunk(t["w_out"], 0, 512 * n, full, "down") for n in range(4)], 1, 0, "x1")
        for g in range(2):
            PH[f"upa{g}"] = Phase([Chunk(t["w_mlp_up"], 0, 4096 * g + 512 * n, full, "up") for n in range(2)], 1, 0, "x1")
            PH[f"up{g}"] = Phase([Chunk(t["w_mlp_up"], 0, 4096 * g + 1024 + 512 * n, full, "up") for n in range(2)], 3, 1024, "x1")
        PH["down0"] = Phase([Chunk(t["w_mlp_down"], 0, 512 * n, 32 // BLK_KT, "down") for n in range(2)], 2, 1024, "hid")
        PH["down1"] = Phase([Chunk(t["w_mlp_down"], 4096, 512 * n, 32 // BLK_KT, "down") for n in range(4)], 1, 0, "hid")
        PH["lr"] = Phase([Chunk(W2, 0, D_LR, 1, "up", n=32)], 1, 0, "x1")
        PH["kv"] = Phase([Chunk(W2, 0, D_KV, full, "down")], 1, 0, "x1")
        PH["qa"] = Phase([Chunk(W2, 0, D_QA + 512 * n, full, "down") for n in range(2)], 1, 0, "x1")
        PH["qkg"] = Phase([Chunk(W2, 0, D_QKG + 512 * n, full, "up") for n in range(2)], 1, 0, "x1")
        PH["vg"] = Phase([Chunk(W2, 0, D_VG + 512 * n, full, "down") for n in range(2)], 1, 0, "x1")
        PH["gg"] = Phase([Chunk(W2, 0, D_GG + 512 * n, full, "down") for n in range(2)], 1, 0, "x1")
        PH["out2"] = Phase([Chunk(t["w_out_2"], 0, 512 * n, full, "down") for n in range(4)], 1, 0, "hid")
        for g, (n0, n1) in enumerate(((0, 6), (6, 11))):
            PH[f"ffa{g}"] = Phase([Chunk(t["w_up_2"], 0, base + 512 * n0, full, "up") for base in (0, DFF2)], 1, 0, "x1")
            PH[f"ff{g}"] = Phase([Chunk(t["w_up_2"], 0, base + 512 * (n0 + 1), full, "up") for base in (0, DFF2)],
                                 n1 - n0 - 1, 512, "x1")
            nk = (n1 - n0)
            PH[f"dd{g}"] = Phase([Chunk(t["w_down_2"], 512 * n0, 512 * n, 4 * nk // BLK_KT, "down") for n in range(4)], 1, 0, "hid")
        order = ["lead", "ba", "v", "qk", "dn0", "dn", "z", "gates", "mix0", "mix", "out", "upa0", "up0", "down0", "upa1", "up1",
                 "down1", "kv", "qa", "lr", "qkg", "vg", "gg", "out2", "ffa0", "ff0", "dd0", "ffa1", "ff1", "dd1"]
        phases = [PH[n] for n in order]
        BLOCKS = number(phases)

        block_loaded = [sem(f"block_loaded{n}") for n in range(RAW_SLOTS)]
        block_high, block_low = sem("block_high"), sem("block_low")
        block_multiplied = sem("block_multiplied")
        product_read = [sem(f"product_read{n}") for n in range(2)]
        s_act, s_dve = sem("s_act"), sem("s_dve")
        gates_stored = [sem(f"gates_stored{n}") for n in range(2)]
        gates_loaded = [sem(f"gates_loaded{n}") for n in range(2)]
        S = {n: sem(n) for n in " ".join((
            "first_tables_loaded tables1_loaded tables2_loaded x_loaded residual_loaded",
            "attention_tables_loaded final_weights_loaded decay_w_cleared decay_w_loaded decay_w_ready band_loaded",
            "norm_squares norm_means norm_roots rows_scaled_ready rows_normed vector_clears",
            "turned_psum turned_high turned_low",
            "conv_taps_added conv_activated",
            "scores_ready scores_masked row_max_ready exp_ready probs_scaled probs_turned probs_turned_out head_out_ready head_out_high head_out_low",
            "decay_inputs decay_vector decay_scalar decay_cumulated decay_columns",
            "unit_squares unit_sums unit_roots unit_scaled",
            "decay_rows_psum decay_exponents decay_exps k_beta_ready gram_psum triangle_ready qk_decayed",
            "level0_inverse level0_turned level0_turned_out token_rows_psum token_rows_scaled q_decayed",
            "triangle_levels level_inner_psum level_inner_out level_outer_psum inverse_updated uw_psum uw_out",
            "w_state_psum values_ready state_gain_psum state_ready step_out_psum step_out_copied step_out_added",
            "delta_norm_scalar delta_norm_vector mixed_ready mixed_high mixed_low",
            "gate_convolved gate_silu gate_product hidden_high hidden_low",
            "qk_norm_scalar qk_norm_means qk_rotated qk_turned qk_turned_out",
            "gla_decay_psum gla_decay_scalar gla_decay_vector gla_cumulated gla_cumulated_out",
            "gla_differences gla_exps gla_operands gla_scores_psum gla_scores_masked gla_k_turned gla_k_turned_out",
            "gla_gain_psum gla_state_ready gla_step_out gla_direction_out gla_out_copied gla_norm_scalar gla_norm_vector",
            "output_stored",
        )).split()}
        bias_loaded = [sem(f"bias_loaded{n}") for n in range(4)]

        def raw_value(idx, i, nb):
            return 16 * (idx // RAW_SLOTS + 1) + i * (16 * nb // RAW_SLOTS)

        def last_block(ph):
            return ph.b0 + ph.nb * ph.trips

        NCONST = 16
        NCONST2 = 11
        TG = {"mix": 0, "yb": 8, "mlp": 12, "norm1": 20, "cat": 28, "norm2": 32}
        NS = {"mix": 0, "mlp": 1, "final": 2, "norm1": 3, "norm2": 4}

        def wait_read_out(eng, ph, trip, n):
            ch = ph.body[n]
            eng.wait_ge(product_read[ch.c % 2], ch.c // 2 + 1 + trip * (ph.nc // 2))

        LV = LEVELS - 1
        HEAD_SLOTS = 4
        STEPS = {"scores": 0, "mask": 1, "exp": 2, "scale": 3, "turn": 4, "turned": 5, "values": 6, "high": 7, "low": 8}
        ATT_START = {0: 8, HEADS: 14}

        def head_at(step, base, k):
            hh, rest = divmod(k - ATT_START[base] - STEPS[step], HEAD_SLOTS)
            return hh if rest == 0 and 0 <= hh < HEADS else None

        def batch_at(late, k):
            j, rest = divmod(k - 51 - late, 3)
            return j if rest == 0 and 0 <= j < 8 else None

        def pair_count(hh, n=1, rounds=1):
            return 2 * rounds * (hh // 2) + 2 * (n - 1) + hh % 2 + 1

        block = ctx.enter_context(nc.Block())

        @block.sync
        def _(sp):
            def stream(ph):
                with Loop(sp, ph.trips) as i:
                    for n, ch in enumerate(ph.body):
                        for j in range(ch.blocks):
                            idx = ch.b + j
                            slot = idx % RAW_SLOTS
                            if ph is PH["mix0"] and j == 0 and n == 1:
                                sp.wait_ge(S["step_out_added"], 4)
                            if idx >= RAW_SLOTS:
                                sp.wait_ge(block_high, idx - RAW_SLOTS + 1 + i * ph.nb)
                                sp.wait_ge(block_low, idx - RAW_SLOTS + 1 + i * ph.nb)
                            if ch.n == BLK_N:
                                rows = ch.w[ch.row + j * BLK_KT * P:ch.row + (j + 1) * BLK_KT * P, :]
                                src = rows.rearrange("(t p) n -> p t n", p=P)[:, :, bass.ds(ch.col + i * ph.step, BLK_N)] \
                                    if ph.trips > 1 else rows.rearrange("(t p) n -> p t n", p=P)[:, :, ch.col:ch.col + BLK_N]
                                sp.dma_start(raw[:, slot], src).then_inc(block_loaded[slot], 16)
                            else:
                                src = ch.w.rearrange("(t p) n -> p t n", p=P)[:, :, ch.col:ch.col + ch.n]
                                dst = raw[:, slot, 0, :].rearrange("p (t n) -> p t n", n=ch.n)
                                sp.dma_start(dst, src).then_inc(block_loaded[slot], 16)
            sp.dma_start(h[:, :, :], t["x"][0].rearrange("(t p) n -> p t n", p=P)).then_inc(S["x_loaded"], 16)
            for name in order:
                stream(PH[name])
            wait_read_out(sp, PH["dd1"], 0, 2)
            wait_read_out(sp, PH["dd1"], 0, 3)
            sp.dma_start(t["out"][0].rearrange("(t p) n -> p t n", p=P), h[:, :, :]).then_inc(S["output_stored"], 16)
            sp.wait_ge(S["output_stored"], 16)

        @block.scalar
        def _(act):
            chain = Chain(act, s_act)

            def split(idx, i, nb):
                if idx >= BLOCKS:
                    return
                act.wait_ge(block_loaded[idx % RAW_SLOTS], raw_value(idx, i, nb))
                if idx >= HL_SLOTS:
                    act.wait_ge(block_multiplied, idx - HL_SLOTS + 1 + i * nb)
                if idx == PH["ba"].b0:
                    sl, rs = idx % HL_SLOTS, idx % RAW_SLOTS
                    nc.scalar.copy(wh[:, sl, 0, :], raw[:, rs, 0, :]).then_inc(block_high, 1)
                else:
                    nc.scalar.copy(wh[:, idx % HL_SLOTS], raw[:, idx % RAW_SLOTS]).then_inc(block_high, 1)

            def gemm(ph, read_out, per=0, between=None, k0=0):
                with Loop(act, ph.trips, chain, per) as i:
                    for n, ch in enumerate(ph.body):
                        for j in range(ch.blocks):
                            if between is not None:
                                between(k0 + ch.b - ph.b0 + j)
                            split(ch.b + HL_SLOTS + j, i, ph.nb)
                        if read_out is not None:
                            act.wait_ge(block_multiplied, ch.b + ch.blocks + i * ph.nb)
                            read_out(n, i, product[ch.c % 2], product_read[ch.c % 2])

            def norm_stats(name, squares=True):
                k = NS[name]
                if squares:
                    for tt in range(TT):
                        if name == "norm1":
                            act.wait_ge(S["rows_normed"], tt + 1)
                        a = nc.scalar.activation(junk[:, :], h[:, tt, :], ACT.Square, accum_out=st[:, tt:tt + 1])
                        if tt == 0:
                            chain(a)
                        else:
                            a.then_inc(S["norm_squares"], 1)
                act.wait_ge(S["norm_means"], k + 1)
                nc.scalar.activation(st[:, 4:6], st[:, 2:4], ACT.Sqrt).then_inc(S["norm_roots"], 1)

            def to_squares(ph):
                def f(n, i, g, free):
                    wait_read_out(act, ph, 0, n)
                    for tt in range(TT):
                        a = nc.scalar.activation(junk_part[:, :], h[:, tt, n * BLK_N:(n + 1) * BLK_N], ACT.Square,
                                                 accum_out=stp[:, tt, n:n + 1])
                        if n == 3 and tt == TT - 1:
                            a.then_inc(S["norm_squares"], 1)
                        else:
                            chain(a)
                return f

            def turn_hi(base, groups, dst, kt0, w=None):
                for g in range(groups):
                    act.wait_ge(S["turned_psum"], base + g + 1)
                    if w is None:
                        a = nc.scalar.copy(dst[:, kt0 + 2 * g:kt0 + 2 * g + 2, :], bank[g % 4][:, :].rearrange("p (k n) -> p k n", k=2))
                    else:
                        for m in range(2):
                            kt = 2 * g + m
                            a = nc.scalar.activation(dst[:, kt0 + kt, :], bank[g % 4][:, m * SEQ:(m + 1) * SEQ], ACT.Copy,
                                                     scale=normw[:, w, kt:kt + 1])
                    a.then_inc(S["turned_high"], 1)

            def attention(base, scores, probsT, sink, k):
                hh = head_at("exp", base, k)
                if hh is not None:
                    act.wait_ge(S["row_max_ready"], base + hh + 1)
                    b = hh % 2
                    for tt in range(TT):
                        x = scores[:, b, tt, :]
                        a = nc.scalar.activation(x, x, ACT.Exp, bias=anm[:, b, tt:tt + 1], accum_out=asm[:, b, tt:tt + 1])
                    if sink:
                        a = nc.scalar.activation(aes[:, b, :], anm[:, b, :], ACT.Exp, bias=sink_bc[:, hh:hh + 1])
                    a.then_inc(S["exp_ready"], 1)
                hh = head_at("turned", base, k)
                if hh is not None:
                    act.wait_ge(S["probs_turned"], base + hh + 1)
                    if hh >= 2:
                        act.wait_ge(S["head_out_ready"], base + hh - 1)
                    nc.scalar.copy(probsT[:, hh % 2], bank[2 + hh % 2][:, :].rearrange("p (k n) -> p k n", k=2)).then_inc(S["probs_turned_out"], 1)
                hh = head_at("high", base, k)
                if hh is not None:
                    act.wait_ge(S["head_out_ready"], base + hh + 1)
                    nc.scalar.copy(a2h[:, hh, :], bank[2 + hh % 2][:, 0:SEQ]).then_inc(S["head_out_high"], 1)

            act.wait_ge(S["x_loaded"], 16)
            norm_stats("mix")
            for n in range(HL_SLOTS):
                split(n, 0, 0)
            act.wait_ge(S["first_tables_loaded"], 32)
            turn_hi(TG["mix"], 8, a1h, 0, 0)

            def to_ba(n, i, g, free):
                nc.scalar.copy(baT[0:32, :], g[0:32, 0:SEQ]).then_inc(free, 1)

            def to_v(col):
                def f(n, i, g, free):
                    nc.scalar.copy(attv[:, :, col:col + 512], g[:, :].rearrange("p (t n) -> p t n", t=TT)).then_inc(free, 1)
                return f

            def to_qk(n, i, g, free):
                nc.scalar.copy(attqk[:, bass.ds(8 * i + 4 * n, 4), :], g[:, :].rearrange("p (m n) -> p m n", m=4)).then_inc(free, 1)

            def activate_dn(q, n):
                act.wait_ge(S["conv_taps_added"], q + 1)
                nc.scalar.activation(dnT[:, span(4 * q, 4), :], conv_out[:, n, :, :], ACT.Silu).then_inc(S["conv_activated"], 1)

            def to_dn(q0):
                def f(n, i, g, free):
                    q = 2 * i + q0 + n
                    if q0:
                        act.wait_ge(S["conv_activated"], q - 1)
                    for m in range(4):
                        nc.scalar.activation(conv_out[:, n, m, :], g[:, m * SEQ:(m + 1) * SEQ], ACT.Copy,
                                             scale=conv1_w[:, 2, span(4 * q + m, 1)])
                    nc.scalar.copy(conv_pad[:, n, :, 2:2 + SEQ], g[:, :].rearrange("p (m n) -> p m n", m=4)).then_inc(free, 1)
                    if q0 or n:
                        activate_dn(q - 1, 1 - n)
                return f

            def to_z(n, i, g, free):
                nc.scalar.activation(z_silu[:, :, n * 512:(n + 1) * 512], g[:, :].rearrange("p (t n) -> p t n", t=TT),
                                     ACT.Silu).then_inc(free, 1)

            def to_gates(n, i, g, free):
                if n >= 2:
                    act.wait_ge(gates_stored[n % 2], 16 * (n // 2))
                nc.scalar.activation(gates_out[:, n % 2, :], g[:, :], ACT.Sigmoid).then_inc(free, 1)

            tb, tc = tmp64["tb"], tmp64["tc"]

            def beside_gates(k):
                if k == 2:
                    activate_dn(5, 1)
                attention(0, att_scores, att_probsT, False, k)
                if k == 43:
                    act.wait_ge(S["decay_inputs"], 1)
                    nc.scalar.copy(ba[:, :, :], bank[0][:, 0:64].rearrange("p (t n) -> p t n", t=TT)).then_inc(S["decay_inputs"], 1)
                    act.wait_ge(S["decay_inputs"], 2)
                if k == 44:
                    beta_in = ba[:, :, 0:16].rearrange("p t (d h) -> p h d t", d=2)
                    nc.scalar.activation(sc32["bt"][:, :, :, :], beta_in, ACT.Sigmoid).then_inc(S["decay_scalar"], 1)
                    chain(nc.scalar.activation(dtal[:, 1, :], dtal[:, 1, :], ACT.Exp))
                if k == 45:
                    act.wait_ge(S["decay_vector"], 1)
                    chain(nc.scalar.activation(tc[:, 0:32], tb[:, 0:32], ACT.Exp))
                    nc.scalar.activation(tc[:, 0:32], tc[:, 0:32], ACT.Ln, bias=1.0).then_inc(S["decay_scalar"], 1)
                if k == 49:
                    act.wait_ge(S["decay_columns"], 1)
                    nc.scalar.activation(sc32["ekg"][:, :, :, :], sc32["gl_c"][:, :, :, :], ACT.Exp)
                    nc.scalar.activation(sc32["bte"][:, :, :, :], sc32["gc"][:, :, :, :], ACT.Exp)
                    nc.scalar.activation(glast[:, :, :, :, :], bank[1][:, 64:128].rearrange("p (a h d t) -> p a h d t", a=2, h=8, d=2),
                                         ACT.Exp).then_inc(S["decay_scalar"], 1)
                j = batch_at(0, k)
                if j is not None:
                    if j >= 2:
                        act.wait_ge(S["unit_sums"], j - 1)
                    nc.scalar.activation(sq_buf[:, j % 2, :], dnT[:, 2 * j:2 * j + 2, :].rearrange("p k n -> p (k n)"),
                                         ACT.Square).then_inc(S["unit_squares"], 1)
                j = batch_at(2, k)
                if j is not None:
                    act.wait_ge(S["unit_sums"], j + 1)
                    if j >= 2:
                        act.wait_ge(S["unit_scaled"], j - 1)
                    nc.scalar.activation(root_buf[:, j % 2, :], bank[2 + j % 2][:, :], ACT.Sqrt, bias=eps[:, 0:1]).then_inc(S["unit_roots"], 1)

            gemm(PH["lead"], to_v(0))
            gemm(PH["ba"], to_ba)
            gemm(PH["v"], to_v(512))
            gemm(PH["qk"], to_qk)
            act.wait_ge(S["tables1_loaded"], 16 * NCONST)
            gemm(PH["dn0"], to_dn(0))
            gemm(PH["dn"], to_dn(2))
            gemm(PH["z"], to_z, 0, beside_gates)
            gemm(PH["gates"], to_gates, 0, beside_gates, 16)
            for n in range(2):
                act.wait_ge(gates_stored[n], 16 * 4)
            for h0 in range(0, HEADS, 2):
                pair = (h0, h0 + 1)
                for hh in pair:
                    act.wait_ge(S["decay_exponents"], hh + 1)
                    x = decays_[hh % 2][:, :, :, :]
                    nc.scalar.activation(x, x, ACT.Exp).then_inc(S["decay_exps"], 1)
                for hh in pair:
                    if hh >= 2:
                        act.wait_ge(S["q_decayed"], hh - 1)
                    nc.scalar.activation(exp_rows[hh % 2][:, :, :, :], bank[2 * (hh % 2)][:, :].rearrange("p (d t n) -> p d t n", d=2, t=TT),
                                         ACT.Exp).then_inc(S["decay_exps"], 1)
                for hh in pair:
                    act.wait_ge(S["level0_turned"], hh + 1)
                    nc.scalar.copy(inverse[hh % 2][:, 0, :, :], bank[2 * (hh % 2)][:, :].rearrange("p (q n) -> p q n", q=4)).then_inc(S["level0_turned_out"], 1)
                for n in range(1, LEVELS):
                    for hh in pair:
                        act.wait_ge(S["level_inner_psum"], pair_count(hh, n, LV))
                        nc.scalar.copy(level_prod[hh % 2][:, :, :], bank[2 * (hh % 2)][:, :].rearrange("p (q n) -> p q n", q=4)).then_inc(S["level_inner_out"], 1)
                for hh in pair:
                    act.wait_ge(S["uw_psum"], hh + 1)
                    nc.scalar.copy(u_rows[:, hh % G], product[hh % 2][:, 0:512].rearrange("p (d t n) -> p d t n", d=2, t=TT))
                    nc.scalar.copy(w_T[:, hh % G], product[hh % 2][:, 512:1024].rearrange("p (d t n) -> p d t n", d=2, t=TT)).then_inc(S["uw_out"], 1)
                g = hh % G
                if g == G - 1:
                    gr = hh // G
                    for s in range(2):
                        act.wait_ge(S["step_out_psum"], 4 * gr + s + 1)
                        for d in range(2):
                            c = s if d == 0 else NCH - 1 - s
                            lo, tl = CHUNK * (c % 2), c // 2
                            a = nc.scalar.copy(delta_out[lo:lo + CHUNK, tl, G * gr:G * gr + G, :],
                                               bank[1][lo:lo + CHUNK, :].rearrange("p (g n) -> p g n", g=G))
                        a.then_inc(S["step_out_copied"], 1)
            act.wait_ge(S["step_out_added"], 4)
            nc.scalar.activation(delta_sq[:, :, :, :], delta_out[:, :, :, :], ACT.Square).then_inc(S["delta_norm_scalar"], 1)
            act.wait_ge(S["delta_norm_vector"], 1)
            nc.scalar.activation(st8[:, 16:32], st8[:, 0:16], ACT.Sqrt).then_inc(S["delta_norm_scalar"], 1)
            turn_hi(TG["yb"], 4, a2h, 8)

            def to_mix(i0):
                def f(n, i, g, free):
                    if n == 1:
                        act.wait_ge(S["mixed_ready"], i + i0 + 1)
                        nc.scalar.copy(a1h[:, span(4 * (i + i0), 4), :], mixb[:, :].rearrange("p (m n) -> p m n", m=4)).then_inc(S["mixed_high"], 1)
                return f
            gemm(PH["mix0"], to_mix(0))
            gemm(PH["mix"], to_mix(1))
            gemm(PH["out"], to_squares(PH["out"]))

            norm_stats("mlp", False)
            turn_hi(TG["mlp"], 8, a1h, 0, 1)

            def to_hidden(ph, i0):
                def f(n, i, g, free):
                    nc.scalar.activation(relu_buf[:, :], g[:, :], ACT.Relu).then_inc(free, 1)
                    wait_read_out(act, ph, i, n)
                    chain(nc.scalar.activation(relu_sq[:, :], relu_buf[:, :], ACT.Square))
                    nc.scalar.copy(a2h[:, span(8 * (i + i0) + 4 * n, 4), :], relu_sq[:, :].rearrange("p (m n) -> p m n", m=4)).then_inc(S["hidden_high"], 1)
                return f

            for k in range(2):
                gemm(PH[f"upa{k}"], to_hidden(PH[f"upa{k}"], 0))
                gemm(PH[f"up{k}"], to_hidden(PH[f"up{k}"], 1), 2)
                gemm(PH[f"down{k}"], to_squares(PH["down1"]) if k else None)
            norm_stats("final", False)
            norm_stats("norm1")
            turn_hi(TG["norm1"], 8, a1h, 0, 2)

            def to_lr(n, i, g, free):
                nc.scalar.copy(lrT[0:32, :], g[0:32, 0:SEQ]).then_inc(free, 1)

            def to_rows(dst, func=ACT.Copy):
                def f(n, i, g, free):
                    nc.scalar.activation(dst[:, :, n * 512:(n + 1) * 512], g[:, :].rearrange("p (t n) -> p t n", t=TT), func).then_inc(free, 1)
                return f

            def to_qkg(n, i, g, free):
                nc.scalar.copy(qkg[:, 4 * n:4 * n + 4, :], g[:, :].rearrange("p (m n) -> p m n", m=4)).then_inc(free, 1)

            gemm(PH["kv"], to_rows(kva))
            gemm(PH["qa"], to_rows(qa))
            gemm(PH["lr"], to_lr)

            def attend2(k):
                if k == 0:
                    wait_read_out(act, PH["qa"], 0, 1)
                    nc.scalar.activation(rot_a[:, :, :], qa[:, :, :], ACT.Square)
                    nc.scalar.activation(rot_b[:, :, 0:256], kva[:, :, 0:256], ACT.Square).then_inc(S["qk_norm_scalar"], 1)
                if k == 2:
                    act.wait_ge(S["qk_norm_means"], 1)
                    nc.scalar.activation(st8[:, 32:52], st8[:, 0:20], ACT.Sqrt).then_inc(S["qk_norm_scalar"], 1)
                if k in (12, 13):
                    for g in range(4) if k == 12 else (4,):
                        act.wait_ge(S["qk_turned"], g + 1)
                        dst = qT2[:, 2 * g:2 * g + 2, :] if g < 4 else kT2[:, :, :]
                        nc.scalar.copy(dst, bank[g % 4][:, :].rearrange("p (k n) -> p k n", k=2)).then_inc(S["qk_turned_out"], 1)
                attention(HEADS, att2_scores, att2_probsT, True, k)
                if k in (18, 22, 26, 30):
                    q = (k - 18) // 4
                    act.wait_ge(S["gla_decay_psum"], q + 1)
                    nc.scalar.copy(log_decay[:, q // 2, q % 2, :], bank[q % 2][:, :]).then_inc(S["gla_decay_scalar"], 1)
                if k == 32:
                    act.wait_ge(S["gla_decay_vector"], 1)
                    chain(nc.scalar.activation(softplus_buf[:, :], softplus_buf[:, :], ACT.Exp))
                    nc.scalar.activation(softplus_buf[:, :], softplus_buf[:, :], ACT.Ln, bias=1.0).then_inc(S["gla_decay_scalar"], 1)

            gemm(PH["qkg"], to_qkg, 0, attend2)
            gemm(PH["vg"], to_rows(vg), 0, attend2, 16)
            gemm(PH["gg"], to_rows(gg2, ACT.Silu), 0, attend2, 32)
            attend2(48)
            attend2(49)
            for d in range(2):
                last = CHUNK - 1 if d == 0 else 0
                act.wait_ge(S["gla_cumulated"], d + 1)
                if d:
                    act.wait_ge(S["gla_operands"], 3)
                    act.wait_ge(S["gla_scores_psum"], 1)
                    act.wait_ge(S["gla_direction_out"], 1)
                nc.scalar.activation(cum[:, :, :], product[0][:, :].rearrange("p (h n) -> p h n", h=4), ACT.Copy, scale=1.0 / 16).then_inc(S["gla_cumulated_out"], 1)
                act.wait_ge(S["gla_cumulated_out"], d + 1)
                act.wait_ge(S["gla_differences"], 2 * d + 1)
                nc.scalar.activation(qga[:, :, :], cum_ref[:, :, :], ACT.Exp)
                nc.scalar.activation(kga[:, :, :], cum_ref[:, :, :], ACT.Exp, scale=-1.0).then_inc(S["gla_exps"], 1)
                act.wait_ge(S["gla_differences"], 2 * d + 2)
                nc.scalar.activation(k_out[:, :, :], cum_last[:, :, :], ACT.Exp, scale=-1.0).then_inc(S["gla_exps"], 1)
                chain(nc.scalar.activation(st8[:, 0:16].rearrange("p (h c) -> p h c", h=4),
                                           cum[:, :, :].rearrange("p h (c n) -> p h c n", n=CHUNK)[:, :, :, last], ACT.Exp))
                nc.scalar.activation(q_in[:, :, :], cum[:, :, :], ACT.Exp).then_inc(S["gla_exps"], 1)
                act.wait_ge(S["gla_k_turned"], d + 1)
                nc.scalar.copy(k_outT[:, :, :, :], product[0][:, :].rearrange("p (h t n) -> p h t n", h=4, t=TT)).then_inc(S["gla_k_turned_out"], 1)
            act.wait_ge(S["gla_direction_out"], 2)
            for tt in range(TT):
                for k in range(2):
                    a = nc.scalar.copy(gla_out[:, tt, 2 * k:2 * k + 2, :], bank[2 * tt + k][:, :].rearrange("p (h n) -> p h n", h=2))
            a.then_inc(S["gla_out_copied"], 1)
            act.wait_ge(S["gla_out_copied"], 1)
            nc.scalar.activation(gla_sq[:, :, :, :], gla_out[:, :, :, :], ACT.Square).then_inc(S["gla_norm_scalar"], 1)
            act.wait_ge(S["gla_norm_vector"], 1)
            nc.scalar.activation(st8[:, 16:24], st8[:, 0:8], ACT.Sqrt).then_inc(S["gla_norm_scalar"], 1)
            turn_hi(TG["cat"], 4, a2h, 8)
            gemm(PH["out2"], to_squares(PH["out2"]))
            norm_stats("norm2", False)
            turn_hi(TG["norm2"], 8, a1h, 0, 3)

            def hidden_hi(q, tile):
                act.wait_ge(S["gate_product"], q + 1)
                nc.scalar.copy(a2h[:, span(tile, 4), :], ffn_conv[:, 1, :].rearrange("p (m n) -> p m n", m=4)).then_inc(S["hidden_high"], 1)

            def to_ff(q0, after):
                def f(n, i, g, free):
                    q = i + q0
                    if n == 0 and after:
                        hidden_hi(q - 1, 4 * i)
                        act.wait_ge(S["hidden_high"], 16 + q)
                    if n == 1 and after:
                        act.wait_ge(S["hidden_low"], 16 + q)
                    for m in range(4):
                        col = span(4 * q + 44 * n + m, 1)
                        nc.scalar.activation(ffn_conv[:, n, m * SEQ:(m + 1) * SEQ], g[:, m * SEQ:(m + 1) * SEQ], ACT.Identity,
                                             scale=conv2_w[:, 1, col], bias=conv2_b[:, col])
                    nc.scalar.copy(ffn_pad[:, n, :, 1:1 + SEQ], g[:, :].rearrange("p (m n) -> p m n", m=4)).then_inc(free, 1)
                    if n == 1:
                        act.wait_ge(S["gate_convolved"], q + 1)
                        nc.scalar.activation(ffn_conv[:, 0, :], ffn_conv[:, 0, :], ACT.Silu).then_inc(S["gate_silu"], 1)
                return f
            gemm(PH["ffa0"], to_ff(0, False))
            gemm(PH["ff0"], to_ff(1, True))
            gemm(PH["dd0"], None, 0, lambda k: hidden_hi(5, 20) if k == 2 else None)
            gemm(PH["ffa1"], to_ff(6, False))
            gemm(PH["ff1"], to_ff(7, True))
            gemm(PH["dd1"], None, 0, lambda k: hidden_hi(10, 16) if k == 2 else None)

        @block.vector
        def _(dve):
            V = nc.vector
            chain = Chain(dve, s_dve)

            def split(idx, i, nb):
                if idx >= BLOCKS:
                    return
                dve.wait_ge(block_loaded[idx % RAW_SLOTS], raw_value(idx, i, nb))
                dve.wait_ge(block_high, idx + 1 + i * nb)
                if idx == PH["ba"].b0:
                    sl, rs = idx % HL_SLOTS, idx % RAW_SLOTS
                    V.tensor_tensor(wl[:, sl, 0, :], raw[:, rs, 0, :], wh[:, sl, 0, :].bitcast(F32), ALU.subtract).then_inc(block_low, 1)
                else:
                    V.tensor_tensor(wl[:, idx % HL_SLOTS], raw[:, idx % RAW_SLOTS], wh[:, idx % HL_SLOTS].bitcast(F32),
                                    ALU.subtract).then_inc(block_low, 1)

            def gemm(ph, read_out, per=0, waits=True, between=None, k0=0):
                with Loop(dve, ph.trips, chain, per) as i:
                    for n, ch in enumerate(ph.body):
                        for j in range(ch.blocks):
                            if between is not None:
                                between(k0 + ch.b - ph.b0 + j)
                            split(ch.b + HL_SLOTS + j, i, ph.nb)
                        if read_out is not None:
                            if waits:
                                dve.wait_ge(block_multiplied, ch.b + ch.blocks + i * ph.nb)
                            read_out(n, i, product[ch.c % 2], product_read[ch.c % 2])

            def norm_rows(name, weights=None, squares=True):
                k = NS[name]
                dve.wait_ge(S["norm_squares"], k + 1)
                if not squares:
                    chain(V.tensor_reduce(st[:, 0:2], stp[:, :, :], AXX, ALU.add))
                V.tensor_scalar(st[:, 2:4], st[:, 0:2], 1.0 / D, EPS, ALU.mult, ALU.add).then_inc(S["norm_means"], 1)
                dve.wait_ge(S["norm_roots"], k + 1)
                chain(V.reciprocal(st[:, 6:8], st[:, 4:6]))
                for tt in range(TT):
                    if weights is None:
                        a = V.tensor_scalar(rows_scaled[:, tt, :], h[:, tt, :], st[:, 6 + tt:7 + tt], None, ALU.mult)
                    else:
                        V.scalar_tensor_tensor(h[:, tt, :], h[:, tt, :], st[:, 6 + tt:7 + tt], weights,
                                               ALU.mult, ALU.mult).then_inc(S["rows_normed"], 1)
                if weights is None:
                    a.then_inc(S["rows_scaled_ready"], 1)

            def turn_lo(base, groups, hi, lo, kt0, w=None):
                for g in range(groups):
                    dve.wait_ge(S["turned_high"], base + g + 1)
                    if w is None:
                        sl = slice(kt0 + 2 * g, kt0 + 2 * g + 2)
                        a = V.tensor_tensor(lo[:, sl, :], bank[g % 4][:, :].rearrange("p (k n) -> p k n", k=2),
                                            hi[:, sl, :].bitcast(F32), ALU.subtract)
                    else:
                        for m in range(2):
                            kt = 2 * g + m
                            a = V.scalar_tensor_tensor(lo[:, kt0 + kt, :], bank[g % 4][:, m * SEQ:(m + 1) * SEQ], normw[:, w, kt:kt + 1],
                                                       hi[:, kt0 + kt, :].bitcast(F32), ALU.mult, ALU.subtract)
                    a.then_inc(S["turned_low"], 1)

            def attention(base, scores, mask, sink, k):
                hh = head_at("scale", base, k)
                if hh is not None:
                    b = hh % 2
                    dve.wait_ge(S["exp_ready"], base + hh + 1)
                    if sink:
                        chain(V.tensor_tensor(asm[:, b, :], asm[:, b, :], aes[:, b, :], ALU.add))
                    chain(V.reciprocal(asm[:, b, :], asm[:, b, :]))
                    for tt in range(TT):
                        x = scores[:, b, tt, :]
                        a = V.tensor_scalar(x, x, asm[:, b, tt:tt + 1], None, ALU.mult)
                    a.then_inc(S["probs_scaled"], 1)
                hh = head_at("mask", base, k)
                if hh is not None:
                    b = hh % 2
                    dve.wait_ge(S["scores_ready"], base + hh + 1)
                    if hh >= 2:
                        dve.wait_ge(S["probs_turned"], base + hh - 1)
                    V.scalar_tensor_tensor(scores[:, b].rearrange("p t (r c) -> p (t r) c", c=mask.shape[2]),
                                           bank[b][:, :].rearrange("p (r c) -> p r c", c=mask.shape[2]), SCALE, mask,
                                           ALU.mult, ALU.add).then_inc(S["scores_masked"], 1)
                    dve.wait_ge(S["scores_masked"], base + hh + 1)
                    chain(V.tensor_reduce(amx[:, b, :], scores[:, b], AXX, ALU.max))
                    if sink:
                        chain(V.tensor_scalar(amx[:, b, :], amx[:, b, :], sink_bc[:, hh:hh + 1], None, ALU.max))
                    V.tensor_scalar(anm[:, b, :], amx[:, b, :], -1.0, None, ALU.mult).then_inc(S["row_max_ready"], 1)
                hh = head_at("low", base, k)
                if hh is not None:
                    dve.wait_ge(S["head_out_high"], base + hh + 1)
                    V.tensor_tensor(a2l[:, hh, :], bank[2 + hh % 2][:, 0:SEQ], a2h[:, hh, :].bitcast(F32), ALU.subtract).then_inc(S["head_out_low"], 1)

            chain(V.memset(eps[:, :], EPS))
            V.memset(ones[:, :], 1.0)
            V.memset(conv_pad[:, :, :, 0:2], 0.0)
            V.memset(conv_pad[:, :, :, 2 + SEQ:4 + SEQ], 0.0).then_inc(S["vector_clears"], 1)
            norm_rows("mix")
            for n in range(HL_SLOTS):
                split(n, 0, 0)
            dve.wait_ge(S["first_tables_loaded"], 32)
            turn_lo(TG["mix"], 8, a1h, a1l, 0, 0)

            def to_dn(q0):
                def f(n, i, g, free):
                    q = 2 * i + q0 + n
                    wait_read_out(dve, PH["dn" if q0 else "dn0"], i, n)
                    for tap in (0, 1, 3, 4):
                        for m in range(4):
                            o = conv_out[:, n, m, :]
                            a = V.scalar_tensor_tensor(o, conv_pad[:, n, m, tap:tap + SEQ], conv1_w[:, tap, span(4 * q + m, 1)], o,
                                                       ALU.mult, ALU.add)
                        if tap < 4:
                            chain(a)
                    a.then_inc(S["conv_taps_added"], 1)
                return f

            for name in ("lead", "ba", "v", "qk"):
                gemm(PH[name], None)
            dve.wait_ge(S["tables1_loaded"], 16 * NCONST)
            gemm(PH["dn0"], to_dn(0), 6, waits=False)
            gemm(PH["dn"], to_dn(2), 6, waits=False)

            bt, gg, gc, glc, bte, ekg = (sc32[n] for n in ("bt", "gg", "gc", "gl_c", "bte", "ekg"))
            ta, tb, tc = (tmp64[n] for n in ("ta", "tb", "tc"))
            hdt = dict(h=HEADS, d=2, t=TT)
            ta4, tc4 = (x[:, 0:32].rearrange("p (h d t) -> p h d t", **hdt) for x in (ta, tc))
            alpha = ba[:, :, 16:32].rearrange("p t (d h) -> p h d t", d=2)

            def per_head_dir(row):
                return row.rearrange("p (d h) -> p h d", d=2).unsqueeze(3).to_broadcast([P, HEADS, 2, TT])

            def beside_gates(k):
                if k == ATT_START[0]:
                    dve.wait_ge(S["attention_tables_loaded"], 32)
                attention(0, att_scores, wmask[:, :].unsqueeze(1).to_broadcast([P, 8, GRID_W]), False, k)
                if k == 44:
                    dve.wait_ge(S["decay_inputs"], 2)
                    chain(V.tensor_tensor(ta4, alpha, per_head_dir(dtal[:, 0, :]), ALU.add))
                    V.scalar_tensor_tensor(tb[:, 0:32], ta[:, 0:32], -1.0, ta[:, 0:32], ALU.mult, ALU.min).then_inc(S["decay_vector"], 1)
                if k == 46:
                    dve.wait_ge(S["decay_scalar"], 2)
                    chain(V.scalar_tensor_tensor(tc[:, 0:32], ta[:, 0:32], 0.0, tc[:, 0:32], ALU.max, ALU.add))
                    chain(V.tensor_scalar(tc[:, 0:32], tc[:, 0:32], -1.0, None, ALU.mult))
                    chain(V.tensor_tensor(gg[:, :, :, :], tc4, per_head_dir(dtal[:, 1, :]), ALU.mult))
                    for a in range(2):
                        i_ = V.tensor_scalar(ghalf[:, a], gg[:, :, :, :], half[:, a:a + 1], None, ALU.mult)
                    i_.then_inc(S["decay_vector"], 1)
                if k == 48:
                    dve.wait_ge(S["decay_cumulated"], 1)
                    chain(V.tensor_copy(gc[:, :, :, :], bank[0][:, 0:32].rearrange("p (d h t) -> p h d t", d=2, h=HEADS)))
                    V.tensor_tensor(glc[:, :, :, :], bank[1][:, 0:32].rearrange("p (h d t) -> p h d t", **hdt), gc[:, :, :, :],
                                    ALU.subtract).then_inc(S["decay_columns"], 1)
                if k == 50:
                    dve.wait_ge(S["decay_scalar"], 3)
                    chain(V.tensor_tensor(bte[:, :, :, :], bte[:, :, :, :], bt[:, :, :, :], ALU.mult))
                j = batch_at(3, k)
                if j is not None:
                    dve.wait_ge(S["unit_roots"], j + 1)
                    chain(V.reciprocal(root_buf[:, j % 2, :], root_buf[:, j % 2, :]))
                    x = dnT[:, 2 * j:2 * j + 2, :].rearrange("p k n -> p (k n)")
                    V.scalar_tensor_tensor(x, x, SCALE if j < 4 else 1.0, root_buf[:, j % 2, :], ALU.mult, ALU.mult).then_inc(S["unit_scaled"], 1)

            gemm(PH["z"], None, between=beside_gates)
            gemm(PH["gates"], None, between=beside_gates, k0=16)
            dve.wait_ge(S["unit_scaled"], 8)
            dve.wait_ge(block_low, PH["mix0"].b0 + HL_SLOTS)

            def over_dirs(x):
                return x.unsqueeze(1).to_broadcast([P, 2] + list(x.shape[1:]))

            def rows(x, hh):
                return x[:, hh].unsqueeze(3).to_broadcast([P, 2, TT, P])

            for h0 in range(0, HEADS, 2):
                pair = (h0, h0 + 1)
                for hh in pair:
                    b = hh % 2
                    dve.wait_ge(S["decay_rows_psum"], hh + 1)
                    for d in range(2):
                        for tt in range(TT):
                            q = d * 2 + tt
                            a = V.scalar_tensor_tensor(decays_[b][:, d, tt, :], bank[2 * b][:, q * P:(q + 1) * P], gc[:, hh, d, tt:tt + 1],
                                                       neg[:, d, :], ALU.subtract, ALU.add)
                    a.then_inc(S["decay_exponents"], 1)
                    V.tensor_tensor(k_betaT[b][:, :, :], bank[2 * b + 1][:, :].rearrange("p (d n) -> p d n", d=2), over_dirs(dnT[:, 8 + hh, :]),
                                    ALU.mult).then_inc(S["k_beta_ready"], 1)
                for hh in pair:
                    b, g = hh % 2, hh % G
                    dve.wait_ge(S["decay_exps"], pair_count(hh, 1, 2))
                    dve.wait_ge(S["gram_psum"], hh + 1)
                    V.tensor_tensor(triT[b][:, :, :, :], product[b][:, 0:512].rearrange("p (d t n) -> p d t n", d=2, t=TT), decays_[b][:, :, :, :],
                                    ALU.mult).then_inc(S["triangle_ready"], 1)
                    V.tensor_tensor(qkT[:, g], over_dirs(product[b][:, 512:768].rearrange("p (t n) -> p t n", t=TT)), decays_[b][:, :, :, :],
                                    ALU.mult).then_inc(S["qk_decayed"], 1)
                    dve.wait_ge(S["triangle_ready"], hh + 1)
                    chain(V.tensor_tensor(level_prod[b][:, :, :].rearrange("p (d t) n -> p d t n", d=2), triT[b][:, :, :, :],
                                          level[:, :, 0, :].unsqueeze(2).to_broadcast([P, 2, TT, P]), ALU.mult))
                    V.tensor_tensor(inverse[b][:, 1, :, :], ident[:, :].unsqueeze(1).to_broadcast([P, 4, P]), level_prod[b][:, :, :],
                                    ALU.subtract).then_inc(S["level0_inverse"], 1)
                for hh in pair:
                    b, g = hh % 2, hh % G
                    dve.wait_ge(S["decay_exps"], pair_count(hh, 2, 2))
                    V.tensor_tensor(q_decayT[:, g], exp_rows[b][:, :, :, :].rearrange("p d t n -> p d (t n)"), over_dirs(dnT[:, hh, :]),
                                    ALU.mult).then_inc(S["q_decayed"], 1)
                    dve.wait_ge(S["token_rows_psum"], hh + 1)
                    ktok = over_dirs(bank[2 * b + 1][:, 0:256].rearrange("p (t n) -> p t n", t=TT))
                    vtok = over_dirs(bank[2 * b + 1][:, 256:512].rearrange("p (t n) -> p t n", t=TT))
                    V.tensor_tensor(k_beta_decay[b][:, :, :, :], ktok, rows(bte, hh), ALU.mult)
                    V.tensor_tensor(k_decay[:, g], ktok, rows(ekg, hh), ALU.mult)
                    V.tensor_tensor(v_beta[b][:, :, :, :], vtok, rows(bt, hh), ALU.mult).then_inc(S["token_rows_scaled"], 1)
                for n in range(1, LEVELS):
                    for hh in pair:
                        b = hh % 2
                        dve.wait_ge(S["level_outer_psum"], pair_count(hh, n, LV))
                        if n == 1:
                            dve.wait_ge(S["level0_turned_out"], hh + 1)
                        else:
                            dve.wait_ge(S["inverse_updated"], pair_count(hh, n - 1, LV))
                        half_ = slice(0, 2) if n < LV else slice(1, 2)
                        x = inverse[b][:, half_, :, :].rearrange("p a q n -> p (a q n)")
                        V.tensor_tensor(x, x, product[b][:, 512 * half_.start:1024], ALU.subtract).then_inc(S["inverse_updated"], 1)
                g, gr = hh % G, hh // G
                if g < G - 1:
                    continue
                for s in range(NCH):
                    step = NCH * gr + s
                    where = []
                    for d in range(2):
                        c = s if d == 0 else NCH - 1 - s
                        where.append((CHUNK * (c % 2), c // 2))
                    if s:
                        dve.wait_ge(S["w_state_psum"], 3 * gr + s)
                    else:
                        dve.wait_ge(S["uw_out"], hh + 1)
                    if step:
                        dve.wait_ge(S["step_out_psum"], step)
                    for d, (lo, tl) in enumerate(where):
                        u = u_rows[lo:lo + CHUNK, :, d, tl, :]
                        o = v_new[lo:lo + CHUNK, :, :]
                        if s:
                            a = V.tensor_tensor(o, u, bank[0][lo:lo + CHUNK, :].rearrange("p (g n) -> p g n", g=G), ALU.subtract)
                        else:
                            a = V.tensor_copy(o, u)
                    a.then_inc(S["values_ready"], 1)
                    if s < NCH - 1:
                        dve.wait_ge(S["state_gain_psum"], 3 * gr + s + 1)
                        old, new = states[(s + 1) % 2], states[s % 2]
                        if s == 0:
                            a = V.tensor_copy(new[:, :, :, :].rearrange("p d g n -> p (d g n)"), product[0][:, :])
                        else:
                            for d, (lo, tl) in enumerate(where):
                                for k in range(G):
                                    o = (d * G + k) * P
                                    a = V.scalar_tensor_tensor(new[:, d, k, :], old[:, d, k, :],
                                                               glast[:, lo // CHUNK, G * gr + k, d, tl:tl + 1], product[0][:, o:o + P],
                                                               ALU.mult, ALU.add)
                        a.then_inc(S["state_ready"], 1)
                        dve.wait_ge(S["state_ready"], 3 * gr + s + 1)
                    if s >= 2:
                        dve.wait_ge(S["step_out_psum"], step + 1)
                        dve.wait_ge(S["step_out_copied"], 2 * gr + 2)
                        for d, (lo, tl) in enumerate(where):
                            x = delta_out[lo:lo + CHUNK, tl, G * gr:G * gr + G, :].rearrange("p g n -> p (g n)")
                            a = V.tensor_tensor(x, x, bank[1][lo:lo + CHUNK, :], ALU.add)
                        a.then_inc(S["step_out_added"], 1)
            dve.wait_ge(S["delta_norm_scalar"], 1)
            chain(V.tensor_reduce(st8[:, 0:16], delta_sq[:, :, :, :].rearrange("p t h n -> p (t h) n"), AXX, ALU.add))
            V.tensor_scalar(st8[:, 0:16], st8[:, 0:16], 1.0 / HD, EPS, ALU.mult, ALU.add).then_inc(S["delta_norm_vector"], 1)
            dve.wait_ge(S["delta_norm_scalar"], 2)
            chain(V.reciprocal(st8[:, 16:32], st8[:, 16:32]))
            o16 = delta_out[:, :, :, :].rearrange("p t h n -> p (t h) n")
            chain(V.tensor_tensor(o16, o16, st8[:, 16:32].unsqueeze(2).to_broadcast([P, 16, HD]), ALU.mult))
            chain(V.tensor_tensor(o16, o16, onorm[:, :].unsqueeze(1).to_broadcast([P, 16, HD]), ALU.mult))
            oflat = delta_out[:, :, :, :].rearrange("p t h n -> p (t h n)")
            V.tensor_tensor(oflat, oflat, z_silu[:, :, :].rearrange("p t n -> p (t n)"), ALU.mult).then_inc(S["delta_norm_vector"], 1)
            turn_lo(TG["yb"], 4, a2h, a2l, 8)

            def to_mix(ph, i0):
                def f(n, i, g, free):
                    dve.wait_ge(gates_loaded[n], 16 * (i + i0) + 16)
                    V.tensor_tensor((mixa, mixb)[n][:, :], g[:, :], gates_in[:, n, :], ALU.mult).then_inc(free, 1)
                    if n == 1:
                        wait_read_out(dve, ph, i, 0)
                        wait_read_out(dve, ph, i, 1)
                        V.tensor_tensor(mixb[:, :], mixb[:, :], mixa[:, :], ALU.add).then_inc(S["mixed_ready"], 1)
                        dve.wait_ge(S["mixed_high"], i + i0 + 1)
                        sl = span(4 * (i + i0), 4)
                        V.tensor_tensor(a1l[:, sl, :], mixb[:, :].rearrange("p (m n) -> p m n", m=4), a1h[:, sl, :].bitcast(F32),
                                        ALU.subtract).then_inc(S["mixed_low"], 1)
                return f

            def to_residual(ph):
                def f(n, i, g, free):
                    x = h[:, :, bass.ds(ph.step * i + 512 * n, 512)] if ph.trips > 1 else h[:, :, 512 * n:512 * (n + 1)]
                    V.tensor_tensor(x, g[:, :].rearrange("p (t n) -> p t n", t=TT), x, ALU.add).then_inc(free, 1)
                return f
            gemm(PH["mix0"], to_mix(PH["mix0"], 0))
            gemm(PH["mix"], to_mix(PH["mix"], 1))
            dve.wait_ge(S["residual_loaded"], 16)
            gemm(PH["out"], to_residual(PH["out"]))
            norm_rows("mlp", squares=False)
            turn_lo(TG["mlp"], 8, a1h, a1l, 0, 1)

            def to_hidden(count0, i0):
                def f(n, i, g, free):
                    dve.wait_ge(S["hidden_high"], count0 + 2 * (i + i0) + n + 1)
                    sl = span(8 * (i + i0) + 4 * n, 4)
                    V.tensor_tensor(a2l[:, sl, :], relu_sq[:, :].rearrange("p (m n) -> p m n", m=4), a2h[:, sl, :].bitcast(F32),
                                    ALU.subtract).then_inc(S["hidden_low"], 1)
                return f
            for k in range(2):
                gemm(PH[f"upa{k}"], to_hidden(8 * k, 0), waits=False)
                gemm(PH[f"up{k}"], to_hidden(8 * k, 1), waits=False)
                gemm(PH[f"down{k}"], to_residual(PH[f"down{k}"]))
            dve.wait_ge(S["final_weights_loaded"], 16)
            norm_rows("final", wrow[:, :], squares=False)
            dve.wait_ge(S["rows_normed"], 2)
            norm_rows("norm1")
            turn_lo(TG["norm1"], 8, a1h, a1l, 0, 2)

            for name in ("kv", "qa", "lr"):
                gemm(PH[name], None)
            x = {"q": (qa[:, :, :], HEADS, 32, 0), "k": (kva[:, :, 0:256], 2, 48, 1)}

            def norm_heads(which):
                x_, nh, c0, w = x[which]
                x4 = x_.rearrange("p t (h n) -> p t h n", h=nh)
                chain(V.tensor_tensor(x4, x4, st8[:, c0:c0 + 2 * nh].rearrange("p (t h) -> p t h", t=TT).unsqueeze(3)
                                      .to_broadcast([P, TT, nh, HD]), ALU.mult))
                chain(V.tensor_tensor(x4, x4, gq_bc[:, w, :].unsqueeze(1).unsqueeze(1).to_broadcast([P, TT, nh, HD]), ALU.mult))

            def rotate(which, part):
                x_, nh, _, _ = x[which]
                x5 = x_.rearrange("p t (h c n) -> p t h c n", h=nh, c=2)
                f1, f2 = (r[:, :, 0:nh * HD].rearrange("p t (h c n) -> p t h c n", h=nh, c=2) for r in (rot_a, rot_b))
                cos, sin = (rope_cs[:, k].unsqueeze(2).to_broadcast([P, TT, nh, HD // 2]) for k in range(2))
                if part < 2:
                    V.tensor_tensor(f1[:, :, :, part], x5[:, :, :, part], cos, ALU.mult)
                    a = V.tensor_tensor(f2[:, :, :, part], x5[:, :, :, 1 - part], sin, ALU.mult)
                    if part == 1:
                        chain(a)
                else:
                    V.tensor_tensor(x5[:, :, :, 0], f1[:, :, :, 0], f2[:, :, :, 0], ALU.subtract)
                    chain(V.tensor_tensor(x5[:, :, :, 1], f1[:, :, :, 1], f2[:, :, :, 1], ALU.add))

            def attend2(k):
                if k == 1:
                    dve.wait_ge(S["qk_norm_scalar"], 1)
                    chain(V.tensor_reduce(st8[:, 0:16], rot_a[:, :, :].rearrange("p t (h n) -> p (t h) n", h=HEADS), AXX, ALU.add))
                    chain(V.tensor_reduce(st8[:, 16:20].rearrange("p (t h) -> p t h", t=TT),
                                          rot_b[:, :, 0:256].rearrange("p t (h n) -> p t h n", h=2), AXX, ALU.add))
                    V.tensor_scalar(st8[:, 0:20], st8[:, 0:20], 1.0 / HD, EPS, ALU.mult, ALU.add).then_inc(S["qk_norm_means"], 1)
                if k == 3:
                    dve.wait_ge(S["qk_norm_scalar"], 2)
                    chain(V.reciprocal(st8[:, 32:52], st8[:, 32:52]))
                    dve.wait_ge(S["tables2_loaded"], 16 * NCONST2)
                    norm_heads("k")
                if k in (4, 5, 6):
                    rotate("k", k - 4)
                if k == 7:
                    norm_heads("q")
                if k in (9, 10, 11):
                    rotate("q", k - 9)
                if k == 11:
                    V.memset(st8[:, 63:64], 0.0).then_inc(S["qk_rotated"], 1)
                if k == 12:
                    dve.wait_ge(S["band_loaded"], 16)
                attention(HEADS, att2_scores, bmask[:, :, :], True, k)
                gflat = log_decay[:, :, :, :].rearrange("p d t n -> p (d t n)")
                if k == 31:
                    dve.wait_ge(S["gla_decay_scalar"], 4)
                    V.scalar_tensor_tensor(softplus_buf[:, :], gflat, -1.0, gflat, ALU.mult, ALU.min).then_inc(S["gla_decay_vector"], 1)
                if k == 34:
                    dve.wait_ge(S["gla_decay_scalar"], 5)
                    V.scalar_tensor_tensor(gflat, gflat, 0.0, softplus_buf[:, :], ALU.min, ALU.subtract).then_inc(S["gla_decay_vector"], 1)
                if k == 36:
                    chain(V.memset(gla_scoresT[:, :, :, :].rearrange("p h t n -> p (h t n)"), 0.0))
            for k0, name in ((0, "qkg"), (16, "vg"), (32, "gg")):
                gemm(PH[name], None, between=attend2, k0=k0)
            for k in (48, 49, 50):
                attend2(k)

            qf, kf = (qkg[:, 4 * k:4 * k + 4, :].rearrange("p h n -> p (h n)") for k in range(2))

            def flat(x):
                return x[:, :, :].rearrange("p h n -> p (h n)")
            for d in range(2):
                ref = CHUNK // 2 if d == 0 else CHUNK - 1 - CHUNK // 2
                last = CHUNK - 1 if d == 0 else 0
                ebc = cum[:, :, :].rearrange("p h (c n) -> p (h c) n", n=CHUNK)
                dve.wait_ge(S["gla_cumulated_out"], d + 1)
                if d:
                    dve.wait_ge(S["gla_k_turned"], 1)
                for k, (x, at_) in enumerate(((cum_ref, ref), (cum_last, last))):
                    V.tensor_tensor(x[:, :, :].rearrange("p h (c n) -> p (h c) n", n=CHUNK), ebc, ebc[:, :, at_:at_ + 1].to_broadcast([P, 16, CHUNK]),
                                    ALU.subtract).then_inc(S["gla_differences"], 1)
                dve.wait_ge(S["gla_exps"], 3 * d + 1)
                V.scalar_tensor_tensor(flat(qga), flat(qga), SCALE, qf, ALU.mult, ALU.mult)
                V.tensor_tensor(flat(kga), flat(kga), kf, ALU.mult).then_inc(S["gla_operands"], 1)
                dve.wait_ge(S["gla_exps"], 3 * d + 2)
                V.tensor_tensor(flat(k_out), flat(k_out), kf, ALU.mult).then_inc(S["gla_operands"], 1)
                dve.wait_ge(S["gla_exps"], 3 * d + 3)
                V.scalar_tensor_tensor(flat(q_in), flat(q_in), SCALE, qf, ALU.mult, ALU.mult).then_inc(S["gla_operands"], 1)
                if d:
                    dve.wait_ge(S["gla_direction_out"], 1)
                    chain(V.memset(gla_scoresT[:, :, :, :].rearrange("p h t n -> p (h t n)"), 0.0))
                dve.wait_ge(S["gla_scores_psum"], d + 1)
                V.copy_predicated(gla_scoresT[:, :, :, :].rearrange("p h t n -> p (h t) n"),
                                  causal[:, d, :].bitcast(U32).unsqueeze(1).to_broadcast([P, 8, P]),
                                  product[1][:, :].rearrange("p (q n) -> p q n", q=8)).then_inc(S["gla_scores_masked"], 1)
                for s in range(NCH - 1):
                    c = s if d == 0 else NCH - 1 - s
                    dve.wait_ge(S["gla_gain_psum"], 3 * d + s + 1)
                    if 3 * d + s >= 2:
                        dve.wait_ge(S["gla_step_out"], 3 * d + s - 1)
                    src = product[s % 2]
                    new = gla_state[:, s % 2]
                    if s == 0:
                        a = V.tensor_copy(new.rearrange("p h n -> p (h n)"), src[:, :])
                    else:
                        for k in range(4):
                            a = V.scalar_tensor_tensor(new[:, k, :], gla_state[:, (s + 1) % 2, k, :], st8[:, 4 * k + c:4 * k + c + 1],
                                                       src[:, k * 256:(k + 1) * 256], ALU.mult, ALU.add)
                    a.then_inc(S["gla_state_ready"], 1)
                    dve.wait_ge(S["gla_state_ready"], 3 * d + s + 1)
            dve.wait_ge(S["gla_norm_scalar"], 1)
            chain(V.tensor_reduce(st8[:, 0:8], gla_sq[:, :, :, :].rearrange("p t h n -> p (t h) n"), AXX, ALU.add))
            V.tensor_scalar(st8[:, 0:8], st8[:, 0:8], 1.0 / GLA_DV, EPS, ALU.mult, ALU.add).then_inc(S["gla_norm_vector"], 1)
            dve.wait_ge(S["gla_norm_scalar"], 2)
            chain(V.reciprocal(st8[:, 16:24], st8[:, 16:24]))
            o8 = gla_out[:, :, :, :].rearrange("p t h n -> p (t h) n")
            chain(V.tensor_tensor(o8, o8, st8[:, 16:24].unsqueeze(2).to_broadcast([P, 8, GLA_DV]), ALU.mult))
            chain(V.tensor_tensor(o8, o8, gout_bc[:, :].unsqueeze(1).to_broadcast([P, 8, GLA_DV]), ALU.mult))
            o2f = gla_out[:, :, :, :].rearrange("p t h n -> p (t h n)")
            V.tensor_tensor(o2f, o2f, gg2[:, :, :].rearrange("p t n -> p (t n)"), ALU.mult).then_inc(S["gla_norm_vector"], 1)
            turn_lo(TG["cat"], 4, a2h, a2l, 8)
            gemm(PH["out2"], to_residual(PH["out2"]))
            norm_rows("norm2", squares=False)
            turn_lo(TG["norm2"], 8, a1h, a1l, 0, 3)

            def hidden_lo(q, tile):
                dve.wait_ge(S["hidden_high"], 16 + q + 1)
                sl = span(tile, 4)
                V.tensor_tensor(a2l[:, sl, :], ffn_conv[:, 1, :].rearrange("p (m n) -> p m n", m=4), a2h[:, sl, :].bitcast(F32),
                                ALU.subtract).then_inc(S["hidden_low"], 1)

            def to_ff(ph, q0, after):
                def f(n, i, g, free):
                    q = i + q0
                    if n == 0 and after:
                        hidden_lo(q - 1, 4 * i)
                    wait_read_out(dve, ph, i, n)
                    for tap in (0, 2):
                        for m in range(4):
                            o = ffn_conv[:, n, m * SEQ:(m + 1) * SEQ]
                            a = V.scalar_tensor_tensor(o, ffn_pad[:, n, m, tap:tap + SEQ], conv2_w[:, tap, span(4 * q + 44 * n + m, 1)], o,
                                                       ALU.mult, ALU.add)
                        if tap == 0 or n == 1:
                            chain(a)
                    if n == 0:
                        a.then_inc(S["gate_convolved"], 1)
                        return
                    dve.wait_ge(S["gate_silu"], q + 1)
                    V.tensor_tensor(ffn_conv[:, 1, :], ffn_conv[:, 1, :], ffn_conv[:, 0, :], ALU.mult).then_inc(S["gate_product"], 1)
                return f
            V.memset(ffn_pad[:, :, :, 0:1], 0.0)
            V.memset(ffn_pad[:, :, :, 1 + SEQ:2 + SEQ], 0.0).then_inc(S["vector_clears"], 1)
            for g, (q0, q1) in enumerate(((0, 6), (6, 11))):
                gemm(PH[f"ffa{g}"], to_ff(PH[f"ffa{g}"], q0, False), 3, waits=False)
                gemm(PH[f"ff{g}"], to_ff(PH[f"ff{g}"], q0 + 1, True), 3, waits=False)
                gemm(PH[f"dd{g}"], to_residual(PH[f"dd{g}"]), between=lambda k: hidden_lo(q1 - 1, 4 * (q1 - q0 - 1)) if k == 3 else None)

        @block.tensor
        def _(pe):
            def gemm(ph, ready=(), ready_last=None, between=None, k0=0):
                for s, v in ready:
                    pe.wait_ge(s, v)
                ah, al = acts[ph.act]
                with Loop(pe, ph.trips) as i:
                    for ch in ph.body:
                        g = product[ch.c % 2]
                        if ch.c >= 2:
                            pe.wait_ge(product_read[ch.c % 2], ch.c // 2 + i * (ph.nc // 2))
                        kts = BLK_KT if ch.n == BLK_N else KT
                        for j in range(ch.blocks):
                            idx = ch.b + j
                            sl = idx % HL_SLOTS
                            if between is not None:
                                between(k0 + idx - ph.b0)
                            pe.wait_ge(block_high, idx + 1 + i * ph.nb)
                            pe.wait_ge(block_low, idx + 1 + i * ph.nb)
                            if ready_last is not None and ch is ph.body[0] and j == ch.blocks - 4 // BLK_KT:
                                pe.wait_ge(*ready_last)
                            for k in range(kts):
                                kt = ch.kt0 + j * BLK_KT + k
                                first, last = j == 0 and k == 0, j == ch.blocks - 1 and k == kts - 1
                                if ch.n == BLK_N:
                                    hi, lo = wh[:, sl, k, :], wl[:, sl, k, :]
                                else:
                                    hi, lo = (w[:, sl, 0, k * ch.n:(k + 1) * ch.n] for w in (wh, wl))
                                if ch.kind == "up":
                                    for m in range((ch.n + P - 1) // P):
                                        cols = slice(m * P, min((m + 1) * P, ch.n))
                                        rows = min(P, ch.n)
                                        for q, (a, b) in enumerate(((hi, ah), (hi, al), (lo, ah))):
                                            mm = pe.matmul(g[0:rows, m * SEQ:(m + 1) * SEQ], a[:, cols], b[:, kt, :],
                                                           start=first and q == 0 and m % 2 == 0, stop=last and q == 2,
                                                           skip_group_check=True)
                                else:
                                    for tt in range(TT):
                                        rows = slice(tt * P, (tt + 1) * P)
                                        for q, (a, b) in enumerate(((ah, hi), (ah, lo), (al, hi))):
                                            mm = pe.matmul(g[:, tt * 512:tt * 512 + ch.n], a[:, kt, rows], b,
                                                           start=first and q == 0, stop=last and q == 2,
                                                           skip_group_check=True)
                            mm.then_inc(block_multiplied, 1)

            def turn(base, g, src):
                if g >= 4:
                    pe.wait_ge(S["turned_low"], base + g - 3)
                for m in range(2):
                    for tt in range(TT):
                        mm = pe.transpose(bank[g % 4][:, m * SEQ + tt * P:m * SEQ + (tt + 1) * P], src(2 * g + m, tt), ident[:, :])
                mm.then_inc(S["turned_psum"], 1)

            def turn_rows(name, count, ph):
                base = TG[name]

                def src(kt, tt):
                    return rows_scaled[:, tt, kt * P:(kt + 1) * P]
                pe.wait_ge(S["rows_scaled_ready"], count)
                for g in range(4):
                    turn(base, g, src)

                def between(k):
                    if k < 8:
                        if 1 <= k <= 4:
                            turn(base, k + 3, src)
                        pe.wait_ge(S["turned_low"], base + k + 1)
                gemm(ph, between=between)

            def products_out(ph):
                wait_read_out(pe, ph, ph.trips - 1, ph.nc - 2)
                wait_read_out(pe, ph, ph.trips - 1, ph.nc - 1)

            def attention(base, scores_, probsT, q, k, v, position, slot):
                hh = head_at("scores", base, slot)
                if hh is not None:
                    if hh >= 2:
                        pe.wait_ge(S["scores_masked"], base + hh - 1)
                    if position is not None:
                        pe.wait_ge(bias_loaded[hh % 4], 64 * (hh // 4 + 1))
                    for tt in range(TT):
                        o = bank[hh % 2][:, tt * SEQ:(tt + 1) * SEQ]
                        mm = pe.matmul(o, q(hh)[:, tt * P:(tt + 1) * P], k(hh), start=True, stop=position is None)
                        if position is not None:
                            mm = pe.matmul(o, flip[:, :], position[:, hh % 4, tt, :], start=False, stop=True)
                    mm.then_inc(S["scores_ready"], 1)
                hh = head_at("turn", base, slot)
                if hh is not None:
                    pe.wait_ge(S["probs_scaled"], base + hh + 1)
                    if hh >= 2:
                        pe.wait_ge(S["head_out_low"], base + hh - 1)
                    for kt in range(TT):
                        for tt in range(TT):
                            mm = pe.transpose(bank[2 + hh % 2][:, kt * SEQ + tt * P:kt * SEQ + (tt + 1) * P],
                                              scores_[:, hh % 2, tt, kt * P:(kt + 1) * P], ident[:, :])
                    mm.then_inc(S["probs_turned"], 1)
                hh = head_at("values", base, slot)
                if hh is not None:
                    pe.wait_ge(S["probs_turned_out"], base + hh + 1)
                    for kt in range(TT):
                        mm = pe.matmul(bank[2 + hh % 2][:, 0:SEQ], v(hh, kt), probsT[:, hh % 2, kt, :], start=kt == 0, stop=kt == TT - 1)
                    mm.then_inc(S["head_out_ready"], 1)

            pe.wait_ge(S["first_tables_loaded"], 32)
            pe.wait_ge(S["vector_clears"], 1)
            turn_rows("mix", 1, PH["lead"])
            pe.wait_ge(S["tables1_loaded"], 16 * NCONST)
            for name in ("ba", "v", "qk", "dn0", "dn"):
                gemm(PH[name])

            bt, gg = sc32["bt"], sc32["gg"]

            def beside_gates(k):
                if k == ATT_START[0]:
                    pe.wait_ge(S["attention_tables_loaded"], 32)
                attention(0, att_scores, att_probsT, lambda hh: attqk[:, hh, :], lambda hh: attqk[:, 8 + hh, :],
                          lambda hh, kt: attv[:, kt, hh * P:(hh + 1) * P], bias, k)
                if k == 42:
                    pe.wait_ge(S["scores_masked"], HEADS - 1)
                    for tt in range(TT):
                        mm = pe.transpose(bank[0][:, tt * 32:(tt + 1) * 32], baT[0:32, tt * P:(tt + 1) * P], ident[0:32, 0:32])
                    mm.then_inc(S["decay_inputs"], 1)
                if k == 47:
                    pe.wait_ge(S["decay_vector"], 2)
                    pe.wait_ge(S["decay_scalar"], 2)
                    pe.wait_ge(S["head_out_low"], HEADS)
                    for d in range(2):
                        pe.matmul(bank[0][:, d * 16:(d + 1) * 16], tri[:, d, :], gg[:, :, d, :], start=True, stop=True)
                    pe.matmul(bank[1][:, 0:32], blockm[:, :], gg[:, :, :, :].rearrange("p h d t -> p (h d t)"), start=True, stop=True)
                    pe.matmul(bank[1][:, 64:128], ones[:, :], ghalf[:, :, :, :, :].rearrange("p a h d t -> p (a h d t)"),
                              start=True, stop=True).then_inc(S["decay_cumulated"], 1)
                j = batch_at(1, k)
                if j is not None:
                    pe.wait_ge(S["unit_squares"], j + 1)
                    if j >= 2:
                        pe.wait_ge(S["unit_roots"], j - 1)
                    pe.matmul(bank[2 + j % 2][:, :], ones[:, :], sq_buf[:, j % 2, :], start=True, stop=True).then_inc(S["unit_sums"], 1)

            gemm(PH["z"], between=beside_gates)
            gemm(PH["gates"], between=beside_gates, k0=16)
            products_out(PH["gates"])

            pe.wait_ge(S["decay_scalar"], 3)
            pe.wait_ge(S["decay_columns"], 1)
            pe.wait_ge(S["unit_scaled"], 8)
            pe.wait_ge(S["head_out_low"], HEADS)
            for h0 in range(0, HEADS, 2):
                pair = (h0, h0 + 1)
                if h0 == G:
                    pe.wait_ge(S["step_out_added"], 2)
                for hh in pair:
                    b = hh % 2
                    if hh >= 2:
                        pe.wait_ge(S["level_inner_out"], pair_count(hh - 2, LV, LV))
                        pe.wait_ge(S["token_rows_scaled"], hh - 1)
                    for d in range(2):
                        for tt in range(TT):
                            q = d * 2 + tt
                            pe.matmul(bank[2 * b][:, q * P:(q + 1) * P], gg[:, hh, d, tt:tt + 1].to_broadcast([P, P]), tri[:, d, :],
                                      start=True, stop=True)
                            mm = pe.matmul(bank[2 * b + 1][:, q * P:(q + 1) * P], bt[:, hh, d, tt:tt + 1].to_broadcast([P, P]), ident[:, :],
                                           start=True, stop=True)
                    mm.then_inc(S["decay_rows_psum"], 1)
                for hh in pair:
                    b = hh % 2
                    qT, kT, vT = dnT[:, hh, :], dnT[:, 8 + hh, :], dnT[:, 16 + hh, :]
                    pe.wait_ge(S["k_beta_ready"], hh + 1)
                    if hh >= 2:
                        pe.wait_ge(S["uw_out"], hh - 1)
                    for tt in range(TT):
                        c = slice(tt * P, (tt + 1) * P)
                        for d in range(2):
                            q = d * 2 + tt
                            pe.matmul(product[b][:, q * P:(q + 1) * P], kT[:, c], k_betaT[b][:, d, c], start=True, stop=True)
                        mm = pe.matmul(product[b][:, 512 + tt * P:512 + (tt + 1) * P], kT[:, c], qT[:, c], start=True, stop=True)
                    mm.then_inc(S["gram_psum"], 1)
                    for tt in range(TT):
                        c = slice(tt * P, (tt + 1) * P)
                        pe.transpose(bank[2 * b + 1][:, c], kT[:, c], ident[:, :])
                        mm = pe.transpose(bank[2 * b + 1][:, 256 + tt * P:256 + (tt + 1) * P], vT[:, c], ident[:, :])
                    mm.then_inc(S["token_rows_psum"], 1)
                for hh in pair:
                    b = hh % 2
                    pe.wait_ge(S["level0_inverse"], hh + 1)
                    pe.wait_ge(S["decay_exps"], pair_count(hh, 2, 2))
                    for q in range(4):
                        mm = pe.transpose(bank[2 * b][:, q * P:(q + 1) * P], inverse[b][:, 1, q, :], ident[:, :])
                    mm.then_inc(S["level0_turned"], 1)
                for n in range(1, LEVELS):
                    for hh in pair:
                        b = hh % 2
                        pe.wait_ge(S["triangle_levels"], pair_count(hh, n, LV))
                        if n == 1:
                            pe.wait_ge(S["level0_turned_out"], hh + 1)
                        else:
                            pe.wait_ge(S["inverse_updated"], pair_count(hh, n - 1, LV))
                        for q in range(4):
                            mm = pe.matmul(bank[2 * b][:, q * P:(q + 1) * P], tri_levels[b][:, q // 2, q % 2, n - 1, :], inverse[b][:, 0, q, :],
                                           start=True, stop=True)
                        mm.then_inc(S["level_inner_psum"], 1)
                    for hh in pair:
                        b = hh % 2
                        pe.wait_ge(S["level_inner_out"], pair_count(hh, n, LV))
                        if n == 1:
                            pe.wait_ge(S["qk_decayed"], hh + 1)
                        for q in range(4):
                            if n < LV:
                                pe.matmul(product[b][:, q * P:(q + 1) * P], inverse[b][:, 1, q, :], level_prod[b][:, q, :], start=True, stop=True)
                            mm = pe.matmul(product[b][:, 512 + q * P:512 + (q + 1) * P], level_prod[b][:, q, :], inverse[b][:, 1, q, :], start=True, stop=True)
                        mm.then_inc(S["level_outer_psum"], 1)
                for hh in pair:
                    b = hh % 2
                    pe.wait_ge(S["inverse_updated"], pair_count(hh, LV, LV))
                    pe.wait_ge(S["token_rows_scaled"], hh + 1)
                    for q in range(4):
                        pe.matmul(product[b][:, q * P:(q + 1) * P], inverse[b][:, 1, q, :], v_beta[b][:, q // 2, q % 2, :], start=True, stop=True)
                        mm = pe.matmul(product[b][:, 512 + q * P:512 + (q + 1) * P], k_beta_decay[b][:, q // 2, q % 2, :], inverse[b][:, 1, q, :],
                                       start=True, stop=True)
                    mm.then_inc(S["uw_psum"], 1)
                g, gr = hh % G, hh // G
                if g < G - 1:
                    continue
                pe.wait_ge(S["uw_out"], hh + 1)
                pe.wait_ge(S["q_decayed"], hh + 1)
                for s in range(NCH):
                    step = NCH * gr + s
                    where = []
                    for d in range(2):
                        c = s if d == 0 else NCH - 1 - s
                        where.append((CHUNK * (c % 2), c // 2))
                    if s:
                        pe.wait_ge(S["state_ready"], 3 * gr + s)
                        for d, (lo, tl) in enumerate(where):
                            for k in range(G):
                                mm = pe.matmul(bank[0][lo:lo + CHUNK, k * P:(k + 1) * P], w_T[:, k, d, tl, lo:lo + CHUNK], states[(s - 1) % 2][:, d, k, :],
                                               start=True, stop=True)
                        mm.then_inc(S["w_state_psum"], 1)
                    pe.wait_ge(S["values_ready"], step + 1)
                    if s < NCH - 1:
                        for d, (lo, tl) in enumerate(where):
                            for k in range(G):
                                o = (d * G + k) * P
                                mm = pe.matmul(product[0][:, o:o + P], k_decay[lo:lo + CHUNK, k, d, tl, :], v_new[lo:lo + CHUNK, k, :], start=True, stop=True)
                        mm.then_inc(S["state_gain_psum"], 1)
                    if s in (1, 2):
                        pe.wait_ge(S["step_out_copied"], 2 * gr + s)
                    elif s == 3:
                        pe.wait_ge(S["step_out_added"], 2 * gr + 1)
                    for d, (lo, tl) in enumerate(where):
                        rows = slice(lo, lo + CHUNK)
                        for k in range(G):
                            o = bank[1][rows, k * P:(k + 1) * P]
                            if s:
                                pe.matmul(o, q_decayT[:, k, d, tl * P + lo:tl * P + lo + CHUNK], states[(s - 1) % 2][:, d, k, :], start=True, stop=False)
                            mm = pe.matmul(o, qkT[rows, k, d, tl, lo:lo + CHUNK], v_new[rows, k, :], start=s == 0, stop=True)
                    mm.then_inc(S["step_out_psum"], 1)
            def second_half(base, ready, src):
                def between(k):
                    if k == 4:
                        pe.wait_ge(*ready)
                        for g in range(4):
                            turn(base, g, src)
                        pe.wait_ge(S["turned_low"], base + 4)
                return between
            gemm(PH["mix0"], between=second_half(TG["yb"], (S["delta_norm_vector"], 2), lambda kt, tt: delta_out[:, tt, kt, :]))
            gemm(PH["mix"])
            gemm(PH["out"], [(S["mixed_low"], 3)], (S["mixed_low"], 4))
            turn_rows("mlp", 2, PH["upa0"])
            gemm(PH["up0"])
            gemm(PH["down0"], [(S["hidden_low"], 7)], (S["hidden_low"], 8))
            gemm(PH["upa1"])
            gemm(PH["up1"])
            gemm(PH["down1"], [(S["hidden_low"], 15)], (S["hidden_low"], 16))
            turn_rows("norm1", 3, PH["kv"])
            gemm(PH["qa"])

            def attend2(k):
                if k == 12:
                    pe.wait_ge(S["qk_rotated"], 1)
                if k in (12, 13):
                    for g in range(4) if k == 12 else (4,):
                        if g == 4:
                            pe.wait_ge(S["qk_turned_out"], 1)
                        for m in range(2):
                            for tt in range(TT):
                                hd = 2 * g + m
                                src = qa[:, tt, hd * P:(hd + 1) * P] if g < 4 else kva[:, tt, m * P:(m + 1) * P]
                                mm = pe.transpose(bank[g % 4][:, m * SEQ + tt * P:m * SEQ + (tt + 1) * P], src, ident[:, :])
                        mm.then_inc(S["qk_turned"], 1)
                if k == 14:
                    pe.wait_ge(S["qk_turned_out"], 5)
                if k in (22, 26, 30, 34):
                    pe.wait_ge(S["gla_decay_scalar"], (k - 18) // 4)
                attention(HEADS, att2_scores, att2_probsT, lambda hh: qT2[:, hh, :], lambda hh: kT2[:, hh // 4, :],
                          lambda hh, kt: kva[:, kt, 256 + (hh // 4) * P:256 + (hh // 4 + 1) * P], None, k)
                if k in (17, 21, 25, 29):
                    q = (k - 17) // 4
                    if q == 0:
                        pe.wait_ge(S["decay_w_ready"], 1)
                        wait_read_out(pe, PH["lr"], 0, 0)
                    pe.wait_ge(S["scores_masked"], HEADS + q + 1)
                    pe.matmul(bank[q % 2][:, :], lrT[0:33, q % 2 * P:(q % 2 + 1) * P], decay_w[0:33, q // 2, :], start=True, stop=True).then_inc(S["gla_decay_psum"], 1)
            gemm(PH["lr"])
            for k0, name in ((0, "qkg"), (16, "vg"), (32, "gg")):
                gemm(PH[name], between=attend2, k0=k0)
            attend2(48)
            products_out(PH["gg"])
            pe.wait_ge(S["head_out_low"], 2 * HEADS)
            pe.wait_ge(S["gla_decay_vector"], 2)
            for d in range(2):
                if d:
                    pe.wait_ge(S["gla_state_ready"], 3)
                for hh in range(4):
                    for tt in range(TT):
                        mm = pe.matmul(product[0][:, hh * SEQ + tt * P:hh * SEQ + (tt + 1) * P], log_decay[:, d, tt, hh * P:(hh + 1) * P], tri[:, d, :],
                                       start=True, stop=True)
                mm.then_inc(S["gla_cumulated"], 1)
                pe.wait_ge(S["gla_operands"], 3 * d + 1)
                for hh in range(4):
                    for tt in range(TT):
                        c = slice(tt * P, (tt + 1) * P)
                        mm = pe.matmul(product[1][:, (hh * 2 + tt) * P:(hh * 2 + tt + 1) * P], kga[:, hh, c], qga[:, hh, c], start=True, stop=True)
                mm.then_inc(S["gla_scores_psum"], 1)
                pe.wait_ge(S["gla_operands"], 3 * d + 2)
                pe.wait_ge(S["gla_cumulated_out"], d + 1)
                for hh in range(4):
                    for tt in range(TT):
                        mm = pe.transpose(product[0][:, (hh * 2 + tt) * P:(hh * 2 + tt + 1) * P], k_out[:, hh, tt * P:(tt + 1) * P], ident[:, :])
                mm.then_inc(S["gla_k_turned"], 1)
                pe.wait_ge(S["gla_scores_masked"], d + 1)
                for tt in range(TT):
                    for hh in range(4):
                        mm = pe.matmul(bank[2 * tt + hh // 2][:, (hh % 2) * 256:(hh % 2 + 1) * 256], gla_scoresT[:, hh, tt, :],
                                       vg[:, tt, hh * 256:(hh + 1) * 256], start=d == 0 and hh % 2 == 0, stop=False, skip_group_check=True)
                pe.wait_ge(S["gla_k_turned_out"], d + 1)
                for s in range(NCH):
                    c = s if d == 0 else NCH - 1 - s
                    lo, tl = CHUNK * (c % 2), c // 2
                    rows = slice(lo, lo + CHUNK)
                    if s < NCH - 1:
                        if s >= 2:
                            pe.wait_ge(S["gla_state_ready"], 3 * d + s - 1)
                        for hh in range(4):
                            mm = pe.matmul(product[s % 2][:, hh * 256:(hh + 1) * 256], k_outT[rows, hh, tl, :], vg[rows, tl, hh * 256:(hh + 1) * 256],
                                           start=True, stop=True)
                        mm.then_inc(S["gla_gain_psum"], 1)
                    if s:
                        pe.wait_ge(S["gla_operands"], 3 * d + 3)
                        pe.wait_ge(S["gla_state_ready"], 3 * d + s)
                        for hh in range(4):
                            mm = pe.matmul(bank[2 * tl + hh // 2][rows, (hh % 2) * 256:(hh % 2 + 1) * 256], q_in[:, hh, c * CHUNK:(c + 1) * CHUNK],
                                           gla_state[:, (s - 1) % 2, hh, :], start=False, stop=d == 1 and s == NCH - 1, skip_group_check=True)
                        if s < NCH - 1:
                            mm.then_inc(S["gla_step_out"], 1)
                        else:
                            mm.then_inc(S["gla_direction_out"], 1)
            gemm(PH["out2"], between=second_half(TG["cat"], (S["gla_norm_vector"], 2),
                                                 lambda kt, tt: gla_out[:, tt, kt // 2, (kt % 2) * P:(kt % 2 + 1) * P]))
            turn_rows("norm2", 4, PH["ffa0"])
            gemm(PH["ff0"])
            gemm(PH["dd0"], [(S["hidden_low"], 16 + 5)], (S["hidden_low"], 16 + 6))
            gemm(PH["ffa1"])
            gemm(PH["ff1"])
            gemm(PH["dd1"], [(S["hidden_low"], 16 + 10)], (S["hidden_low"], 16 + 11))

        @block.gpsimd
        def _(pool):
            G_ = nc.gpsimd

            def load(dst, src, s):
                pool.dma_start(dst, src).then_inc(s, 16)

            with nc.allow_non_contiguous_dma(reason="small per-feature table"):
                load(normw[:, 0, :], t["norm_mix_w"].rearrange("(k p) -> p k", p=P), S["first_tables_loaded"])
            load(ident[:, :], t["ident"], S["first_tables_loaded"])
            for dst, name in ((tri[:, :, :], "tri"), (blockm[:, :], "block"), (neg[:, :, :], "neg"),
                              (half[:, :], "half"), (level[:, :, :, :], "level")):
                load(dst, t[name], S["tables1_loaded"])
            with nc.allow_non_contiguous_dma(reason="small per-feature tables"):
                load(normw[:, 1, :], t["norm_mlp_w"].rearrange("(k p) -> p k", p=P), S["tables1_loaded"])
                for k, name in enumerate(("norm1_g_2", "norm2_g_2")):
                    load(normw[:, 2 + k, :], t[name][0].rearrange("(k p) -> p k", p=P), S["tables1_loaded"])
                for tap in range(5):
                    load(conv1_w[:, tap, :], t["conv_w"][tap].rearrange("(k p) -> p k", p=P), S["tables1_loaded"])
                load(dtal[:, 0, :], t["dt_bias"].rearrange("d h -> (d h)").partition_broadcast(P), S["tables1_loaded"])
                load(dtal[:, 1, :], t["a_log"].rearrange("d h -> (d h)").partition_broadcast(P), S["tables1_loaded"])
                load(onorm[:, :], t["onorm_w"].partition_broadcast(P), S["tables1_loaded"])
            pool.wait_ge(S["conv_activated"], 6)
            load(wmask[:, :], t["window"], S["attention_tables_loaded"])
            load(flip[:, :], t["flip"], S["attention_tables_loaded"])
            for hh in range(HEADS):
                if hh >= 4:
                    pool.wait_ge(S["scores_ready"], hh - 3)
                for row in range(SEQ // GRID_W):
                    lo, tl = GRID_W * (row % 2), row // 2
                    first = hh * 15 * 31 + (7 - row) * 31 + 15 - (GRID_W - 1)
                    src = bass.AP(t["rpb"].tensor, first, [[1, GRID_W], [31, SEQ // GRID_W], [1, GRID_W]])
                    load(bias[lo:lo + GRID_W, hh % 4, tl, :].rearrange("p (r c) -> p r c", c=GRID_W), src, bias_loaded[hh % 4])
            for n in range(8):
                wait_read_out(pool, PH["gates"], 0, n)
                load(gates_dram[n], gates_out[:, n % 2, :], gates_stored[n % 2])
            for h0 in range(0, HEADS, 2):
                for n in range(1, LEVELS):
                    for hh in (h0, h0 + 1):
                        if n == 1:
                            pool.wait_ge(S["triangle_ready"], hh + 1)
                            if hh >= 2:
                                pool.wait_ge(S["level_inner_psum"], pair_count(hh - 2, LV, LV))
                        G_.tensor_tensor(tri_levels[hh % 2][:, :, :, n - 1, :], triT[hh % 2][:, :, :, :],
                                         level[:, :, n, :].unsqueeze(2).to_broadcast([P, 2, TT, P]), ALU.mult).then_inc(S["triangle_levels"], 1)
            pool.wait_ge(S["turned_low"], TG["yb"] + 4)
            load(h[:, :, :], t["x"][0].rearrange("(t p) n -> p t n", p=P), S["residual_loaded"])
            for n in range(2):
                pool.wait_ge(gates_stored[n], 16 * 4)
            for i in range(4):
                for n in range(2):
                    if i >= 1:
                        ph = PH["mix0" if i == 1 else "mix"]
                        wait_read_out(pool, ph, max(i - 2, 0), n)
                    load(gates_in[:, n, :], gates_dram[4 * n + i], gates_loaded[n])
            load(causal[:, :, :], t["causal"].rearrange("p (d n) -> p d n", d=2), S["tables2_loaded"])
            for k, name in enumerate(("cos", "sin")):
                load(rope_cs[:, k], t[name].rearrange("p (t n) -> p t n", t=TT), S["tables2_loaded"])
            with nc.allow_non_contiguous_dma(reason="small per-feature tables"):
                for tap in range(3):
                    load(conv2_w[:, tap, :], t["conv_w_2"][0, tap].rearrange("(k p) -> p k", p=P), S["tables2_loaded"])
                load(conv2_b[:, :], t["conv_b_2"][0].rearrange("(k p) -> p k", p=P), S["tables2_loaded"])
                load(gq_bc[:, 0, :], t["attn_q_norm_g_2"][0].partition_broadcast(P), S["tables2_loaded"])
                load(gq_bc[:, 1, :], t["attn_k_norm_g_2"][0].partition_broadcast(P), S["tables2_loaded"])
                load(gout_bc[:, :], t["gla_out_norm_g_2"][0].partition_broadcast(P), S["tables2_loaded"])
                load(sink_bc[:, :], t["attn_sink_2"][0].partition_broadcast(P), S["tables2_loaded"])
            pool.wait_ge(block_multiplied, last_block(PH["down1"]))
            load(wrow[:, :], t["norm_final_w"].partition_broadcast(P), S["final_weights_loaded"])
            G_.memset(lrT[32:33, :], 1.0)
            G_.memset(decay_w[0:32, :, :], 0.0).then_inc(S["decay_w_cleared"], 1)
            pool.wait_ge(S["decay_w_cleared"], 1)
            for d, s in enumerate(("fwd", "bwd")):
                load(decay_w[16 * d:16 * d + 16, d, :], t[f"gla_wa2_{s}_2"][0], S["decay_w_loaded"])
                load(decay_w[32:33, d, :], t[f"gla_ba_{s}_2"], S["decay_w_loaded"])
            pool.wait_ge(S["decay_w_loaded"], 64)
            G_.memset(pdum[:, 0:1], 0.0).then_inc(S["decay_w_ready"], 1)
            pool.wait_ge(S["turned_low"], TG["norm1"] + 8)
            load(bmask[:, :, :], t["band"].rearrange("p (t k) -> p t k", t=TT), S["band_loaded"])


_INS = ['x', 'norm_mix_w', 'w_in', 'conv_w', 'a_log', 'dt_bias', 'onorm_w', 'rpb', 'w_proj_a', 'w_proj_b', 'w_out',
        'norm_mlp_w', 'w_mlp_up', 'w_mlp_down', 'norm_final_w', 'norm1_g_2', 'w_in_2', 'attn_q_norm_g_2',
        'attn_k_norm_g_2', 'attn_sink_2', 'gla_wa2_fwd_2', 'gla_ba_fwd_2', 'gla_wa2_bwd_2', 'gla_ba_bwd_2',
        'gla_out_norm_g_2', 'w_out_2', 'norm2_g_2', 'w_up_2', 'conv_w_2', 'conv_b_2', 'w_down_2']
_SQUEEZED = ('w_in_2', 'w_out_2', 'w_up_2', 'w_down_2')


def program(nc, shapes):
    t = {}
    for name, (shape, dtype) in shapes.items():
        ap = nc.dram_tensor(f"in_{name}", shape, dtype, kind="ExternalInput").ap()
        t[name] = ap[0] if name in _SQUEEZED else ap
    t["out"] = nc.dram_tensor("out_0", (1, SEQ, D), F32, kind="ExternalOutput").ap()
    return t


def kernel(**inputs):
    import concourse.bacc as _bacc
    from concourse.bass_utils import run_bass_kernel_spmd as _run

    nc = _bacc.Bacc("TRN2", target_bir_lowering=False, num_devices=1)
    arrays = {n: np.ascontiguousarray(inputs[n]) for n in _INS}
    arrays.update(constants())
    t = program(nc, {n: (a.shape, mybir.dt.from_np(a.dtype)) for n, a in arrays.items()})
    build(nc, t)
    r = _run(nc, [{f"in_{n}": a for n, a in arrays.items()}], core_ids=[0])
    return r.results[0]["out_0"]
```
